# Optimizing a Trainium2 kernel written in Bass

```python
import math
import jax, jax.numpy as jnp
from jax import lax
import numpy as np

D_MODEL = 1024
BATCH = 1
SEQ = 256
DEPTH = 2
DEC_BATCH = 8
DEC_SEQ = 1
PAST_LEN = 2048
PAGE_SIZE = 128

N_MIXERS = 2
N_LRU_LAYERS = (DEPTH + 1) // 2
N_MLSTM_LAYERS = DEPTH // 2
CONV_W = 4
D_RNN = D_MODEL
LRU_BLOCKS = 16
LRU_BW = D_RNN // LRU_BLOCKS
LRU_C = 8.0
M_INNER = 2 * D_MODEL
M_HEADS = 4
M_HD = M_INNER // M_HEADS
QKV_BS = 4
M_CHUNK = 64
N_KEYS = 128
N_EXPERTS = N_KEYS * N_KEYS
P_HEADS = 8
P_DKEY = 256
P_HALF = P_DKEY // 2
P_TOPK = 16
PEER_BLOCK = 256
EPS = 1e-6

kernel_name = 'hybrid_rglru_mlstm_peer_adaln_step'

def rmsnorm(x, g):
    xf = x.astype(jnp.float32)
    return xf * lax.rsqrt(jnp.mean(xf * xf, axis=-1, keepdims=True) + EPS) * g.astype(jnp.float32)

def causal_conv(x, buf, w, b):
    T = x.shape[1]
    xp = jnp.concatenate([buf.astype(x.dtype), x], axis=1)
    y = b.astype(x.dtype)
    for j in range(CONV_W):
        y = y + w[j] * xp[:, j:j + T]
    return y, xp[:, -(CONV_W - 1):]

def blockdiag(x, w):
    nb, bi, bo = w.shape
    xb = x.reshape(*x.shape[:-1], nb, bi)
    return jnp.einsum('...gi,gio->...go', xb, w).reshape(*x.shape[:-1], nb * bo)

def rglru_mixer(h, h0, conv_buf, w_in, conv_w, conv_b, w_a, b_a, w_i, b_i, lam, w_out):
    proj = h @ w_in
    y_br = jax.nn.gelu(proj[..., :D_RNN])
    xr, new_buf = causal_conv(proj[..., D_RNN:], conv_buf, conv_w, conv_b)
    r = jax.nn.sigmoid(blockdiag(xr, w_a) + b_a)
    i = jax.nn.sigmoid(blockdiag(xr, w_i) + b_i)
    log_a = LRU_C * r * jax.nn.log_sigmoid(lam.astype(jnp.float32))
    a = jnp.exp(log_a)
    bx = jnp.sqrt(-jnp.expm1(2.0 * log_a)) * (i * xr)
    bx = bx.at[:, 0].add(a[:, 0] * h0.astype(jnp.float32))

    def comb(lhs, rhs):
        a1, b1 = lhs
        a2, b2 = rhs
        return a1 * a2, a2 * b1 + b2

    _, hs = lax.associative_scan(comb, (a, bx), axis=1)
    out = (hs * y_br) @ w_out
    return out, hs[:, -1], new_buf

def mlstm_cell(q, k, v, i_pre, logf, C0, n0, m0):
    B, T, H, Dh = q.shape
    L = math.gcd(T, M_CHUNK)
    nc = T // L

    def chunks(t):
        t = t.reshape(B, nc, L, H, *t.shape[3:])
        return jnp.moveaxis(t, (1, 3), (0, 2))

    mask = jnp.tril(jnp.ones((L, L), dtype=bool))

    def step(carry, inp):
        C, n, m = carry
        qc, kc, vc, ic, fc = inp
        b = jnp.cumsum(fc, axis=-1)
        dmat = jnp.where(mask, b[..., :, None] - b[..., None, :] + ic[..., None, :], -jnp.inf)
        m_inter = b + m[..., None]
        m_j = jnp.maximum(m_inter, dmat.max(-1))
        w = jnp.exp(dmat - m_j[..., None])
        s_inter = jnp.exp(m_inter - m_j)
        s = jnp.einsum('bhjd,bhsd->bhjs', qc, kc) * w
        num = s_inter[..., None] * jnp.einsum('bhjd,bhde->bhje', qc, C) + jnp.einsum('bhjs,bhse->bhje', s, vc)
        den = s_inter * jnp.einsum('bhjd,bhd->bhj', qc, n) + s.sum(-1)
        hout = num / jnp.maximum(jnp.abs(den), jnp.exp(-m_j))[..., None]
        g = b[..., -1:] - b + ic
        m_new = jnp.maximum(b[..., -1] + m, g.max(-1))
        wg = jnp.exp(g - m_new[..., None])
        decay = jnp.exp(b[..., -1] + m - m_new)
        C_new = decay[..., None, None] * C + jnp.einsum('bhs,bhsd,bhse->bhde', wg, kc, vc)
        n_new = decay[..., None] * n + jnp.einsum('bhs,bhsd->bhd', wg, kc)
        return (C_new, n_new, m_new), hout

    carry0 = (C0.astype(jnp.float32), n0.astype(jnp.float32), m0.astype(jnp.float32))
    (C, n, m), hs = lax.scan(step, carry0, (chunks(q), chunks(k), chunks(v), chunks(i_pre), chunks(logf)))
    hs = jnp.moveaxis(hs, (0, 2), (1, 3)).reshape(B, T, H, Dh)
    return hs, C, n, m

def mlstm_mixer(h, C0, n0, m0, conv_buf, w_in, conv_w, conv_b, w_q, w_k, w_v, w_ig, b_ig, w_fg, b_fg, skip, ln_g, w_out):
    B, T, _ = h.shape
    proj = h @ w_in
    xm, z = proj[..., :M_INNER], proj[..., M_INNER:]
    xc, new_buf = causal_conv(xm, conv_buf, conv_w, conv_b)
    xc = jax.nn.silu(xc)
    q = blockdiag(xc, w_q)
    k = blockdiag(xc, w_k) * (M_HD ** -0.5)
    v = blockdiag(xm, w_v)
    qkv = jnp.concatenate([q, k, v], axis=-1)
    i_pre = qkv @ w_ig + b_ig
    logf = jax.nn.log_sigmoid(qkv @ w_fg + b_fg)
    heads = lambda t: t.reshape(B, T, M_HEADS, M_HD)
    hc, C, n, m = mlstm_cell(heads(q), heads(k), heads(v), i_pre, logf, C0, n0, m0)
    mu = hc.mean(-1, keepdims=True)
    var = jnp.mean(jnp.square(hc - mu), axis=-1, keepdims=True)
    hn = ((hc - mu) * lax.rsqrt(var + EPS)).reshape(B, T, M_INNER) * ln_g
    out = ((hn + skip * xc) * jax.nn.silu(z)) @ w_out
    return out, C, n, m, new_buf

def peer_ffn(h, w_q, sub_keys, u, v):
    B, T, D = h.shape
    n_tok = B * T
    nb = -(-n_tok // PEER_BLOCK)
    xt = jnp.pad(h.reshape(n_tok, D), ((0, nb * PEER_BLOCK - n_tok), (0, 0))).reshape(nb, PEER_BLOCK, D)

    def block(xb):
        q = (xb @ w_q).reshape(PEER_BLOCK, P_HEADS, 2, P_HALF)
        s = jnp.einsum('thpd,hpkd->thpk', q, sub_keys).astype(jnp.float32)
        s1, i1 = lax.top_k(s[:, :, 0], P_TOPK)
        s2, i2 = lax.top_k(s[:, :, 1], P_TOPK)
        cand = (s1[..., :, None] + s2[..., None, :]).reshape(PEER_BLOCK, P_HEADS, P_TOPK * P_TOPK)
        cidx = (i1[..., :, None] * N_KEYS + i2[..., None, :]).reshape(PEER_BLOCK, P_HEADS, P_TOPK * P_TOPK)
        top, pos = lax.top_k(cand, P_TOPK)
        idx = jnp.take_along_axis(cidx, pos, axis=-1)
        g = jax.nn.softmax(top, axis=-1)
        act = jax.nn.gelu(jnp.einsum('td,thkd->thk', xb, u[idx]))
        return jnp.einsum('thk,thkd->td', g * act, v[idx])

    out = lax.map(block, xt).reshape(nb * PEER_BLOCK, D)[:n_tok]
    return out.reshape(B, T, D)

def trunk(x, c, lru_h, lru_conv, ml_C, ml_n, ml_m, ml_conv, p):
    out_dtype = x.dtype
    x = x.astype(jnp.float32)
    c = c.astype(jnp.float32)
    new_lh, new_lc, new_C, new_n, new_m, new_mc = [], [], [], [], [], []
    for l in range(DEPTH):
        mod = (c @ p['w_ada'][l] + p['b_ada'][l])[:, None, :]
        sh1, sc1, g1, sh2, sc2, g2 = jnp.split(mod, 6, axis=-1)
        hm = rmsnorm(x, p['norm_mix'][l]) * (1.0 + sc1) + sh1
        j = l // N_MIXERS
        if l % N_MIXERS == 0:
            mix, hT, cb = rglru_mixer(hm, lru_h[j], lru_conv[j], p['lru_w_in'][j], p['lru_conv_w'][j], p['lru_conv_b'][j],
                                      p['lru_w_a'][j], p['lru_b_a'][j], p['lru_w_i'][j], p['lru_b_i'][j],
                                      p['lru_lambda'][j], p['lru_w_out'][j])
            new_lh.append(hT)
            new_lc.append(cb)
        else:
            mix, C, n, m, cb = mlstm_mixer(hm, ml_C[j], ml_n[j], ml_m[j], ml_conv[j], p['ml_w_in'][j], p['ml_conv_w'][j],
                                           p['ml_conv_b'][j], p['ml_w_q'][j], p['ml_w_k'][j], p['ml_w_v'][j],
                                           p['ml_w_ig'][j], p['ml_b_ig'][j], p['ml_w_fg'][j], p['ml_b_fg'][j],
                                           p['ml_skip'][j], p['ml_ln_g'][j], p['ml_w_out'][j])
            new_C.append(C)
            new_n.append(n)
            new_m.append(m)
            new_mc.append(cb)
        x = x + g1 * mix
        hf = rmsnorm(x, p['norm_ffn'][l]) * (1.0 + sc2) + sh2
        x = x + g2 * peer_ffn(hf, p['peer_w_q'][l], p['peer_keys'][l], p['peer_u'][l], p['peer_v'][l])
    y = rmsnorm(x, p['norm_f']).astype(out_dtype)
    return y, (jnp.stack(new_lh), jnp.stack(new_lc), jnp.stack(new_C), jnp.stack(new_n), jnp.stack(new_m), jnp.stack(new_mc))

def setup_inputs(seed: int = 0) -> dict:
    key = jax.random.key(seed)
    ks = list(jax.random.split(key, 64))

    def nrm(shape, scale):
        return jax.random.normal(ks.pop(), shape, jnp.float32) * scale

    D = D_MODEL
    NA, NB = N_LRU_LAYERS, N_MLSTM_LAYERS
    u_lam = jax.random.uniform(ks.pop(), (NA, D_RNN), jnp.float32, 0.9, 0.999)
    a_base = u_lam ** (1.0 / LRU_C)
    lru_lambda = jnp.log(a_base) - jnp.log1p(-a_base)
    fg_bias = jnp.broadcast_to(jnp.linspace(3.0, 6.0, M_HEADS, dtype=jnp.float32), (NB, M_HEADS)) + nrm((NB, M_HEADS), 0.1)
    return {
        'x_prompt': nrm((BATCH, SEQ, D), 1.0),
        'x_sample': nrm((DEC_BATCH, DEC_SEQ, D), 1.0),
        'c_prompt': nrm((BATCH, D), 1.0),
        'c_sample': nrm((DEC_BATCH, D), 1.0),
        'state_lru_h': nrm((NA, DEC_BATCH, D_RNN), 0.5),
        'state_lru_conv': nrm((NA, DEC_BATCH, CONV_W - 1, D_RNN), 1.0),
        'state_mlstm_C': nrm((NB, DEC_BATCH, M_HEADS, M_HD, M_HD), M_HD ** -0.5),
        'state_mlstm_n': nrm((NB, DEC_BATCH, M_HEADS, M_HD), 0.1),
        'state_mlstm_m': nrm((NB, DEC_BATCH, M_HEADS), 0.5),
        'state_mlstm_conv': nrm((NB, DEC_BATCH, CONV_W - 1, M_INNER), 1.0),
        'w_ada': nrm((DEPTH, D, 6 * D), 0.3 * D ** -0.5),
        'b_ada': nrm((DEPTH, 6 * D), 0.02),
        'norm_mix': 1.0 + nrm((DEPTH, D), 0.02),
        'norm_ffn': 1.0 + nrm((DEPTH, D), 0.02),
        'norm_f': 1.0 + nrm((D,), 0.02),
        'lru_w_in': nrm((NA, D, 2 * D_RNN), D ** -0.5),
        'lru_conv_w': nrm((NA, CONV_W, D_RNN), 0.5),
        'lru_conv_b': nrm((NA, D_RNN), 0.02),
        'lru_w_a': nrm((NA, LRU_BLOCKS, LRU_BW, LRU_BW), LRU_BW ** -0.5),
        'lru_b_a': nrm((NA, D_RNN), 0.02),
        'lru_w_i': nrm((NA, LRU_BLOCKS, LRU_BW, LRU_BW), LRU_BW ** -0.5),
        'lru_b_i': nrm((NA, D_RNN), 0.02),
        'lru_lambda': lru_lambda,
        'lru_w_out': nrm((NA, D_RNN, D), D_RNN ** -0.5),
        'ml_w_in': nrm((NB, D, 2 * M_INNER), D ** -0.5),
        'ml_conv_w': nrm((NB, CONV_W, M_INNER), 0.5),
        'ml_conv_b': nrm((NB, M_INNER), 0.02),
        'ml_w_q': nrm((NB, M_INNER // QKV_BS, QKV_BS, QKV_BS), QKV_BS ** -0.5),
        'ml_w_k': nrm((NB, M_INNER // QKV_BS, QKV_BS, QKV_BS), QKV_BS ** -0.5),
        'ml_w_v': nrm((NB, M_INNER // QKV_BS, QKV_BS, QKV_BS), QKV_BS ** -0.5),
        'ml_w_ig': nrm((NB, 3 * M_INNER, M_HEADS), 0.5 * (3 * M_INNER) ** -0.5),
        'ml_b_ig': nrm((NB, M_HEADS), 0.1),
        'ml_w_fg': nrm((NB, 3 * M_INNER, M_HEADS), 0.5 * (3 * M_INNER) ** -0.5),
        'ml_b_fg': fg_bias,
        'ml_skip': 1.0 + nrm((NB, M_INNER), 0.02),
        'ml_ln_g': 1.0 + nrm((NB, M_INNER), 0.02),
        'ml_w_out': nrm((NB, M_INNER, D), M_INNER ** -0.5),
        'peer_w_q': nrm((DEPTH, D, P_HEADS * P_DKEY), D ** -0.5),
        'peer_keys': nrm((DEPTH, P_HEADS, 2, N_KEYS, P_HALF), P_HALF ** -0.5),
        'peer_u': nrm((DEPTH, N_EXPERTS, D), D ** -0.5),
        'peer_v': nrm((DEPTH, N_EXPERTS, D), 0.5),
    }

def reference(x_prompt, x_sample, c_prompt, c_sample, state_lru_h, state_lru_conv, state_mlstm_C, state_mlstm_n,
              state_mlstm_m, state_mlstm_conv, w_ada, b_ada, norm_mix, norm_ffn, norm_f, lru_w_in, lru_conv_w,
              lru_conv_b, lru_w_a, lru_b_a, lru_w_i, lru_b_i, lru_lambda, lru_w_out, ml_w_in, ml_conv_w, ml_conv_b,
              ml_w_q, ml_w_k, ml_w_v, ml_w_ig, ml_b_ig, ml_w_fg, ml_b_fg, ml_skip, ml_ln_g, ml_w_out, peer_w_q,
              peer_keys, peer_u, peer_v):
    p = dict(w_ada=w_ada, b_ada=b_ada, norm_mix=norm_mix, norm_ffn=norm_ffn, norm_f=norm_f,
             lru_w_in=lru_w_in, lru_conv_w=lru_conv_w, lru_conv_b=lru_conv_b, lru_w_a=lru_w_a, lru_b_a=lru_b_a,
             lru_w_i=lru_w_i, lru_b_i=lru_b_i, lru_lambda=lru_lambda, lru_w_out=lru_w_out,
             ml_w_in=ml_w_in, ml_conv_w=ml_conv_w, ml_conv_b=ml_conv_b, ml_w_q=ml_w_q, ml_w_k=ml_w_k, ml_w_v=ml_w_v,
             ml_w_ig=ml_w_ig, ml_b_ig=ml_b_ig, ml_w_fg=ml_w_fg, ml_b_fg=ml_b_fg, ml_skip=ml_skip, ml_ln_g=ml_ln_g,
             ml_w_out=ml_w_out, peer_w_q=peer_w_q, peer_keys=peer_keys, peer_u=peer_u, peer_v=peer_v)
    B = x_prompt.shape[0]
    f32 = jnp.float32
    z_lh = jnp.zeros((N_LRU_LAYERS, B, D_RNN), f32)
    z_lc = jnp.zeros((N_LRU_LAYERS, B, CONV_W - 1, D_RNN), f32)
    z_C = jnp.zeros((N_MLSTM_LAYERS, B, M_HEADS, M_HD, M_HD), f32)
    z_n = jnp.zeros((N_MLSTM_LAYERS, B, M_HEADS, M_HD), f32)
    z_m = jnp.zeros((N_MLSTM_LAYERS, B, M_HEADS), f32)
    z_mc = jnp.zeros((N_MLSTM_LAYERS, B, CONV_W - 1, M_INNER), f32)
    y_prompt, (lh_p, lc_p, C_p, n_p, m_p, mc_p) = trunk(x_prompt, c_prompt, z_lh, z_lc, z_C, z_n, z_m, z_mc, p)
    y_sample, (lh_s, lc_s, C_s, n_s, m_s, mc_s) = trunk(x_sample, c_sample, state_lru_h, state_lru_conv, state_mlstm_C,
                                                        state_mlstm_n, state_mlstm_m, state_mlstm_conv, p)
    return (y_prompt, y_sample, lh_p, lc_p, C_p, n_p, m_p, mc_p, lh_s, lc_s, C_s, n_s, m_s, mc_s)


_drawn_inputs = setup_inputs


def setup_inputs(seed=0):
    import zlib

    import numpy as np

    out = dict(_drawn_inputs(seed))
    spreads = {}
    factors = {'norm_ffn': 3.333,
     'norm_f': 2.89,
     'lru_b_a': 8.0,
     'lru_b_i': 6.891,
     'ml_skip': 8.0,
     'ml_ln_g': 8.0}
    for name, (base, spread) in spreads.items():
        noise = np.random.default_rng([zlib.crc32(name.encode()), seed]).standard_normal(out[name].shape)
        drawn = base * np.exp(spread * noise) if base else spread * noise
        out[name] = __import__('jax').numpy.asarray(drawn.astype(out[name].dtype))
    for name, factor in factors.items():
        out[name] = (out[name] * factor).astype(out[name].dtype)
    return out
```

```python
from contextlib import ExitStack

import concourse.bass as bass
from concourse import mybir

ALU = mybir.AluOpType
ACT = mybir.ActivationFunctionType
F32 = mybir.dt.float32
U32 = mybir.dt.uint32
AX_X = mybir.AxisListType.X

P = 128
TILE = 1024
SLOTS = 8
PAIRS = SLOTS // 2
BANK = 512
LRU_C = 8.0
EPS = 1e-6
MASKED = -1e30
LOWEST = -3e38
N_LOG1P = 9


def column_layout(D, D_RNN, M_INNER):
    at, out = 0, {}
    kd, kr, km = D // P, D_RNN // P, M_INNER // P
    for name, n in [("norm_mix0", kd), ("norm_mix1", kd), ("norm_ffn0", kd), ("norm_ffn1", kd), ("norm_f", kd),
                    ("b_ada0", 6 * kd), ("b_ada1", 6 * kd), ("lru_conv_w", 4 * kr), ("lru_conv_b", kr),
                    ("lru_b_a", kr), ("lru_b_i", kr), ("lru_lambda", kr), ("ml_conv_w", 4 * km),
                    ("ml_conv_b", km), ("ml_skip", km), ("ml_ln_g", km), ("ml_b_ig", 1), ("ml_b_fg", 1),
                    ("ml_m0", 8)]:
        out[name] = (at, n)
        at += n
    return out, at


def tile_plan(D, D_RNN, M_INNER, DEPTH, N_KEYS):
    kd, kr, km = D // P, D_RNN // P, M_INNER // P
    at, first = 0, {}
    for name, n in [("ada0", 6 * kd), ("ada1", 6 * kd),
                    ("lru_in", 2 * kr), ("lru_gates", 2), ("lru_out", kd),
                    ("wq0", 16), ("keys0", 2), ("u0", N_KEYS), ("v0", N_KEYS),
                    ("ml_x", km), ("ml_qkv", 6), ("ml_z", km), ("ml_out", 2 * kd),
                    ("wq1", 16), ("keys1", 2), ("u1", N_KEYS), ("v1", N_KEYS)]:
        first[name] = at
        at += n
    return first, at


def decoder_step(nc, stream, cols_d, consts_d, c_d, x_d, lru_h_d, lru_conv_d, ml_conv_d, ml_n_d, gates_d, C_d,
                 y_o, lru_h_o, lru_conv_p_o, lru_conv_s_o, ml_conv_p_o, ml_conv_s_o, n_p_o, n_s_o, m_o,
                 C_p_o, C_s_o):
    NC, TOK = x_d.shape[1], x_d.shape[2]
    NSMP = lru_conv_d.shape[3]
    NPR = TOK - NSMP
    KM = ml_conv_d.shape[1]
    D, M_INNER = NC * P, KM * P
    HEADS = 4
    HC = KM // HEADS
    MHD = M_INNER // HEADS
    NSEQ = NSMP + 1
    KEYS = P
    PH, TOPK = 8, 16
    PICKS = PH * TOPK
    COL, NCOLS = column_layout(D, D, M_INNER)
    FIRST, NTILES = tile_plan(D, D, M_INNER, 2, KEYS)
    BLOCKS = [(0, 128), (128, 128), (256, NSMP)]
    NB = len(BLOCKS)
    assert D == TILE and NPR == 256 and NSMP == 8 and KM == 16

    with ExitStack() as ctx:
        def sb(name, shape, dt=F32):
            return ctx.enter_context(nc.sbuf_tensor(name, shape, dt))

        def sem(name):
            return ctx.enter_context(nc.semaphore(name))

        ring = sb("ring", [P, SLOTS, TILE])
        x = sb("x", [P, NC, TOK])
        h = sb("h", [P, NC, TOK])
        mod = [sb(f"mod{l}", [P, 6 * NC, NSEQ]) for l in range(2)]
        cols = sb("cols", [P, NCOLS])
        consts = sb("consts", [P, 3 * P + 2 * P])
        ident, iota, ones = (consts[:, i * P:(i + 1) * P] for i in range(3))
        causal = consts[:, 3 * P:5 * P]
        c_sb = sb("c_sb", [P, NC, NSEQ])
        scale = sb("scale", [P, NC, NSEQ])
        lam8 = sb("lam8", [P, NC])
        SCR = sb("SCR", [P, 4096])
        BIG = sb("BIG", [P, KEYS * TOK])
        ps = ctx.enter_context(nc.psum_tensor("ps", [P, 8, BANK], F32))

        def big(at, *shape):
            n = 1
            for s in shape:
                n *= s
            assert at + n <= KEYS * TOK
            v = BIG[:, at:at + n]
            names = "abcd"[:len(shape)]
            if len(shape) == 1:
                return v
            return v.rearrange(f"p ({' '.join(names)}) -> p {' '.join(names)}", **dict(zip(names[1:], shape[1:])))

        def scr(at, *shape):
            n = 1
            for s in shape:
                n *= s
            assert at + n <= 4096
            v = SCR[:, at:at + n]
            names = "abcd"[:len(shape)]
            if len(shape) == 1:
                return v
            return v.rearrange(f"p ({' '.join(names)}) -> p {' '.join(names)}", **dict(zip(names[1:], shape[1:])))

        def col(name, i=0, n=1):
            return cols[:, COL[name][0] + i:COL[name][0] + i + n]

        NT = NC * TOK
        rstd = scr(0, TOK)
        xp = big(0, NC, 3 + NPR)
        xs = big(NC * (3 + NPR), NC, 4, NSMP)
        LB = NC * (3 + NPR) + NC * 4 * NSMP
        ybr, xr, ra, ig, la, bx = (big(LB + i * NT, NC, TOK) for i in range(6))
        sq = ra
        h0 = big(LB + 6 * NT, NC, NSMP)
        stmp = big(LB + 6 * NT + NC * NSMP, NC, NSMP)
        MT = KM * TOK
        xm = big(0, KM, 3 + NPR)
        xms = big(KM * (3 + NPR), KM, 4, NSMP)
        MB = KM * (3 + NPR) + KM * 4 * NSMP
        xc, qT, kT, vT = (big(MB + i * MT, KM, TOK) for i in range(4))
        hT = vT
        z = big(0, KM, TOK)
        hsq = kT
        VB = MB + 4 * MT
        vt, kt = (big(VB + i * 2 * M_INNER, 2, M_INNER) for i in range(2))
        Cbuf = big(VB, 4, HC, MHD)
        Cst = big(0, 8, MHD)
        RB = VB + 4 * M_INNER
        vs = big(RB, M_INNER)
        GB = RB + M_INNER
        gates = big(GB, 3 * KM, 2 * HEADS)
        irow = big(GB + 384, TOK)
        frow = big(GB + 384 + TOK, TOK)
        Grow = big(GB + 384 + 2 * TOK, TOK)
        mrow = big(GB + 384 + 3 * TOK, TOK)
        nst = big(GB + 384 + 4 * TOK, KM, NSMP)
        SB0 = GB + 384 + 4 * TOK + KM * NSMP
        kw = big(SB0, KM, NSMP)
        bc = big(SB0 + 128, HEADS, 3, NSMP)
        gcol = big(SB0 + 224, 8)
        srow = big(SB0 + 232, 3, NSMP)
        sden = big(SB0 + 256, HEADS, NSMP)
        npr = big(SB0 + 288, KM)
        qn = big(GB, KM, NSMP)
        em = big(0, HEADS, NPR)
        Wt = scr(0, HEADS, 384)
        Sw = scr(1536, HEADS, 384)
        vk = [scr(i * 2048, HC, MHD) for i in range(2)]
        hstd = scr(0, HEADS, TOK)
        exp_f, zero, Frow, t_a, t_b, t_c = (scr(i * TOK, TOK) for i in range(6))
        G = big(0, KEYS, TOK)
        G_FREE = 62
        TB = G_FREE * TOK
        pq = big(TB, 16, TOK)
        S = big(TB + 16 * TOK, NB, 16, KEYS)
        TC = TB + 16 * TOK + NB * 2048
        cand = big(TC, PH, TOPK * TOPK)
        eq = big(TC + 2048, PICKS, TOPK)
        vals = big(TC + 4096, 16, TOPK)
        idxf = big(TC + 4352, 16, TOPK)
        top = big(TC + 4608, PH, TOPK)
        abf = big(TC + 4736, 2, PICKS)
        idx = big(TC + 4992, 16, TOPK).bitcast(U32)
        pos = big(TC + 5248, PH, TOPK).bitcast(U32)
        ab = big(TC + 5376, 2, PICKS).bitcast(U32)
        ssum = big(TC + 5632, PH)
        wexp = big(TC + 5640, PH, TOPK)
        picks = scr(0, NB, 3, PICKS)
        pickT = scr(1152, 3, TOK)
        oh_j = [scr(1952 + i * 1024, 4, KEYS) for i in range(2)]
        oh_i = [scr(1952 + i * 1024 + 512, 4, KEYS) for i in range(2)]

        pair_in = [sem(f"pair_in{i}") for i in range(PAIRS)]
        pairs_used = sem("pairs_used")
        inputs_in = sem("inputs_in")
        ml_inputs_in = sem("ml_inputs_in")
        dve_seq = sem("dve_seq")
        ada_done = sem("ada_done")
        mod_ready = sem("mod_ready")
        squares_done = sem("squares_done")
        ssq_done = sem("ssq_done")
        ms_ready = sem("ms_ready")
        rms_ready = sem("rms_ready")
        h_ready = sem("h_ready")
        out_done = sem("out_done")
        x_ready = sem("x_ready")
        lin_done = sem("lin_done")
        lin_x = sem("lin_x")
        lin_y = sem("lin_y")
        lam_exp = sem("lam_exp")
        xr_ready = sem("xr_ready")
        lgate_done = sem("lgate_done")
        lgate_act = sem("lgate_act")
        loga_ready = sem("loga_ready")
        a_ready = sem("a_ready")
        tt_ready = sem("tt_ready")
        sqrt_ready = sem("sqrt_ready")
        hs_ready = sem("hs_ready")
        ly_ready = sem("ly_ready")
        stores = sem("stores")
        mx_done = sem("mx_done")
        mx_copied = sem("mx_copied")
        conv_ready = sem("conv_ready")
        xc_ready = sem("xc_ready")
        qkv_done = sem("qkv_done")
        qkv_act = sem("qkv_act")
        vk_done = sem("vk_done")
        vk_copied = sem("vk_copied")
        gate_done = sem("gate_done")
        gate_raw = sem("gate_raw")
        gate_exp = sem("gate_exp")
        rows_ready = sem("rows_ready")
        bcast_done = sem("bcast_done")
        srow_exp = sem("srow_exp")
        gcol_done = sem("gcol_done")
        st_done = sem("st_done")
        wexp_in = sem("wexp_in")
        w_ready = sem("w_ready")
        em_ready = sem("em_ready")
        sw_ready = sem("sw_ready")
        den_done = sem("den_done")
        num_done = sem("num_done")
        num_read = sem("num_read")
        kw_ready = sem("kw_ready")
        cp_done = sem("cp_done")
        cp_copied = sem("cp_copied")
        cp_stored = [sem(f"cp_stored{i}") for i in range(8)]
        sbc_done = sem("sbc_done")
        sqn_ready = sem("sqn_ready")
        sden_done = sem("sden_done")
        C_in = [sem(f"C_in{i}") for i in range(4)]
        C_out = [sem(f"C_out{i}") for i in range(4)]
        vb_done = sem("vb_done")
        vb_used = sem("vb_used")
        C_new = sem("C_new")
        C_read = sem("C_read")
        hT_ready = sem("hT_ready")
        mu_done = sem("mu_done")
        hc_ready = sem("hc_ready")
        hsq_ready = sem("hsq_ready")
        var_done = sem("var_done")
        hvar_ready = sem("hvar_ready")
        hstd_ready = sem("hstd_ready")
        z_done = sem("z_done")
        z_ready = sem("z_ready")
        mly_ready = sem("mly_ready")
        pq_done = [sem(f"pq_done{l}") for l in range(2)]
        pq_ready = [sem(f"pq_ready{l}") for l in range(2)]
        sc_done = [sem(f"sc_done{l}") for l in range(2)]
        sc_ready = [sem(f"sc_ready{l}") for l in range(2)]
        u_done = [sem(f"u_done{l}") for l in range(2)]
        g_ready = [sem(f"g_ready{l}") for l in range(2)]
        top_ready = [sem(f"top_ready{l}") for l in range(2)]
        topexp_ready = [sem(f"topexp_ready{l}") for l in range(2)]
        picks_ready = [sem(f"picks_ready{l}") for l in range(2)]
        pickT_done = [sem(f"pickT_done{l}") for l in range(2)]
        pickT_ready = [sem(f"pickT_ready{l}") for l in range(2)]
        onehot_ready = [sem(f"onehot_ready{l}") for l in range(2)]
        route_done = [sem(f"route_done{l}") for l in range(2)]
        routed = [sem(f"routed{l}") for l in range(2)]
        y_ready = sem("y_ready")
        lam_abs = sem("lam_abs")
        ml_conv_stored = sem("ml_conv_stored")
        npr_ready = sem("npr_ready")

        block = ctx.enter_context(nc.Block())
        GROUPS = TOK // 4
        N_STORES = 10

        @block.sync
        def _(sp):
            def pair(n, slot):
                sp.dma_start(ring[:, 2 * slot:2 * slot + 2, :].rearrange("p a b -> p (a b)"),
                             stream[n]).then_inc(pair_in[slot], 16)

            for n in range(PAIRS):
                pair(n, n)
            rounds = NTILES // 2 // PAIRS
            with sp.Fori(1, rounds) as r:
                for s in range(PAIRS):
                    sp.wait_ge(pairs_used, r * PAIRS + (s - PAIRS + 1))
                    pair(r * PAIRS + s, s)
            for n in range(rounds * PAIRS, NTILES // 2):
                sp.wait_ge(pairs_used, n - PAIRS + 1)
                pair(n, n % PAIRS)

        @block.tensor
        def _(pe):
            def need(n0, k, r=0):
                if (n0 + k) % 2 == 0:
                    pe.wait_ge(pair_in[(n0 + k) // 2 % PAIRS], (r + (n0 + k) // SLOTS + 1) * 16)

            def w_at(n0, k, c):
                return ring[:, (n0 + k) % SLOTS, c * P:(c + 1) * P]

            def begins(ins, n0, k):
                if (n0 + k) % 2 == 0:
                    ins.then_inc(pairs_used, 1)

            def mm(out, lhsT, rhs, start=True, stop=True, shared=False):
                return nc.tensor.matmul(out, lhsT, rhs, start=start, stop=stop, skip_group_check=shared)

            def chunk(out, n0, k, src, first=False):
                for c in range(NC):
                    last = mm(out, w_at(n0, k, c), src(c), c == 0, c == NC - 1)
                    if c == 0 and not first:
                        begins(last, n0, k)
                return last

            def h_in(c):
                return h[:, c, :]

            def norm_sum(n):
                pe.wait_ge(squares_done, n + 1)
                for c in range(NC):
                    last = mm(ps[:, 0, 0:TOK], ones, sq[:, c, :], c == 0, c == NC - 1)
                last.then_inc(ssq_done, 1)

            def residual_out(name, rhs, KC):
                per = KC // NC
                for m in range(NC):
                    for t in range(per):
                        k = m * per + t
                        need(FIRST[name], k)
                        for c in range(NC):
                            last = mm(ps[:, m, 0:TOK], w_at(FIRST[name], k, c), rhs[:, t * NC + c, :],
                                      t == 0 and c == 0, t == per - 1 and c == NC - 1)
                            if c == 0:
                                begins(last, FIRST[name], k)
                last.then_inc(out_done, 1)

            pe.wait_ge(inputs_in, 16 * 6)

            def ada(l, r):
                n0 = FIRST[f"ada{l}"]
                for k in range(SLOTS):
                    need(n0, k, r)
                    last = chunk(ps[:, 6 + l, bass.ds(r * (SLOTS * NSEQ) + k * NSEQ, NSEQ)], n0, k,
                                 lambda c: c_sb[:, c, :], first=l == 0 and isinstance(r, int) and k == 0)
                last.then_inc(ada_done, 1)
            for l in range(2):
                ada(l, 0)
                with pe.Fori(1, 6 * NC // SLOTS) as r:
                    ada(l, r)

            norm_sum(0)
            pe.wait_ge(h_ready, 1)
            n0 = FIRST["lru_in"]
            for k in range(2 * NC):
                need(n0, k)
                if k >= 4:
                    if k - 4 < NC:
                        pe.wait_ge(lin_x, k - 3)
                    else:
                        pe.wait_ge(lin_y, k - 3 - NC)
                chunk(ps[:, k % 4, 0:TOK], n0, k, h_in).then_inc(lin_done, 1)
            n0 = FIRST["lru_gates"]
            need(n0, 0)
            pe.wait_ge(xr_ready, 1)
            pe.wait_ge(lin_y, NC)
            for g in range(2):
                for c in range(NC):
                    n = g * NC + c
                    if n >= 6:
                        pe.wait_ge(lgate_act, n - 5)
                    if n == 0:
                        begins(mm(ps[:, 0, NPR:TOK], w_at(n0, 0, 0), xr[:, 0, NPR:TOK]), n0, 0)
                        last = mm(ps[:, 0, 0:NPR], w_at(n0, 0, 0), xr[:, 0, 0:NPR])
                    else:
                        last = mm(ps[:, n % 6, 0:TOK], w_at(n0, g, c), xr[:, c, :])
                    last.then_inc(lgate_done, 1)
            pe.wait_ge(ly_ready, 1)
            pe.wait_ge(mod_ready, 2)
            residual_out("lru_out", ybr, NC)

            def peer(l):
                pe.wait_ge(x_ready, 2 * l + 1)
                norm_sum(2 * l + 1)
                pe.wait_ge(h_ready, 2 * l + 2)
                n0 = FIRST[f"wq{l}"]
                for k in range(2 * PH):
                    need(n0, k)
                    if k >= 4:
                        pe.wait_ge(pq_ready[l], k - 3)
                    chunk(ps[:, k % 4, 0:TOK], n0, k, h_in).then_inc(pq_done[l], 1)
                n0 = FIRST[f"keys{l}"]
                need(n0, 0)
                pe.wait_ge(pq_ready[l], 2 * PH)
                n = 0
                for b, (t0, nb) in enumerate(BLOCKS):
                    for q in range(4):
                        if n >= 4:
                            pe.wait_ge(sc_ready[l], n - 3)
                        for i in range(4):
                            k = 4 * q + i
                            last = mm(ps[0:nb, 4 + n % 4, i * P:(i + 1) * P], pq[:, k, t0:t0 + nb],
                                      w_at(n0, k // 8, k % 8))
                            if n == 0 and i == 0:
                                begins(last, n0, 0)
                        last.then_inc(sc_done[l], 1)
                        n += 1
                n0 = FIRST[f"u{l}"]

                def u_round(r):
                    for k in range(SLOTS):
                        need(n0, k, r)
                        if not (isinstance(r, int) and k < 4):
                            pe.wait_ge(g_ready[l], r * SLOTS + (k - 3))
                        chunk(ps[:, k % 4, 0:TOK], n0, k, h_in).then_inc(u_done[l], 1)
                u_round(0)
                with pe.Fori(1, KEYS // SLOTS) as r:
                    u_round(r)
                for b, (t0, nb) in enumerate(BLOCKS):
                    pe.wait_ge(picks_ready[l], b + 1)
                    for i in range(3):
                        last = nc.tensor.transpose(ps[:, 4 + b, i * P:i * P + nb], picks[0:nb, b, i, :],
                                                   ident[0:nb, 0:nb])
                    last.then_inc(pickT_done[l], 1)

                def route(s):
                    for i in range(4):
                        last = mm(ps[:, s, i * P:(i + 1) * P], oh_j[s][:, i, :], oh_i[s][:, i, :])
                    last.then_inc(route_done[l], 1)
                pe.wait_ge(g_ready[l], KEYS)
                for g in range(2):
                    pe.wait_ge(onehot_ready[l], g + 1)
                    route(g)
                with pe.Fori(1, GROUPS // 2) as r:
                    for s in range(2):
                        pe.wait_ge(onehot_ready[l], r * 2 + (s + 1))
                        pe.wait_ge(routed[l], r * 2 + (s - 1))
                        route(s)
                n0 = FIRST[f"v{l}"]
                pe.wait_ge(routed[l], GROUPS)

                def v_round(r, first=False, end=False):
                    for k in range(SLOTS):
                        need(n0, k, r)
                        for m in range(NC):
                            last = mm(ps[:, m, 0:TOK], w_at(n0, k, m),
                                      BIG[:, bass.ds(r * (SLOTS * TOK) + k * TOK, TOK)],
                                      first and k == 0, end and k == SLOTS - 1)
                            if m == 0:
                                begins(last, n0, k)
                    return last
                v_round(0, first=True)
                with pe.Fori(1, KEYS // SLOTS - 1) as r:
                    v_round(r)
                v_round(KEYS // SLOTS - 1, end=True).then_inc(out_done, 1)

            peer(0)

            pe.wait_ge(x_ready, 2)
            norm_sum(2)
            pe.wait_ge(h_ready, 3)
            n0 = FIRST["ml_x"]
            for k in range(KM):
                need(n0, k)
                if k >= 4:
                    pe.wait_ge(mx_copied, k - 3)
                chunk(ps[:, k % 4, 0:TOK], n0, k, h_in).then_inc(mx_done, 1)
            n0 = FIRST["ml_qkv"]
            pe.wait_ge(ml_inputs_in, 16 * 3)
            pe.wait_ge(mx_copied, KM)
            pe.wait_ge(xc_ready, 1)
            n = nt = 0
            for j in range(3):
                need(n0, 2 * j)

                def tokens(c, lo, hi):
                    if j < 2:
                        return xc[:, c, lo:hi]
                    return xms[:, c, 3, :] if lo == NPR else xm[:, c, 3 + lo:3 + hi]
                for c in range(KM):
                    if n >= 4:
                        pe.wait_ge(qkv_act, n - 3)
                    w = w_at(n0, 2 * j + c // NC, c % NC)
                    first = mm(ps[:, 4 + n % 4, NPR:TOK], w, tokens(c, NPR, TOK))
                    if c == 0:
                        begins(first, n0, 2 * j)
                    mm(ps[:, 4 + n % 4, 0:NPR], w, tokens(c, 0, NPR)).then_inc(qkv_done, 1)
                    n += 1
                for t0, nb in BLOCKS[:(0, 2, 3)[j]]:
                    for q in range(KM // 4):
                        if nt >= 4:
                            pe.wait_ge(vk_copied, nt - 3)
                        for i in range(4):
                            c = 4 * q + i
                            last = mm(ps[0:nb, nt % 4, i * P:(i + 1) * P], tokens(c, t0, t0 + nb),
                                      w_at(n0, 2 * j + c // NC, c % NC))
                        last.then_inc(vk_done, 1)
                        nt += 1
            pe.wait_ge(qkv_act, 3 * KM)
            for g in range(2):
                for j, src in enumerate((qT, kT, vT)):
                    for c in range(KM):
                        last = mm(ps[0:HEADS, 4 + g, 0:TOK], gates[:, j * KM + c, g * HEADS:(g + 1) * HEADS],
                                  src[:, c, :], j == 0 and c == 0, j == 2 and c == KM - 1)
            last.then_inc(gate_done, 1)
            pe.wait_ge(vk_copied, nt)
            for hd in range(HEADS):
                for b in range(2):
                    o = ps[:, hd, 0:NPR] if b == 0 else ps[:, hd, NPR:NPR + P]
                    for c in range(HC):
                        last = mm(o, kT[:, hd * HC + c, b * P:(b + 1) * P], qT[:, hd * HC + c, b * P:NPR],
                                  c == 0, c == HC - 1)
            last.then_inc(st_done, 1)
            pe.wait_ge(rows_ready, 1)
            for hd in range(HEADS):
                pick = ident[0:HEADS, hd:hd + 1].to_broadcast([HEADS, P])
                half = slice(hd % 2 * NPR, (hd % 2 + 1) * NPR)
                mm(ps[:, 4 + hd // 2, half], pick, frow[0:HEADS, 0:NPR])
                last = mm(ps[:, 6 + hd // 2, half], pick, mrow[0:HEADS, 0:NPR])
            last.then_inc(bcast_done, 1)
            pe.wait_ge(em_ready, 1)
            for b in range(2):
                last = nc.tensor.transpose(ps[:, 6, b * HEADS:(b + 1) * HEADS], Grow[0:HEADS, b * P:(b + 1) * P],
                                           ident[0:HEADS, 0:HEADS])
            last.then_inc(gcol_done, 1)
            pe.wait_ge(srow_exp, 1)
            for hd in range(HEADS):
                last = mm(ps[:, 7, hd * 3 * NSMP:(hd + 1) * 3 * NSMP],
                          ident[0:HEADS, hd:hd + 1].to_broadcast([HEADS, P]),
                          srow[0:HEADS].rearrange("p a b -> p (a b)"))
            last.then_inc(sbc_done, 1)
            pe.wait_ge(sw_ready, 1)
            for hd in range(HEADS):
                o = ps[:, 4 + hd // 2, hd % 2 * NPR:(hd % 2 + 1) * NPR]
                mm(o, ones, Sw[:, hd, 0:NPR])
                last = mm(o[:, P:NPR], ones, Sw[:, hd, NPR:NPR + P], False, True, True)
            last.then_inc(den_done, 1)
            for hd in range(HEADS):
                if hd >= 2:
                    pe.wait_ge(num_read, hd - 1)
                for e in range(HC):
                    o = ps[:, hd % 2 * 2 + e // 2, e % 2 * NPR:(e % 2 + 1) * NPR]
                    e0 = (hd * HC + e) * P
                    mm(o, vt[:, 0, e0:e0 + P], Sw[:, hd, 0:NPR])
                    last = mm(o[:, P:NPR], vt[:, 1, e0:e0 + P], Sw[:, hd, NPR:NPR + P], False, True, True)
                last.then_inc(num_done, 1)
            pe.wait_ge(sqn_ready, 1)
            for hd in range(HEADS):
                for c in range(HC):
                    last = mm(ps[:, 7, P + hd * NSMP:P + (hd + 1) * NSMP], ones, qn[:, hd * HC + c, :],
                              c == 0, c == HC - 1)
            last.then_inc(sden_done, 1)
            pe.wait_ge(kw_ready, 1)
            pe.wait_ge(num_read, HEADS)
            for n in range(KM):
                hd = n // HC
                if n >= 4:
                    pe.wait_ge(cp_copied, n - 3)
                for b in range(2):
                    mm(ps[:, 6, 16 + n:17 + n], kt[:, b, n * P:(n + 1) * P], ones[:, 0:1], b == 0, b == 1)
                for b in range(2):
                    last = mm(ps[:, n % 4, :], kt[:, b, n * P:(n + 1) * P],
                              vt[:, b, hd * MHD:(hd + 1) * MHD], b == 0, b == 1)
                last.then_inc(cp_done, 1)
            pe.wait_ge(cp_copied, KM)

            def read_C(m):
                b, hd = m // HEADS, m % HEADS
                pe.wait_ge(C_new, m + 1)
                for e in range(HC):
                    o = (hd * HC + e) * NSMP + b
                    for c in range(HC):
                        last = mm(ps[:, 2, o:o + 1], Cbuf[:, m % 4, c, e * P:(e + 1) * P],
                                  qT[:, hd * HC + c, NPR + b:NPR + b + 1], c == 0, c == HC - 1)
                last.then_inc(C_read, 1)
            for m in range(NSMP * HEADS):
                b, hd = m // HEADS, m % HEADS
                if m >= 2:
                    pe.wait_ge(vb_used, m - 1)
                mm(ps[:, m % 2, :], ident[0:NSMP, b:b + 1].to_broadcast([NSMP, P]),
                   vs[0:NSMP, hd * MHD:(hd + 1) * MHD]).then_inc(vb_done, 1)
                if m >= 1:
                    read_C(m - 1)
            read_C(NSMP * HEADS - 1)
            pe.wait_ge(hT_ready, 1)
            for src, ready in ((hT, mu_done), (hsq, var_done)):
                if src is hsq:
                    pe.wait_ge(hsq_ready, 1)
                for hd in range(HEADS):
                    for c in range(HC):
                        last = mm(ps[:, 4 + hd, 0:TOK], ones, src[:, hd * HC + c, :], c == 0, c == HC - 1)
                last.then_inc(ready, 1)
            n0 = FIRST["ml_z"]
            for k in range(KM):
                need(n0, k)
                if k >= 4:
                    pe.wait_ge(z_ready, k - 3)
                chunk(ps[:, k % 4, 0:TOK], n0, k, h_in).then_inc(z_done, 1)
            pe.wait_ge(mly_ready, 1)
            residual_out("ml_out", hT, KM)
            peer(1)
            pe.wait_ge(x_ready, 4)
            norm_sum(4)

        @block.scalar
        def _(act):
            def flat(v):
                return v.rearrange("p c t -> p (c t)")

            def func(to, of, f, **kw_):
                return nc.scalar.activation(to, of, f, **kw_)

            for to, of in ((c_sb[:], c_d), (cols[:], cols_d), (consts[:], consts_d), (x[:], x_d), (h0, lru_h_d)):
                act.dma_start(to, of).then_inc(inputs_in, 16)
            act.dma_start(xs[:, :, 0:3, :].rearrange("p c j b -> p c (j b)"),
                          lru_conv_d.rearrange("p c j b -> p c (j b)")).then_inc(inputs_in, 16)
            act.wait_ge(inputs_in, 16 * 6)

            def norm(n):
                if n > 0:
                    act.wait_ge(x_ready, n)
                func(flat(sq), flat(x[:]), ACT.Square).then_inc(squares_done, 1)
                act.wait_ge(ms_ready, n + 1)
                func(rstd, rstd, ACT.Sqrt).then_inc(rms_ready, 1)

            func(lam8[:], col("lru_lambda", 0, NC), ACT.Abs).then_inc(lam_abs, 1)
            act.wait_ge(lam_abs, 1)
            func(lam8[:], lam8[:], ACT.Exp, scale=-1.0).then_inc(lam_exp, 1)
            norm(0)
            for c in range(NC):
                act.wait_ge(lin_done, NC + c + 1)
                func(ybr[:, c, :], ps[:, (NC + c) % 4, 0:TOK], ACT.Gelu_apprx_tanh).then_inc(lin_y, 1)
            act.wait_ge(h_ready, 1)
            for g, (to, bias) in enumerate(((ra, "lru_b_a"), (ig, "lru_b_i"))):
                for c in range(NC):
                    n = g * NC + c
                    act.wait_ge(lgate_done, n + 1)
                    func(to[:, c, :], ps[:, n % 6, 0:TOK], ACT.Sigmoid, bias=col(bias, c)).then_inc(lgate_act, 1)
            act.wait_ge(loga_ready, 1)
            func(flat(ra), flat(la), ACT.Exp).then_inc(a_ready, 1)
            act.wait_ge(a_ready, 1)
            func(flat(la), flat(la), ACT.Tanh, scale=-1.0).then_inc(a_ready, 1)
            act.wait_ge(tt_ready, 1)
            func(flat(la), flat(la), ACT.Sqrt).then_inc(sqrt_ready, 1)

            def peer(l):
                norm(2 * l + 1)
                for k in range(2 * PH):
                    act.wait_ge(pq_done[l], k + 1)
                    func(pq[:, k, :], ps[:, k % 4, 0:TOK], ACT.Copy).then_inc(pq_ready[l], 1)
                if l == 1:
                    act.wait_ge(stores, 16 * 6)
                    for i in range(4):
                        act.wait_ge(C_out[i], 16 * NSMP * HEADS // 4)
                n = 0
                for b, (t0, nb) in enumerate(BLOCKS):
                    for q in range(4):
                        act.wait_ge(sc_done[l], n + 1)
                        func(flat(S[0:nb, b, 4 * q:4 * q + 4, :]), ps[0:nb, 4 + n % 4, :], ACT.Copy)\
                            .then_inc(sc_ready[l], 1)
                        n += 1

                def gelu(r, k):
                    act.wait_ge(u_done[l], r * 4 + (k + 1))
                    func(BIG[:, bass.ds(r * (4 * TOK) + k * TOK, TOK)], ps[:, k, 0:TOK], ACT.Gelu_apprx_tanh)\
                        .then_inc(g_ready[l], 1)
                if l == 0:
                    act.wait_ge(stores, 16 * 3)
                done = 0
                for b, until in enumerate((20, 40, 60)):
                    with act.Fori(done // 4, until // 4) as r:
                        for k in range(4):
                            gelu(r, k)
                    done = until
                    nb = BLOCKS[b][1]
                    act.wait_ge(top_ready[l], b + 1)
                    func(flat(wexp[0:nb]), flat(wexp[0:nb]), ACT.Exp).then_inc(topexp_ready[l], 1)
                act.wait_ge(picks_ready[l], NB)
                with act.Fori(done // 4, KEYS // 4) as r:
                    for k in range(4):
                        gelu(r, k)

            peer(0)

            norm(2)
            act.wait_ge(conv_ready, 1)
            func(flat(xc), flat(xc), ACT.Silu).then_inc(xc_ready, 1)
            n = 0
            for j, to in enumerate((qT, kT, vT)):
                for c in range(KM):
                    act.wait_ge(qkv_done, n + 1)
                    func(to[:, c, :], ps[:, 4 + n % 4, 0:TOK], ACT.Copy,
                         scale=float(MHD) ** -0.5 if j == 1 else 1.0).then_inc(qkv_act, 1)
                    n += 1
            act.wait_ge(gate_raw, 1)
            func(exp_f[0:HEADS], frow[0:HEADS], ACT.Abs).then_inc(gate_exp, 1)
            act.wait_ge(gate_exp, 1)
            func(exp_f[0:HEADS], exp_f[0:HEADS], ACT.Exp, scale=-1.0).then_inc(gate_exp, 1)
            act.wait_ge(bcast_done, 1)
            act.wait_ge(ml_conv_stored, 32)
            for i in range(2):
                last = func(flat(em[:, 2 * i:2 * i + 2, :]), ps[:, 6 + i, :], ACT.Exp, scale=-1.0)
            last.then_inc(em_ready, 1)
            act.wait_ge(rows_ready, 1)
            func(flat(srow[0:HEADS]), flat(srow[0:HEADS]), ACT.Exp).then_inc(srow_exp, 1)
            act.wait_ge(wexp_in, 1)
            for hd in range(HEADS):
                for b in range(2):
                    w = Wt[:, hd, 0:NPR] if b == 0 else Wt[:, hd, NPR:NPR + P]
                    last = func(w, w, ACT.Exp, bias=gcol[:, b * HEADS + hd:b * HEADS + hd + 1])
            last.then_inc(w_ready, 1)
            act.wait_ge(sqn_ready, 1)
            act.wait_ge(cp_copied, KM)
            for m in range(NSMP * HEADS):
                b, hd = m // HEADS, m % HEADS
                act.wait_ge(vb_done, m + 1)
                if m >= 2:
                    act.wait_ge(C_new, m - 1)
                for c in range(HC):
                    last = func(vk[m % 2][:, c, :], ps[:, m % 2, :], ACT.Copy, scale=kw[:, hd * HC + c, b:b + 1])
                last.then_inc(vb_used, 1)
            act.wait_ge(hc_ready, 1)
            func(flat(hsq), flat(hT), ACT.Square).then_inc(hsq_ready, 1)
            act.wait_ge(hvar_ready, 1)
            func(flat(hstd), flat(hstd), ACT.Sqrt).then_inc(hstd_ready, 1)
            for i in range(8):
                act.wait_ge(cp_stored[i], 16 * KM // 8)
            for k in range(KM):
                act.wait_ge(z_done, k + 1)
                func(z[:, k, :], ps[:, k % 4, 0:TOK], ACT.Silu).then_inc(z_ready, 1)
            peer(1)
            norm(4)

        @block.gpsimd
        def _(pool):
            def joined(v):
                return v.rearrange("p c j b -> p c (j b)")

            pool.wait_ge(hs_ready, 1)
            pool.dma_start(lru_h_o, xr[:, :, NPR - 1:TOK]).then_inc(stores, 16)
            pool.dma_start(lru_conv_p_o, xp[:, :, NPR:NPR + 3]).then_inc(stores, 16)
            pool.dma_start(joined(lru_conv_s_o), joined(xs[:, :, 1:4, :])).then_inc(stores, 16)
            pool.wait_ge(x_ready, 2)
            pool.dma_start(gates, gates_d).then_inc(ml_inputs_in, 16)
            pool.dma_start(nst, ml_n_d).then_inc(ml_inputs_in, 16)
            pool.dma_start(joined(xms[:, :, 0:3, :]), joined(ml_conv_d)).then_inc(ml_inputs_in, 16)
            pool.wait_ge(conv_ready, 1)
            pool.dma_start(ml_conv_p_o, xm[:, :, NPR:NPR + 3]).then_inc(ml_conv_stored, 16)
            pool.dma_start(joined(ml_conv_s_o), joined(xms[:, :, 1:4, :])).then_inc(ml_conv_stored, 16)
            pool.wait_ge(rows_ready, 1)
            pool.dma_start(m_o, mrow[0:HEADS, NPR - 1:TOK]).then_inc(stores, 16)
            pool.wait_ge(sqn_ready, 1)
            pool.dma_start(n_s_o, nst).then_inc(stores, 16)
            for n in range(KM):
                pool.wait_ge(cp_copied, n + 1)
                pool.dma_start(C_p_o[n], Cst[:, n % 8, :]).then_inc(cp_stored[n % 8], 16)
            pool.wait_ge(npr_ready, 1)
            pool.dma_start(n_p_o, npr).then_inc(stores, 16)
            pool.wait_ge(cp_done, KM)

            def load_C(m):
                pool.dma_start(Cbuf[:, m % 4, :, :].rearrange("p a b -> p (a b)"), C_d[m]).then_inc(C_in[m % 4], 16)
            for m in range(4):
                load_C(m)
            for m in range(NSMP * HEADS):
                pool.wait_ge(C_read, m + 1)
                pool.dma_start(C_s_o[m], Cbuf[:, m % 4, :, :].rearrange("p a b -> p (a b)")).then_inc(C_out[m % 4], 16)
                if m + 4 < NSMP * HEADS:
                    pool.wait_ge(C_out[m % 4], 16 * (m // 4 + 1))
                    load_C(m + 4)
            pool.wait_ge(y_ready, 1)
            pool.dma_start(y_o, h[:]).then_inc(stores, 16)
            pool.wait_ge(stores, 16 * 7)
            pool.wait_ge(ml_conv_stored, 16 * 2)
            for i in range(8):
                pool.wait_ge(cp_stored[i], 16 * KM // 8)
            for i in range(4):
                pool.wait_ge(C_out[i], 16 * NSMP * HEADS // 4)

        @block.vector
        def _(dve):
            count = [0]

            def link(ins):
                count[0] += 1
                ins.then_inc(dve_seq, 1)
                dve.wait_ge(dve_seq, count[0])

            vec = nc.vector
            tt, ts, stt = vec.tensor_tensor, vec.tensor_scalar, vec.scalar_tensor_tensor

            def flat(v):
                return v.rearrange("p c t -> p (c t)")

            def minus_softplus(out, raw, e, z_, z2, p, scale_):
                link(ts(z_, e, 2.0, None, ALU.add))
                link(vec.reciprocal(z_, z_))
                link(tt(z_, z_, e, ALU.mult))
                link(tt(z2, z_, z_, ALU.mult))
                link(ts(p, z2, 1.0 / (2 * N_LOG1P + 1), None, ALU.mult))
                for i in range(N_LOG1P - 1, 0, -1):
                    link(stt(p, p, 1.0 / (2 * i + 1), z2, ALU.add, ALU.mult))
                link(stt(p, p, 1.0, z_, ALU.add, ALU.mult))
                link(ts(out, raw, 0.0, None, ALU.min))
                link(stt(out, p, -2.0, out, ALU.mult, ALU.add))
                if scale_ != 1.0:
                    link(ts(out, out, scale_, None, ALU.mult))

            def over_tokens(v, n):
                return v.unsqueeze(2).to_broadcast([P, v.shape[1], n])

            def norm(n, gain, l, part):
                shift = mod[l][:, part * NC:(part + 1) * NC, :]
                link(stt(scale[:], mod[l][:, (part + 1) * NC:(part + 2) * NC, :], 1.0,
                         over_tokens(col(gain, 0, NC), NSEQ), ALU.add, ALU.mult))
                dve.wait_ge(ssq_done, n + 1)
                ts(rstd, ps[:, 0, 0:TOK], 1.0 / D, EPS, ALU.mult, ALU.add).then_inc(ms_ready, 1)
                dve.wait_ge(rms_ready, n + 1)
                link(vec.reciprocal(rstd, rstd))
                link(tt(h[:], x[:], rstd.unsqueeze(1).to_broadcast([P, NC, TOK]), ALU.mult))
                for c in range(NC):
                    ts(h[:, c, 0:NPR], h[:, c, 0:NPR], scale[:, c, 0:1], shift[:, c, 0:1], ALU.mult, ALU.add)
                link(tt(h[:, :, NPR:TOK], h[:, :, NPR:TOK], scale[:, :, 1:NSEQ], ALU.mult))
                tt(h[:, :, NPR:TOK], h[:, :, NPR:TOK], shift[:, :, 1:NSEQ], ALU.add).then_inc(h_ready, 1)

            def residual(n, l, part):
                gate = mod[l][:, part * NC:(part + 1) * NC, :]
                gated = scr(TOK, NC, NSMP)
                dve.wait_ge(out_done, n + 1)
                link(tt(gated, ps[:, 0:NC, NPR:TOK], gate[:, :, 1:NSEQ], ALU.mult))
                for m in range(NC):
                    stt(x[:, m, 0:NPR], ps[:, m, 0:NPR], gate[:, m, 0:1], x[:, m, 0:NPR], ALU.mult, ALU.add)
                tt(x[:, :, NPR:TOK], x[:, :, NPR:TOK], gated, ALU.add).then_inc(x_ready, 1)
                dve.wait_ge(x_ready, n + 1)

            def convolve(out, prompt, samples, chunks, w, b, tmp):
                nch = chunks
                for c in range(nch):
                    last = ts(out[:, c, 0:NPR], prompt[:, c, 0:NPR], col(w, c), col(b, c), ALU.mult, ALU.add)
                link(last)
                for j in range(1, 4):
                    for c in range(nch):
                        last = stt(out[:, c, 0:NPR], prompt[:, c, j:j + NPR], col(w, j * nch + c),
                                   out[:, c, 0:NPR], ALU.mult, ALU.add)
                    link(last)
                link(tt(out[:, :, NPR:TOK], samples[:, :, 0, :], over_tokens(col(w, 0, nch), NSMP), ALU.mult))
                link(tt(out[:, :, NPR:TOK], out[:, :, NPR:TOK], over_tokens(col(b, 0, nch), NSMP), ALU.add))
                for j in range(1, 4):
                    link(tt(tmp, samples[:, :, j, :], over_tokens(col(w, j * nch, nch), NSMP), ALU.mult))
                    last = tt(out[:, :, NPR:TOK], out[:, :, NPR:TOK], tmp, ALU.add)
                    if j < 3:
                        link(last)
                return last

            dve.wait_ge(inputs_in, 16 * 6)
            link(vec.memset(xp[:, :, 0:3], 0.0))
            dve.wait_ge(lam_exp, 1)
            minus_softplus(lam8[:], col("lru_lambda", 0, NC), lam8[:], scr(512, NC), scr(520, NC), scr(528, NC),
                           LRU_C)
            for l in range(2):
                dve.wait_ge(ada_done, (l + 1) * 6 * NC // SLOTS)
                tt(mod[l][:], ps[:, 6 + l, 0:6 * NC * NSEQ].rearrange("p (c s) -> p c s", s=NSEQ),
                   over_tokens(col(f"b_ada{l}", 0, 6 * NC), NSEQ), ALU.add).then_inc(mod_ready, 1)
                dve.wait_ge(mod_ready, l + 1)

            norm(0, "norm_mix0", 0, 0)
            for c in range(NC):
                dve.wait_ge(lin_done, c + 1)
                vec.tensor_copy(xp[:, c, 3:3 + NPR], ps[:, c % 4, 0:NPR])
                vec.tensor_copy(xs[:, c, 3, :], ps[:, c % 4, NPR:TOK]).then_inc(lin_x, 1)
            dve.wait_ge(lin_x, NC)
            convolve(xr, xp, xs, NC, "lru_conv_w", "lru_conv_b", stmp).then_inc(xr_ready, 1)
            dve.wait_ge(lgate_act, 2 * NC)
            tt(la, ra, over_tokens(lam8[:], TOK), ALU.mult).then_inc(loga_ready, 1)
            link(tt(ig, ig, xr, ALU.mult))
            dve.wait_ge(a_ready, 2)
            link(tt(bx, ra, ra, ALU.mult))
            stt(la, bx, 1.0, la, ALU.add, ALU.mult).then_inc(tt_ready, 1)
            dve.wait_ge(sqrt_ready, 1)
            link(tt(bx, la, ig, ALU.mult))
            link(tt(stmp, ra[:, :, NPR:TOK], h0, ALU.mult))
            for c in range(NC):
                vec.tensor_tensor_scan(xr[:, c, 0:NPR], ra[:, c, 0:NPR], bx[:, c, 0:NPR], 0.0, ALU.mult, ALU.add)
            tt(xr[:, :, NPR:TOK], bx[:, :, NPR:TOK], stmp, ALU.add).then_inc(hs_ready, 1)
            dve.wait_ge(hs_ready, 1)
            dve.wait_ge(lin_y, NC)
            tt(ybr, ybr, xr, ALU.mult).then_inc(ly_ready, 1)
            residual(0, 0, 2)

            def peer(l):
                norm(2 * l + 1, f"norm_ffn{l}", l, 3)
                for b, (t0, nb) in enumerate(BLOCKS):
                    Sb, V, I = S[0:nb, b], vals[0:nb], idx[0:nb]
                    cd, tp, ps_ = cand[0:nb], top[0:nb], pos[0:nb]

                    def top16(v, i, of, n):
                        for k in range(n):
                            last = vec.max(v[:, k, 0:8], of[:, k, :])
                        link(last)
                        for k in range(n):
                            last = vec.max_index(i[:, k, 0:8], v[:, k, 0:8], of[:, k, :])
                        link(last)
                        for k in range(n):
                            last = vec.match_replace(of[:, k, :], v[:, k, 0:8], of[:, k, :], LOWEST)
                        link(last)
                        for k in range(n):
                            last = vec.max(v[:, k, 8:16], of[:, k, :])
                        link(last)
                        for k in range(n):
                            last = vec.max_index(i[:, k, 8:16], v[:, k, 8:16], of[:, k, :])
                        link(last)

                    dve.wait_ge(sc_ready[l], 4 * (b + 1))
                    top16(V, I, Sb, 2 * PH)
                    vec.tensor_copy(flat(idxf[0:nb]), flat(I))
                    V4 = V.rearrange("p (a two) k -> p a two k", two=2)
                    I4 = idxf[0:nb].rearrange("p (a two) k -> p a two k", two=2)
                    full = [nb, PH, TOPK, TOPK]
                    link(tt(cd.rearrange("p a (i j) -> p a i j", j=TOPK),
                            V4[:, :, 0, :].unsqueeze(3).to_broadcast(full),
                            V4[:, :, 1, :].unsqueeze(2).to_broadcast(full), ALU.add))
                    top16(tp, ps_, cd, PH)
                    tt(wexp[0:nb], tp, tp[:, :, 0:1].to_broadcast([nb, PH, TOPK]), ALU.subtract)\
                        .then_inc(top_ready[l], 1)
                    vec.tensor_single_scalar(ab[0:nb, 0, :], flat(ps_), 4, ALU.logical_shift_right)
                    link(vec.tensor_single_scalar(ab[0:nb, 1, :], flat(ps_), TOPK - 1, ALU.bitwise_and))
                    link(vec.tensor_copy(flat(abf[0:nb]), flat(ab[0:nb])))
                    for i in range(2):
                        e = eq[0:nb]
                        link(tt(e, abf[0:nb, i, :].unsqueeze(2).to_broadcast([nb, PICKS, TOPK]),
                                iota[0:nb, 0:TOPK].unsqueeze(1).to_broadcast([nb, PICKS, TOPK]), ALU.is_equal))
                        e4 = e.rearrange("p (a k) j -> p a k j", a=PH)
                        link(tt(e4, e4, I4[:, :, i, :].unsqueeze(2).to_broadcast(full), ALU.mult))
                        link(vec.reduce_sum(picks[0:nb, b, i, :], e, axis=AX_X))
                    dve.wait_ge(topexp_ready[l], b + 1)
                    link(vec.reduce_sum(ssum[0:nb], wexp[0:nb], axis=AX_X))
                    link(vec.reciprocal(ssum[0:nb], ssum[0:nb]))
                    tt(picks[0:nb, b, 2, :].rearrange("p (a k) -> p a k", a=PH), wexp[0:nb],
                       ssum[0:nb].unsqueeze(2).to_broadcast([nb, PH, TOPK]), ALU.mult).then_inc(picks_ready[l], 1)
                for b, (t0, nb) in enumerate(BLOCKS):
                    dve.wait_ge(pickT_done[l], b + 1)
                    last = vec.tensor_copy(
                        pickT[:, :, t0:t0 + nb],
                        ps[:, 4 + b, 0:3 * P].rearrange("p (i t) -> p i t", i=3)[:, :, 0:nb])
                last.then_inc(pickT_ready[l], 1)
                dve.wait_ge(pickT_ready[l], 1)

                def build(g, s):
                    for i in range(4):
                        t = bass.ds(g * 4 + i, 1)
                        ts(oh_j[s][:, i, :], iota, pickT[:, 1, t], None, ALU.is_equal)
                        last = ts(oh_i[s][:, i, :], iota, pickT[:, 0, t], pickT[:, 2, t], ALU.is_equal, ALU.mult)
                    last.then_inc(onehot_ready[l], 1)

                def weigh(g, s):
                    Gt = G[:, :, bass.ds(g * 4, 4)].rearrange("p r t -> p t r")
                    tt(Gt, ps[:, s, :].rearrange("p (t r) -> p t r", t=4), Gt, ALU.mult).then_inc(routed[l], 1)
                build(0, 0)
                build(1, 1)
                dve.wait_ge(g_ready[l], KEYS)
                with dve.Fori(0, GROUPS // 2 - 1) as r:
                    for s in range(2):
                        dve.wait_ge(route_done[l], r * 2 + (s + 1))
                        weigh(r * 2 + s, s)
                        build(r * 2 + (s + 2), s)
                for s in range(2):
                    dve.wait_ge(route_done[l], GROUPS - 1 + s)
                    weigh(GROUPS - 2 + s, s)
                residual(2 * l + 1, l, 5)

            peer(0)

            norm(2, "norm_mix1", 1, 0)
            vec.memset(xm[:, :, 0:3], 0.0)
            for k in range(KM):
                dve.wait_ge(mx_done, k + 1)
                vec.tensor_copy(xm[:, k, 3:3 + NPR], ps[:, k % 4, 0:NPR])
                vec.tensor_copy(xms[:, k, 3, :], ps[:, k % 4, NPR:TOK]).then_inc(mx_copied, 1)
            dve.wait_ge(mx_copied, KM)
            dve.wait_ge(ml_inputs_in, 16 * 3)
            convolve(xc, xm, xms, KM, "ml_conv_w", "ml_conv_b", scr(512, KM, NSMP)).then_inc(conv_ready, 1)
            n = 0
            for to, factor, nblocks in ((kt, float(MHD) ** -0.5, 2), (vt, 1.0, 3)):
                for b in range(nblocks):
                    nb = BLOCKS[b][1]
                    for q in range(KM // 4):
                        dve.wait_ge(vk_done, n + 1)
                        o = to[:, b, q * BANK:(q + 1) * BANK] if b < 2 else vs[0:nb, q * BANK:(q + 1) * BANK]
                        ts(o, ps[0:nb, n % 4, :], factor, None, ALU.mult).then_inc(vk_copied, 1)
                        n += 1
            H_ = slice(0, HEADS)
            dve.wait_ge(gate_done, 1)
            ts(irow[H_], ps[H_, 4, 0:TOK], col("ml_b_ig")[H_], None, ALU.add)
            ts(frow[H_], ps[H_, 5, 0:TOK], col("ml_b_fg")[H_], None, ALU.add).then_inc(gate_raw, 1)
            dve.wait_ge(gate_exp, 2)
            link(vec.memset(zero[H_], 0.0))
            minus_softplus(t_c[H_], frow[H_], exp_f[H_], t_a[H_], t_b[H_], Frow[H_], 1.0)
            link(vec.tensor_tensor_scan(Frow[H_, 0:NPR], t_c[H_, 0:NPR], zero[H_, 0:NPR], 0.0, ALU.add, ALU.add))
            link(tt(Grow[H_, 0:NPR], irow[H_, 0:NPR], Frow[H_, 0:NPR], ALU.subtract))
            link(vec.tensor_tensor_scan(frow[H_, 0:NPR], Grow[H_, 0:NPR], Grow[H_, 0:NPR], 0.0, ALU.max, ALU.max))
            tt(mrow[H_, 0:NPR], Frow[H_, 0:NPR], frow[H_, 0:NPR], ALU.add)
            fs, is_, ms = t_c[H_, NPR:TOK], irow[H_, NPR:TOK], mrow[H_, NPR:TOK]
            link(tt(fs, fs, col("ml_m0", 0, NSMP)[H_], ALU.add))
            link(tt(ms, fs, is_, ALU.max))
            tt(srow[H_, 0, :], fs, ms, ALU.subtract)
            tt(srow[H_, 1, :], is_, ms, ALU.subtract)
            ts(srow[H_, 2, :], ms, -1.0, None, ALU.mult).then_inc(rows_ready, 1)
            dve.wait_ge(bcast_done, 1)
            for hd in range(HEADS):
                M = ps[:, 4 + hd // 2, hd % 2 * NPR:(hd % 2 + 1) * NPR]
                stt(Wt[:, hd, 0:NPR], M, -1.0, causal, ALU.mult, ALU.add)
                stt(Wt[:, hd, NPR:NPR + P], M[:, P:NPR], -1.0, causal[:, 0:P], ALU.mult, ALU.add)
            dve.wait_ge(gcol_done, 1)
            vec.tensor_copy(gcol, ps[:, 6, 0:2 * HEADS]).then_inc(wexp_in, 1)
            dve.wait_ge(sbc_done, 1)
            link(vec.tensor_copy(bc.rearrange("p a b c -> p (a b c)"), ps[:, 7, 0:HEADS * 3 * NSMP]))

            def per_head(v):
                return v.rearrange("p (a c) b -> p a c b", a=HEADS)

            def factor_of(i):
                return bc[:, :, i, :].unsqueeze(2).to_broadcast([P, HEADS, HC, NSMP])
            link(tt(per_head(nst), per_head(nst), factor_of(0), ALU.mult))
            link(tt(per_head(kw), per_head(kT[:, :, NPR:TOK]), factor_of(1), ALU.mult))
            link(tt(nst, nst, kw, ALU.add))
            tt(qn, qT[:, :, NPR:TOK], nst, ALU.mult).then_inc(sqn_ready, 1)
            dve.wait_ge(w_ready, 1)
            dve.wait_ge(st_done, 1)
            for hd in range(HEADS):
                last = tt(Sw[:, hd, :], ps[:, hd, 0:384], Wt[:, hd, :], ALU.mult)
            last.then_inc(sw_ready, 1)
            for hd in range(HEADS):
                for b in range(2):
                    e0 = NPR - 1 if b == 0 else NPR + P - 1
                    kh = kt[:, b, hd * MHD:(hd + 1) * MHD]
                    last = ts(kh, kh, Wt[:, hd, e0:e0 + 1], None, ALU.mult)
            last.then_inc(kw_ready, 1)
            dve.wait_ge(den_done, 1)
            dve.wait_ge(em_ready, 1)
            for i in range(2):
                e = flat(em[:, 2 * i:2 * i + 2, :])
                link(stt(e, ps[:, 4 + i, :], -1.0, e, ALU.mult, ALU.max))
                link(tt(e, ps[:, 4 + i, :], e, ALU.max))
            link(vec.reciprocal(flat(em), flat(em)))
            for hd in range(HEADS):
                dve.wait_ge(num_done, hd + 1)
                tt(hT[:, hd * HC:(hd + 1) * HC, 0:NPR],
                   ps[:, hd % 2 * 2:hd % 2 * 2 + 2, :].rearrange("p a (b t) -> p (a b) t", b=2),
                   em[:, hd:hd + 1, :].to_broadcast([P, HC, NPR]), ALU.mult).then_inc(num_read, 1)
            dve.wait_ge(sden_done, 1)
            sd = ps[:, 7, P:P + HEADS * NSMP].rearrange("p (a b) -> p a b", a=HEADS)
            link(stt(sden, sd, -1.0, bc[:, :, 2, :], ALU.mult, ALU.max))
            link(tt(sden, sd, sden, ALU.max))
            link(vec.reciprocal(sden, sden))
            dve.wait_ge(num_read, HEADS)
            for n in range(KM):
                dve.wait_ge(cp_done, n + 1)
                if n >= 8:
                    dve.wait_ge(cp_stored[n % 8], 16 * (n // 8))
                vec.tensor_copy(Cst[:, n % 8, :], ps[:, n % 4, :]).then_inc(cp_copied, 1)
            vec.tensor_copy(npr, ps[:, 6, 16:16 + KM]).then_inc(npr_ready, 1)
            for m in range(NSMP * HEADS):
                b, hd = m // HEADS, m % HEADS
                dve.wait_ge(C_in[m % 4], 16 * (m // 4 + 1))
                dve.wait_ge(vb_used, m + 1)
                Cm = flat(Cbuf[:, m % 4, :, :])
                stt(Cm, Cm, bc[:, hd, 0, b:b + 1], flat(vk[m % 2]), ALU.mult, ALU.add).then_inc(C_new, 1)
            dve.wait_ge(C_read, NSMP * HEADS)
            tt(per_head(hT[:, :, NPR:TOK]),
               ps[:, 2, 0:KM * NSMP].rearrange("p (a c b) -> p a c b", a=HEADS, c=HC),
               sden.unsqueeze(2).to_broadcast([P, HEADS, HC, NSMP]), ALU.mult).then_inc(hT_ready, 1)
            dve.wait_ge(mu_done, 1)
            dve.wait_ge(hT_ready, 1)
            for hd in range(HEADS):
                part = hT[:, hd * HC:(hd + 1) * HC, :]
                last = stt(part, ps[:, 4 + hd, 0:TOK].unsqueeze(1).to_broadcast([P, HC, TOK]), -1.0 / MHD, part,
                           ALU.mult, ALU.add)
            last.then_inc(hc_ready, 1)
            dve.wait_ge(var_done, 1)
            ts(hstd, ps[:, 4:8, 0:TOK], 1.0 / MHD, EPS, ALU.mult, ALU.add).then_inc(hvar_ready, 1)
            dve.wait_ge(hstd_ready, 1)
            link(vec.reciprocal(hstd, hstd))
            link(tt(per_head(hT), per_head(hT), hstd.unsqueeze(2).to_broadcast([P, HEADS, HC, TOK]), ALU.mult))
            for c in range(KM):
                last = ts(hT[:, c, :], hT[:, c, :], col("ml_ln_g", c), None, ALU.mult)
            link(last)
            for c in range(KM):
                last = stt(hT[:, c, :], xc[:, c, :], col("ml_skip", c), hT[:, c, :], ALU.mult, ALU.add)
            link(last)
            dve.wait_ge(z_ready, KM)
            tt(hT, hT, z, ALU.mult).then_inc(mly_ready, 1)
            residual(2, 1, 2)
            peer(1)

            dve.wait_ge(ssq_done, 5)
            ts(rstd, ps[:, 0, 0:TOK], 1.0 / D, EPS, ALU.mult, ALU.add).then_inc(ms_ready, 1)
            dve.wait_ge(rms_ready, 5)
            link(vec.reciprocal(rstd, rstd))
            link(tt(h[:], x[:], rstd.unsqueeze(1).to_broadcast([P, NC, TOK]), ALU.mult))
            for c in range(NC):
                last = ts(h[:, c, :], h[:, c, :], col("norm_f", c), None, ALU.mult)
            last.then_inc(y_ready, 1)


def kernel(**inputs):
    import numpy as np
    import concourse.bacc as bacc
    from concourse.bass_utils import run_bass_kernel_spmd as run

    a = {k: np.asarray(v) for k, v in inputs.items()}
    xpr, xsm = a["x_prompt"], a["x_sample"]
    T, D = xpr.shape[1:]
    B = xsm.shape[0]
    DR, MI = a["lru_w_out"].shape[1], a["ml_w_out"].shape[1]
    NC, KM = D // P, MI // P
    H = a["state_mlstm_m"].shape[2]
    f32 = np.float32

    def channels(v):
        return np.ascontiguousarray(v.reshape(v.shape[0], -1, P).transpose(2, 1, 0))

    def tiles(w):
        k, n = w.shape
        return w.reshape(k // TILE, NC, P, n // P, P).transpose(3, 0, 2, 1, 4).reshape(-1, P, TILE)

    def diagonal(w):
        n, b, _ = w.shape
        per = P // b
        out = np.zeros((n // per, P, P), f32)
        for i in range(per):
            out[:, i * b:(i + 1) * b, i * b:(i + 1) * b] = w[i::per]
        return out.reshape(-1, TILE // P, P, P).transpose(0, 2, 1, 3).reshape(-1, P, TILE)

    first, n_tiles = tile_plan(D, DR, MI, 2, P)
    stream = np.empty((n_tiles // 2, P, 2, TILE), f32)

    def put(name, t):
        n = first[name] // 2
        stream[n:n + len(t) // 2] = t.reshape(-1, 2, P, TILE).transpose(0, 2, 1, 3)

    for l in range(2):
        put(f"ada{l}", tiles(a["w_ada"][l]))
        put(f"wq{l}", tiles(a["peer_w_q"][l]))
        keys = a["peer_keys"][l].reshape(-1, P, P).transpose(0, 2, 1)
        put(f"keys{l}", keys.reshape(2, 8, P, P).transpose(0, 2, 1, 3).reshape(2, P, TILE))
        put(f"u{l}", a["peer_u"][l].reshape(P, P, NC, P).transpose(0, 3, 2, 1).reshape(P, P, TILE))
        put(f"v{l}", a["peer_v"][l].reshape(P, P, TILE))
    w_in = a["lru_w_in"][0]
    put("lru_in", np.concatenate([tiles(w_in[:, DR:]), tiles(w_in[:, :DR])]))
    put("lru_gates", np.concatenate([diagonal(a["lru_w_a"][0]), diagonal(a["lru_w_i"][0])]))
    put("lru_out", tiles(a["lru_w_out"][0]))
    w_in = a["ml_w_in"][0]
    put("ml_x", tiles(w_in[:, :MI]))
    put("ml_z", tiles(w_in[:, MI:]))
    put("ml_qkv", np.concatenate([diagonal(a[f"ml_w_{c}"][0]) for c in "qkv"]))
    put("ml_out", tiles(a["ml_w_out"][0]))

    where, n_cols = column_layout(D, DR, MI)
    cols = np.zeros((P, n_cols), f32)

    def put_cols(name, v):
        v = v.reshape(-1, P).T
        cols[:, where[name][0]:where[name][0] + v.shape[1]] = v

    for l in range(2):
        for name in ("norm_mix", "norm_ffn", "b_ada"):
            put_cols(f"{name}{l}", a[name][l])
    put_cols("norm_f", a["norm_f"])
    for name in ("lru_conv_w", "lru_conv_b", "lru_b_a", "lru_b_i", "lru_lambda", "ml_conv_w", "ml_conv_b",
                 "ml_skip", "ml_ln_g"):
        put_cols(name, a[name][0])
    for name in ("ml_b_ig", "ml_b_fg"):
        cols[:H, where[name][0]] = a[name][0]
    cols[:H, where["ml_m0"][0]:where["ml_m0"][0] + B] = a["state_mlstm_m"][0].T

    consts = np.zeros((P, 5 * P), f32)
    consts[:, :P] = np.eye(P)
    consts[:, P:2 * P] = np.arange(P)
    consts[:, 2 * P:3 * P] = 1.0
    consts[:, 3 * P:4 * P] = np.where(np.arange(P)[:, None] > np.arange(P)[None], MASKED, 0.0)

    gates = np.concatenate([a["ml_w_ig"][0], a["ml_w_fg"][0]], axis=1)
    arrays = {
        "stream": stream.reshape(n_tiles // 2, P, 2 * TILE),
        "cols": cols,
        "consts": consts,
        "c": channels(np.concatenate([a["c_prompt"], a["c_sample"]])),
        "x": channels(np.concatenate([xpr[0], xsm[:, 0]])),
        "lru_h": channels(a["state_lru_h"][0]),
        "lru_conv": np.ascontiguousarray(a["state_lru_conv"][0].reshape(B, 3, NC, P).transpose(3, 2, 1, 0)),
        "ml_conv": np.ascontiguousarray(a["state_mlstm_conv"][0].reshape(B, 3, KM, P).transpose(3, 2, 1, 0)),
        "ml_n": channels(a["state_mlstm_n"][0].reshape(B, MI)),
        "gates": np.ascontiguousarray(gates.reshape(3 * KM, P, 2 * H).transpose(1, 0, 2)),
        "C": np.ascontiguousarray(a["state_mlstm_C"][0].reshape(B * H, MI // H // P, P, MI // H)
                                  .transpose(0, 2, 1, 3)).reshape(B * H, P, -1),
    }
    outs = {
        "y": (P, NC, T + B), "lru_h_o": (P, NC, B + 1), "lru_conv_p": (P, NC, 3), "lru_conv_s": (P, NC, 3, B),
        "ml_conv_p": (P, KM, 3), "ml_conv_s": (P, KM, 3, B), "n_p": (P, KM), "n_s": (P, KM, B), "m": (H, B + 1),
        "C_p": (KM, P, MI // H), "C_s": (B * H, P, MI),
    }
    nc = bacc.Bacc("TRN2", target_bir_lowering=False, num_devices=1)
    args = [nc.dram_tensor(f"in_{k}", v.shape, F32, kind="ExternalInput").ap() for k, v in arrays.items()]
    args += [nc.dram_tensor(f"out_{k}", s, F32, kind="ExternalOutput").ap() for k, s in outs.items()]
    decoder_step(nc, *args)
    r = run(nc, [{f"in_{k}": v for k, v in arrays.items()}], core_ids=[0]).results[0]
    r = {k: r[f"out_{k}"] for k in outs}

    def rows(v):
        return np.ascontiguousarray(v.transpose(2, 1, 0)).reshape(v.shape[2], -1)

    def conv(v):
        return np.ascontiguousarray(v.transpose(3, 2, 1, 0)).reshape(v.shape[3], 3, -1)

    y = rows(r["y"])
    hs = rows(r["lru_h_o"])
    mh = MI // H
    C_s = r["C_s"].reshape(B, H, P, mh // P, mh).transpose(0, 1, 3, 2, 4).reshape(B, H, mh, mh)
    return (y[None, :T], y[T:, None],
            hs[None, :1], conv(r["lru_conv_p"][..., None])[None],
            r["C_p"].reshape(1, 1, H, mh, mh), rows(r["n_p"][..., None]).reshape(1, 1, H, mh),
            np.ascontiguousarray(r["m"][:, :1].T)[None], conv(r["ml_conv_p"][..., None])[None],
            hs[None, 1:], conv(r["lru_conv_s"])[None],
            np.ascontiguousarray(C_s)[None], rows(r["n_s"]).reshape(1, B, H, mh),
            np.ascontiguousarray(r["m"][:, 1:].T)[None], conv(r["ml_conv_s"])[None])
```

```python
from contextlib import ExitStack

import concourse.bass as bass
from concourse import mybir

ALU = mybir.AluOpType
ACT = mybir.ActivationFunctionType
F32 = mybir.dt.float32
F32R = mybir.dt.float32r
U32 = mybir.dt.uint32
AX_X = mybir.AxisListType.X

P = 128
TILE = 1024
SLOTS = 8
HALVES = 4
PAIRS = SLOTS // 2
BANK = 512
LRU_C = 8.0
EPS = 1e-6
MASKED = -1e30
LOWEST = -3e38
N_LOG1P = 9


def column_layout(D, D_RNN, M_INNER):
    at, out = 0, {}
    kd, kr, km = D // P, D_RNN // P, M_INNER // P
    for name, n in [("norm_mix0", kd), ("norm_mix1", kd), ("norm_ffn0", kd), ("norm_ffn1", kd), ("norm_f", kd),
                    ("b_ada0", 6 * kd), ("b_ada1", 6 * kd), ("lru_conv_w", 4 * kr), ("lru_conv_b", kr),
                    ("lru_b_a", kr), ("lru_b_i", kr), ("lru_lambda", kr), ("ml_conv_w", 4 * km),
                    ("ml_conv_b", km), ("ml_skip", km), ("ml_ln_g", km), ("ml_b_ig", 1), ("ml_b_fg", 1),
                    ("ml_m0", 8)]:
        out[name] = (at, n)
        at += n
    return out, at


def tile_plan(D, D_RNN, M_INNER, DEPTH, N_KEYS):
    kd, kr, km = D // P, D_RNN // P, M_INNER // P
    at, first = 0, {}
    for name, n in [("ada0", 2 * kd), ("lru_in", 2 * kr + 4 * kd), ("lru_gates", 2), ("lru_out", kd),
                    ("wq0", 16), ("keys0", 2), ("u0_ada1", 2 * 6 * kd), ("u0", N_KEYS - 6 * kd), ("v0", N_KEYS),
                    ("ml_x", km), ("ml_qkv", 6), ("ml_z", km), ("ml_out", 2 * kd),
                    ("wq1", 16), ("keys1", 2), ("u1", N_KEYS), ("v1", N_KEYS)]:
        first[name] = at
        at += n
    return first, at


def half_plan(D, D_RNN, M_INNER, N_KEYS):
    kd, kr, km = D // P, D_RNN // P, M_INNER // P
    at, first = 0, {}
    for name, n in [("lru_in", 2 * kr), ("wq0", 16), ("u0", N_KEYS), ("v0", N_KEYS), ("ml_x", km), ("ml_z", km),
                    ("wq1", 16), ("u1", N_KEYS), ("v1", N_KEYS)]:
        first[name] = at
        at += 2 * n
        assert at % 16 == 0
    return first


def decoder_step(nc, stream, cols_d, consts_d, c_d, x_d, lru_h_d, lru_conv_d, ml_conv_d, ml_n_d, gates_d, C_d,
                 y_o, lru_h_o, lru_conv_p_o, lru_conv_s_o, ml_conv_p_o, ml_conv_s_o, n_p_o, n_s_o, m_o,
                 C_p_o, C_s_o):
    NC, TOK = x_d.shape[1], x_d.shape[2]
    NSMP = lru_conv_d.shape[3]
    NPR = TOK - NSMP
    KM = ml_conv_d.shape[1]
    D, M_INNER = NC * P, KM * P
    HEADS = 4
    HC = KM // HEADS
    MHD = M_INNER // HEADS
    NSEQ = NSMP + 1
    KEYS = P
    PH, TOPK = 8, 16
    PICKS = PH * TOPK
    COL, NCOLS = column_layout(D, D, M_INNER)
    FIRST, NTILES = tile_plan(D, D, M_INNER, 2, KEYS)
    HALF = half_plan(D, D, M_INNER, KEYS)
    BLOCKS = [(0, 128), (128, 128), (256, NSMP)]
    NB = len(BLOCKS)
    assert D == TILE and NPR == 256 and NSMP == 8 and KM == 16

    with ExitStack() as ctx:
        def sb(name, shape, dt=F32):
            return ctx.enter_context(nc.sbuf_tensor(name, shape, dt))

        def sem(name):
            return ctx.enter_context(nc.semaphore(name))

        ring = sb("ring", [P, SLOTS, TILE])
        x = sb("x", [P, NC, TOK])
        h_hi, h_lo = sb("h_hi", [P, NC, TOK], F32R), sb("h_lo", [P, NC, TOK], F32R)
        mod = [sb(f"mod{l}", [P, 6 * NC, NSEQ]) for l in range(2)]
        cols = sb("cols", [P, NCOLS])
        consts = sb("consts", [P, 3 * P + P])
        ident, iota, ones = (consts[:, i * P:(i + 1) * P] for i in range(3))
        causal = consts[:, 3 * P:4 * P]
        c_sb = sb("c_sb", [P, NC, NSEQ])
        lam8 = sb("lam8", [P, NC])
        BIG = sb("BIG", [P, KEYS * TOK])
        with nc.sbuf_tensor("SCR", [P, 6144], F32) as SCR:
            pass
        g_parts = sb("g_parts", [P, 2, 2, TOK], F32R)
        sb("between", [P, 2048 - 4 * TOK])
        w_parts = sb("w_parts", [P, 2, HALVES, BANK], F32R)
        w_hi, w_lo = w_parts[:, 0], w_parts[:, 1]
        g_hi, g_lo = g_parts[:, 0], g_parts[:, 1]
        ps = ctx.enter_context(nc.psum_tensor("ps", [P, 8, BANK], F32))

        def big(at, *shape):
            n = 1
            for s in shape:
                n *= s
            assert at + n <= KEYS * TOK
            v = BIG[:, at:at + n]
            names = "abcd"[:len(shape)]
            if len(shape) == 1:
                return v
            return v.rearrange(f"p ({' '.join(names)}) -> p {' '.join(names)}", **dict(zip(names[1:], shape[1:])))

        def scr(at, *shape):
            n = 1
            for s in shape:
                n *= s
            assert at + n <= 6144
            v = SCR[:, at:at + n]
            names = "abcd"[:len(shape)]
            if len(shape) == 1:
                return v
            return v.rearrange(f"p ({' '.join(names)}) -> p {' '.join(names)}", **dict(zip(names[1:], shape[1:])))

        def col(name, i=0, n=1):
            return cols[:, COL[name][0] + i:COL[name][0] + i + n]

        NT = NC * TOK
        rstd = scr(0, TOK)
        h = scr(2048, NC, TOK)
        scale = scr(2048 + NC * TOK, NC, NSEQ)
        xp = big(0, NC, 3 + NPR)
        xs = big(NC * (3 + NPR), NC, 4, NSMP)
        LB = NC * (3 + NPR) + NC * 4 * NSMP
        ybr, xr, ra, ig, la, bx = (big(LB + i * NT, NC, TOK) for i in range(6))
        sq = ra
        h0 = big(LB + 6 * NT, NC, NSMP)
        stmp = big(LB + 6 * NT + NC * NSMP, NC, NSMP)
        MT = KM * TOK
        xm = big(0, KM, 3 + NPR)
        xms = big(KM * (3 + NPR), KM, 4, NSMP)
        MB = KM * (3 + NPR) + KM * 4 * NSMP
        xc, qT, kT, vT = (big(MB + i * MT, KM, TOK) for i in range(4))
        hT = vT
        z = big(0, KM, TOK)
        VB = MB + 4 * MT
        vt, kt = (big(VB + i * 2 * M_INNER, 2, M_INNER) for i in range(2))
        KT2 = MB + 2 * MT + HC * MHD
        Cbuf = [big(MB + 2 * MT, HC, MHD)] + [big(VB + i * HC * MHD, HC, MHD) for i in range(4)]
        CBUFS = len(Cbuf)
        Cst = big(0, 8, MHD)
        RB = VB + 4 * M_INNER
        vs = Cq = big(RB, M_INNER)
        GB = RB + M_INNER
        gates = big(GB, 3 * KM, 2 * HEADS)
        irow = big(GB + 384, TOK)
        frow = big(GB + 384 + TOK, TOK)
        Grow = big(GB + 384 + 2 * TOK, TOK)
        mrow = big(GB + 384 + 3 * TOK, TOK)
        nst = big(GB + 384 + 4 * TOK, KM, NSMP)
        SB0 = GB + 384 + 4 * TOK + KM * NSMP
        kw = big(SB0, KM, NSMP)
        bc = big(SB0 + 128, HEADS, 3, NSMP)
        gcol = big(SB0 + 224, 8)
        srow = big(SB0 + 232, 3, NSMP)
        sden = big(SB0 + 256, HEADS, NSMP)
        npr = big(SB0 + 288, KM)
        qn = big(GB, KM, NSMP)
        qz = big(GB + 384, KM, NSMP * NSMP)
        em = big(0, HEADS, NPR)
        Wt = scr(0, HEADS, 384)
        Sw = scr(1536, HEADS, 384)
        vk = [scr(i * 1024, HC // 2, MHD) for i in range(2)]
        hsq = scr(2048, KM, NPR)
        hstd = big(KT2, HEADS, NPR)
        hsq_s = big(KT2 + HEADS * NPR, KM, NSMP)
        mu_s = big(KT2 + HEADS * NPR + KM * NSMP, HEADS, NSMP)
        std_s = big(KT2 + HEADS * NPR + KM * NSMP + HEADS * NSMP, HEADS, NSMP)
        exp_f, zero, Frow, t_a, t_b, t_c = (scr(i * TOK, TOK) for i in range(6))
        G = big(0, KEYS, TOK)
        TB = KEYS * TOK - 16 * TOK - NB * 2048 - 5768
        pq = big(TB, 16, TOK)
        S = big(TB + 16 * TOK, NB, 16, KEYS)
        TC = TB + 16 * TOK + NB * 2048
        cand = big(TC, PH, TOPK * TOPK)
        eq = big(TC + 2048, PICKS, TOPK)
        vals = big(TC + 4096, 16, TOPK)
        idxf = big(TC + 4352, 16, TOPK)
        top = big(TC + 4608, PH, TOPK)
        abf = big(TC + 4736, 2, PICKS)
        idx = big(TC + 4992, 16, TOPK).bitcast(U32)
        pos = big(TC + 5248, PH, TOPK).bitcast(U32)
        ab = big(TC + 5376, 2, PICKS).bitcast(U32)
        ssum = scr(1944, NB, PH)
        EXP_ROWS, FREE_ROW = (40, 72, (TB + 16 * TOK + 2 * 2048) // TOK // 8 * 8), TC // TOK // 8 * 8
        picks = scr(0, NB, 3, PICKS)
        pickT = scr(1152, 3, TOK)
        OH = 4
        oh_j = [scr(2048 + i * 1024, 4, KEYS) for i in range(OH)]
        oh_i = [scr(2048 + i * 1024 + 512, 4, KEYS) for i in range(OH)]

        pair_in = [sem(f"pair_in{i}") for i in range(PAIRS)]
        pairs_used = sem("pairs_used")
        inputs_in = sem("inputs_in")
        ml_inputs_in = sem("ml_inputs_in")
        dve_seq = sem("dve_seq")
        ada_done = sem("ada_done")
        mod_ready = sem("mod_ready")
        squares_done = sem("squares_done")
        ssq_done = sem("ssq_done")
        ms_ready = sem("ms_ready")
        rms_ready = sem("rms_ready")
        h_ready = sem("h_ready")
        out_done = sem("out_done")
        x_ready = sem("x_ready")
        lin_x = sem("lin_x")
        lin_y = sem("lin_y")
        lam_exp = sem("lam_exp")
        xr_ready = sem("xr_ready")
        lgate_done = sem("lgate_done")
        lgate_act = sem("lgate_act")
        loga_ready = sem("loga_ready")
        a_ready = sem("a_ready")
        tt_ready = sem("tt_ready")
        sqrt_ready = sem("sqrt_ready")
        hs_ready = sem("hs_ready")
        ly_ready = sem("ly_ready")
        stores = sem("stores")
        mx_copied = sem("mx_copied")
        conv_ready = sem("conv_ready")
        xc_ready = sem("xc_ready")
        qkv_done = sem("qkv_done")
        qkv_act = sem("qkv_act")
        vk_done = sem("vk_done")
        vk_copied = sem("vk_copied")
        gate_done = sem("gate_done")
        gate_raw = sem("gate_raw")
        gate_exp = sem("gate_exp")
        rows_ready = sem("rows_ready")
        bcast_done = sem("bcast_done")
        srow_exp = sem("srow_exp")
        gcol_done = sem("gcol_done")
        st_done = sem("st_done")
        wexp_in = sem("wexp_in")
        w_ready = sem("w_ready")
        em_ready = sem("em_ready")
        sw_ready = sem("sw_ready")
        den_done = sem("den_done")
        num_done = sem("num_done")
        num_read = sem("num_read")
        kw_ready = sem("kw_ready")
        cp_done = sem("cp_done")
        cp_copied = sem("cp_copied")
        cp_stored = [sem(f"cp_stored{i}") for i in range(8)]
        sbc_done = sem("sbc_done")
        sqn_ready = sem("sqn_ready")
        sden_done = sem("sden_done")
        C_in = [sem(f"C_in{i}") for i in range(CBUFS)]
        C_out = [sem(f"C_out{i}") for i in range(CBUFS)]
        vb_done = sem("vb_done")
        vb_used = sem("vb_used")
        C_new = sem("C_new")
        C_read = sem("C_read")
        qz_ready = sem("qz_ready")
        skip_ready = sem("skip_ready")
        Cq_copied = sem("Cq_copied")
        Cq_turned = sem("Cq_turned")
        hT_ready = sem("hT_ready")
        mu_done = sem("mu_done")
        hc_ready = sem("hc_ready")
        hsq_ready = sem("hsq_ready")
        var_done = sem("var_done")
        hvar_ready = sem("hvar_ready")
        hstd_ready = sem("hstd_ready")
        z_ready = sem("z_ready")
        mly_ready = sem("mly_ready")
        pq_ready = [sem(f"pq_ready{l}") for l in range(2)]
        sc_done = [sem(f"sc_done{l}") for l in range(2)]
        sc_ready = [sem(f"sc_ready{l}") for l in range(2)]
        g_ready = [sem(f"g_ready{l}") for l in range(2)]
        top_ready = [sem(f"top_ready{l}") for l in range(2)]
        topexp_ready = [sem(f"topexp_ready{l}") for l in range(2)]
        picks_ready = [sem(f"picks_ready{l}") for l in range(2)]
        pickT_done = [sem(f"pickT_done{l}") for l in range(2)]
        pickT_ready = [sem(f"pickT_ready{l}") for l in range(2)]
        oh_i_ready = [sem(f"oh_i_ready{l}") for l in range(2)]
        oh_j_abs = [sem(f"oh_j_abs{l}") for l in range(2)]
        oh_j_ready = [sem(f"oh_j_ready{l}") for l in range(2)]
        route_done = [sem(f"route_done{l}") for l in range(2)]
        routed = [sem(f"routed{l}") for l in range(2)]
        y_ready = sem("y_ready")
        hi_ready = sem("hi_ready")
        lo_ready = sem("lo_ready")
        half_used = sem("half_used")
        g_hi_ready = [sem(f"g_hi_ready{l}") for l in range(2)]
        g_lo_ready = [sem(f"g_lo_ready{l}") for l in range(2)]
        h_made = sem("h_made")
        h_hi_ready = sem("h_hi_ready")
        work_free = [sem(f"work_free{l}") for l in range(2)]
        def u_tile_at(l, row, r=0):
            if l == 0 and row < 6 * NC:
                return FIRST["u0_ada1"] + 2 * row, 2 * r
            return FIRST[f"u{l}"] + row - (6 * NC if l == 0 else 0), r
        def half_of(n, half):
            return ring[:, n % SLOTS, half * BANK:(half + 1) * BANK]
        def C_uses(i):
            return len(range(i, NSMP * HEADS, CBUFS))
        AT_MU, AT_CENTRE, AT_SQUARE, AT_VAR, AT_MS, AT_SQRT, AT_SCALE, AT_SKIP, AT_Z = 17, 18, 19, 21, 22, 23, 24, 26, 28
        lam_abs = sem("lam_abs")
        ml_conv_stored = sem("ml_conv_stored")
        npr_ready = sem("npr_ready")

        block = ctx.enter_context(nc.Block())
        GROUPS = TOK // 4
        N_STORES = 10

        @block.sync
        def _(sp):
            def pair(n, slot):
                sp.dma_start(ring[:, 2 * slot:2 * slot + 2, :].rearrange("p a b -> p (a b)"),
                             stream[n]).then_inc(pair_in[slot], 16)

            for n in range(PAIRS):
                pair(n, n)
            rounds = NTILES // 2 // PAIRS
            with sp.Fori(1, rounds) as r:
                for s in range(PAIRS):
                    sp.wait_ge(pairs_used, r * PAIRS + (s - PAIRS + 1))
                    pair(r * PAIRS + s, s)
            for n in range(rounds * PAIRS, NTILES // 2):
                sp.wait_ge(pairs_used, n - PAIRS + 1)
                pair(n, n % PAIRS)

        @block.tensor
        def _(pe):
            def need(n0, k, r=0):
                pe.wait_ge(pair_in[(n0 + k) // 2 % PAIRS], (r + (n0 + k) // SLOTS + 1) * 16)

            def w_at(n0, k, c):
                return ring[:, (n0 + k) % SLOTS, c * P:(c + 1) * P]

            def begins(ins, n0, k):
                if (n0 + k) % 2 == 0:
                    ins.then_inc(pairs_used, 1)

            def mm(out, lhsT, rhs, start=True, stop=True, shared=False):
                return nc.tensor.matmul(out, lhsT, rhs, start=start, stop=stop, skip_group_check=shared)

            def chunk(out, n0, k, src, first=False):
                for c in range(NC):
                    last = mm(out, w_at(n0, k, c), src(c), c == 0, c == NC - 1)
                    if c == 0 and not first:
                        begins(last, n0, k)
                return last

            def split_chunk(out, n, k, stage, r=0, start=True, stop=True, v_row=None):
                for half in range(2):
                    j = HALF[stage] + 2 * k + half
                    pe.wait_ge(lo_ready, r * (2 * SLOTS) + (j + 1))
                    for i in range(4):
                        c = 4 * half + i
                        w = (w_hi[:, j % HALVES, i * P:(i + 1) * P], w_lo[:, j % HALVES, i * P:(i + 1) * P])
                        if v_row is None:
                            x_hi, x_lo = h_hi[:, c, :], h_lo[:, c, :]
                            first, end = start and c == 0, stop and c == NC - 1
                        else:
                            x_hi, x_lo = g_hi[:, v_row % 2, :], g_lo[:, v_row % 2, :]
                            out, first, end = ps[:, c, 0:TOK], start, stop
                        last = mm(out, w[0], x_hi, first, False)
                        if c == 0:
                            begins(last, n, 0)
                        mm(out, w[0], x_lo, False, False)
                        last = mm(out, w[1], x_hi, False, end)
                    last.then_inc(half_used, 1)

            def norm_sum(n):
                pe.wait_ge(squares_done, n + 1)
                for c in range(NC):
                    last = mm(ps[:, 0, 0:TOK], ones, sq[:, c, :], c == 0, c == NC - 1)
                last.then_inc(ssq_done, 1)

            def residual_out(name, rhs, KC):
                per = KC // NC
                for m in range(NC):
                    for t in range(per):
                        k = m * per + t
                        need(FIRST[name], k)
                        for c in range(NC):
                            last = mm(ps[:, m, 0:TOK], w_at(FIRST[name], k, c), rhs[:, t * NC + c, :],
                                      t == 0 and c == 0, t == per - 1 and c == NC - 1)
                            if c == 0:
                                begins(last, FIRST[name], k)
                last.then_inc(out_done, 1)

            def c_in(c):
                return c_sb[:, c, :]

            pe.wait_ge(inputs_in, 16 * 6)
            for k in range(2 * NC):
                need(0, k)
                last = chunk(ps[:, 6, k * NSEQ:(k + 1) * NSEQ], 0, k, c_in, first=k == 0)
            last.then_inc(ada_done, 1)

            norm_sum(0)
            pe.wait_ge(h_ready, 1)
            n0 = FIRST["lru_in"]
            for k in range(2 * NC):
                if k >= 4:
                    if k - 4 < NC:
                        pe.wait_ge(lin_x, k - 3)
                    else:
                        pe.wait_ge(lin_y, k - 3 - NC)
                split_chunk(ps[:, k % 4, 0:TOK], n0 + 3 * k, k, "lru_in")
                for i in range(2):
                    need(n0, 3 * k + 1 + i)
                    at = (2 * NC + 2 * k + i) * NSEQ
                    last = chunk(ps[:, 6, at:at + NSEQ], n0, 3 * k + 1 + i, c_in)
            last.then_inc(ada_done, 1)
            n0 = FIRST["lru_gates"]
            need(n0, 0)
            pe.wait_ge(xr_ready, NC)
            pe.wait_ge(lin_y, NC)
            for g in range(2):
                for c in range(NC):
                    n = g * NC + c
                    if n >= 6:
                        pe.wait_ge(lgate_act, n - 5)
                    if n == 0:
                        begins(mm(ps[:, 0, NPR:TOK], w_at(n0, 0, 0), xr[:, 0, NPR:TOK]), n0, 0)
                        last = mm(ps[:, 0, 0:NPR], w_at(n0, 0, 0), xr[:, 0, 0:NPR])
                    else:
                        last = mm(ps[:, n % 6, 0:TOK], w_at(n0, g, c), xr[:, c, :])
                    last.then_inc(lgate_done, 1)
            pe.wait_ge(ly_ready, 1)
            pe.wait_ge(mod_ready, 2)
            residual_out("lru_out", ybr, NC)

            def peer(l):
                pe.wait_ge(x_ready, 2 * l + 1)
                norm_sum(2 * l + 1)
                pe.wait_ge(h_ready, 2 * l + 2)
                n0 = FIRST[f"wq{l}"]
                for k in range(2 * PH):
                    if k >= 4:
                        pe.wait_ge(pq_ready[l], k - 3)
                    split_chunk(ps[:, k % 4, 0:TOK], n0 + k, k, f"wq{l}")
                n0 = FIRST[f"keys{l}"]
                need(n0, 0)
                pe.wait_ge(pq_ready[l], 2 * PH)
                n = 0
                for b, (t0, nb) in enumerate(BLOCKS):
                    for q in range(4):
                        if n >= 4:
                            pe.wait_ge(sc_ready[l], n - 3)
                        for i in range(4):
                            k = 4 * q + i
                            last = mm(ps[0:nb, 4 + n % 4, i * P:(i + 1) * P], pq[:, k, t0:t0 + nb],
                                      w_at(n0, k // 8, k % 8))
                            if n == 0 and i == 0:
                                begins(last, n0, 0)
                        last.then_inc(sc_done[l], 1)
                        n += 1

                def u_rows(r, first_row):
                    for k in range(SLOTS):
                        row = first_row + k
                        n, rounds = u_tile_at(l, row, r)
                        if not (isinstance(r, int) and row + SLOTS * r < 4):
                            pe.wait_ge(g_ready[l], r * SLOTS + (row - 3))
                        split_chunk(ps[:, row % 4, 0:TOK], n, row, f"u{l}", r)
                        if l == 0 and first_row == 0:
                            need(n + 1, 0, rounds)
                            chunk(ps[:, 7, bass.ds(r * (SLOTS * NSEQ) + k * NSEQ, NSEQ)], n + 1, 0, c_in)\
                                .then_inc(ada_done, 1)
                mixed = 6 * NC // SLOTS if l == 0 else KEYS // SLOTS
                pe.wait_ge(sc_ready[l], n)
                u_rows(0, 0)
                with pe.Fori(1, mixed) as r:
                    u_rows(r, 0)
                if l == 0:
                    with pe.Fori(0, KEYS // SLOTS - mixed) as r:
                        u_rows(r, 6 * NC)
                for b, (t0, nb) in enumerate(BLOCKS):
                    pe.wait_ge(picks_ready[l], b + 1)
                    for i in range(3):
                        last = nc.tensor.transpose(ps[:, 4 + b, i * P:i * P + nb], picks[0:nb, b, i, :],
                                                   ident[0:nb, 0:nb])
                    last.then_inc(pickT_done[l], 1)

                def route(r, s):
                    pe.wait_ge(oh_i_ready[l], r * OH + (s + 1))
                    pe.wait_ge(oh_j_ready[l], r * OH + (s + 1))
                    if not (isinstance(r, int) and r == 0):
                        pe.wait_ge(routed[l], r * OH + (s + 1 - OH))
                    for i in range(4):
                        last = mm(ps[:, s, i * P:(i + 1) * P], oh_j[s][:, i, :], oh_i[s][:, i, :])
                    last.then_inc(route_done[l], 1)
                pe.wait_ge(g_ready[l], KEYS)
                for s in range(OH):
                    route(0, s)
                with pe.Fori(1, GROUPS // OH) as r:
                    for s in range(OH):
                        route(r, s)
                for s in range(GROUPS % OH):
                    route(GROUPS // OH, s)
                n0 = FIRST[f"v{l}"]
                pe.wait_ge(routed[l], GROUPS)
                pe.wait_ge(mod_ready, 3)

                def v_rows(r, first=False, end=False):
                    for k in range(SLOTS):
                        pe.wait_ge(g_lo_ready[l], r * SLOTS + (k + 1))
                        split_chunk(None, n0 + k, k, f"v{l}", r, first and k == 0, end and k == SLOTS - 1, k)
                v_rows(0, first=True)
                with pe.Fori(1, KEYS // SLOTS - 1) as r:
                    v_rows(r)
                v_rows(KEYS // SLOTS - 1, end=True)

            peer(0)

            pe.wait_ge(x_ready, 2)
            norm_sum(2)
            pe.wait_ge(h_ready, 3)
            n0 = FIRST["ml_x"]
            for k in range(KM):
                if k >= 4:
                    pe.wait_ge(mx_copied, k - 3)
                split_chunk(ps[:, k % 4, 0:TOK], n0 + k, k, "ml_x")
            n0 = FIRST["ml_qkv"]
            pe.wait_ge(ml_inputs_in, 16 * 3)
            n = nt = 0
            for j in range(3):
                need(n0, 2 * j)

                def tokens(c, lo, hi):
                    if j < 2:
                        return xc[:, c, lo:hi]
                    return xms[:, c, 3, :] if lo == NPR else xm[:, c, 3 + lo:3 + hi]
                for c in range(KM):
                    if n >= 4:
                        pe.wait_ge(qkv_act, n - 3)
                    if j == 0:
                        pe.wait_ge(xc_ready, c + 1)
                    w = w_at(n0, 2 * j + c // NC, c % NC)
                    first = mm(ps[:, 4 + n % 4, NPR:TOK], w, tokens(c, NPR, TOK))
                    if c == 0:
                        begins(first, n0, 2 * j)
                    mm(ps[:, 4 + n % 4, 0:NPR], w, tokens(c, 0, NPR)).then_inc(qkv_done, 1)
                    n += 1
                for t0, nb in BLOCKS[:(0, 2, 3)[j]]:
                    for q in range(KM // 4):
                        if nt >= 4:
                            pe.wait_ge(vk_copied, nt - 3)
                        for i in range(4):
                            c = 4 * q + i
                            last = mm(ps[0:nb, nt % 4, i * P:(i + 1) * P], tokens(c, t0, t0 + nb),
                                      w_at(n0, 2 * j + c // NC, c % NC))
                        last.then_inc(vk_done, 1)
                        nt += 1
            pe.wait_ge(qkv_act, 3 * KM)
            for g in range(2):
                for j, src in enumerate((qT, kT, vT)):
                    for c in range(KM):
                        last = mm(ps[0:HEADS, 4 + g, 0:TOK], gates[:, j * KM + c, g * HEADS:(g + 1) * HEADS],
                                  src[:, c, :], j == 0 and c == 0, j == 2 and c == KM - 1)
            last.then_inc(gate_done, 1)
            pe.wait_ge(vk_copied, nt)
            for hd in range(HEADS):
                for b in range(2):
                    o = ps[:, hd, 0:NPR] if b == 0 else ps[:, hd, NPR:NPR + P]
                    for c in range(HC):
                        last = mm(o, kT[:, hd * HC + c, b * P:(b + 1) * P], qT[:, hd * HC + c, b * P:NPR],
                                  c == 0, c == HC - 1)
            last.then_inc(st_done, 1)
            pe.wait_ge(rows_ready, 1)
            for hd in range(HEADS):
                pick = ident[0:HEADS, hd:hd + 1].to_broadcast([HEADS, P])
                half = slice(hd % 2 * NPR, (hd % 2 + 1) * NPR)
                mm(ps[:, 4 + hd // 2, half], pick, frow[0:HEADS, 0:NPR])
                last = mm(ps[:, 6 + hd // 2, half], pick, mrow[0:HEADS, 0:NPR])
            last.then_inc(bcast_done, 1)
            pe.wait_ge(em_ready, 1)
            for b in range(2):
                last = nc.tensor.transpose(ps[:, 6, b * HEADS:(b + 1) * HEADS], Grow[0:HEADS, b * P:(b + 1) * P],
                                           ident[0:HEADS, 0:HEADS])
            last.then_inc(gcol_done, 1)
            pe.wait_ge(srow_exp, 1)
            for hd in range(HEADS):
                last = mm(ps[:, 7, hd * 3 * NSMP:(hd + 1) * 3 * NSMP],
                          ident[0:HEADS, hd:hd + 1].to_broadcast([HEADS, P]),
                          srow[0:HEADS].rearrange("p a b -> p (a b)"))
            last.then_inc(sbc_done, 1)
            pe.wait_ge(sw_ready, 1)
            for hd in range(HEADS):
                o = ps[:, 4 + hd // 2, hd % 2 * NPR:(hd % 2 + 1) * NPR]
                mm(o, ones, Sw[:, hd, 0:NPR])
                last = mm(o[:, P:NPR], ones, Sw[:, hd, NPR:NPR + P], False, True, True)
            last.then_inc(den_done, 1)
            for hd in range(HEADS):
                if hd >= 2:
                    pe.wait_ge(num_read, hd - 1)
                for e in range(HC):
                    o = ps[:, hd % 2 * 2 + e // 2, e % 2 * NPR:(e % 2 + 1) * NPR]
                    e0 = (hd * HC + e) * P
                    mm(o, vt[:, 0, e0:e0 + P], Sw[:, hd, 0:NPR])
                    last = mm(o[:, P:NPR], vt[:, 1, e0:e0 + P], Sw[:, hd, NPR:NPR + P], False, True, True)
                last.then_inc(num_done, 1)
            pe.wait_ge(sqn_ready, 1)
            for hd in range(HEADS):
                for c in range(HC):
                    last = mm(ps[:, 7, P + hd * NSMP:P + (hd + 1) * NSMP], ones, qn[:, hd * HC + c, :],
                              c == 0, c == HC - 1)
            last.then_inc(sden_done, 1)
            pe.wait_ge(kw_ready, 1)
            pe.wait_ge(num_read, HEADS)
            for n in range(KM):
                hd = n // HC
                if n >= 4:
                    pe.wait_ge(cp_copied, n - 3)
                for b in range(2):
                    mm(ps[:, 6, 16 + n:17 + n], kt[:, b, n * P:(n + 1) * P], ones[:, 0:1], b == 0, b == 1)
                for b in range(2):
                    last = mm(ps[:, n % 4, :], kt[:, b, n * P:(n + 1) * P],
                              vt[:, b, hd * MHD:(hd + 1) * MHD], b == 0, b == 1)
                last.then_inc(cp_done, 1)
            pe.wait_ge(cp_copied, KM)
            pe.wait_ge(qz_ready, 1)

            def read_C(m):
                b, hd = m // HEADS, m % HEADS
                pe.wait_ge(C_new, 2 * m + 2)
                for c in range(HC):
                    last = mm(ps[0:NSMP, 4 + hd, :], qz[:, hd * HC + c, b * NSMP:(b + 1) * NSMP],
                              Cbuf[m % CBUFS][:, c, :], b == 0 and c == 0, b == NSMP - 1 and c == HC - 1)
                last.then_inc(C_read, 1)

            def head_sums(i, src, ready):
                for hd in (2 * i, 2 * i + 1):
                    o = ps[:, 2 + i, hd % 2 * NPR:(hd % 2 + 1) * NPR]
                    for c in range(HC):
                        last = mm(o, ones, src[:, hd * HC + c, 0:NPR], c == 0, c == HC - 1)
                last.then_inc(ready, 1)
            n0 = FIRST["ml_z"]
            for m in range(NSMP * HEADS):
                b, hd = m // HEADS, m % HEADS
                if m >= 2:
                    pe.wait_ge(vb_used, 2 * m - 2)
                mm(ps[:, m % 2, :], ident[0:NSMP, b:b + 1].to_broadcast([NSMP, P]),
                   vs[0:NSMP, hd * MHD:(hd + 1) * MHD]).then_inc(vb_done, 1)
                if m >= 1:
                    read_C(m - 1)
                if m < KM:
                    if m >= 2:
                        pe.wait_ge(z_ready, m - 1)
                    split_chunk(ps[:, 2 + m % 2, 0:TOK], n0 + m, m, "ml_z")
                for i in range(2):
                    if m == AT_MU + i:
                        pe.wait_ge(z_ready, KM)
                        head_sums(i, hT, mu_done)
                    if m == AT_VAR + i:
                        pe.wait_ge(hsq_ready, i + 1)
                        head_sums(i, hsq, var_done)
            read_C(NSMP * HEADS - 1)
            for hd in range(HEADS):
                pe.wait_ge(Cq_copied, hd + 1)
                for e in range(hd * HC, (hd + 1) * HC):
                    last = nc.tensor.transpose(ps[:, 0, e * NSMP:(e + 1) * NSMP], Cq[0:NSMP, e * P:(e + 1) * P],
                                               ident[0:NSMP, 0:NSMP])
            last.then_inc(Cq_turned, 1)
            pe.wait_ge(hT_ready, 1)
            mm(ps[:, 2, 0:KM * NSMP], ones, hT[:, :, NPR:TOK]).then_inc(mu_done, 1)
            pe.wait_ge(hsq_ready, 3)
            mm(ps[:, 3, 0:KM * NSMP], ones, hsq_s).then_inc(var_done, 1)
            pe.wait_ge(mly_ready, 1)
            residual_out("ml_out", hT, KM)
            peer(1)
            pe.wait_ge(x_ready, 4)
            norm_sum(4)

        @block.scalar
        def _(act):
            def flat(v):
                return v.rearrange("p c t -> p (c t)")

            def func(to, of, f, **kw_):
                return nc.scalar.activation(to, of, f, **kw_)

            def high(n, k, stage, r=0, rounds=None):
                rounds = r if rounds is None else rounds
                act.wait_ge(pair_in[n // 2 % PAIRS], (rounds + n // SLOTS + 1) * 16)
                for half in range(2):
                    j = HALF[stage] + 2 * k + half
                    if j >= HALVES or not isinstance(r, int):
                        act.wait_ge(half_used, r * (2 * SLOTS) + (j - HALVES + 1))
                    func(w_hi[:, j % HALVES, :], half_of(n, half), ACT.Copy).then_inc(hi_ready, 1)

            def tile_used(stage, k, r=0):
                act.wait_ge(half_used, r * (2 * SLOTS) + (HALF[stage] + 2 * k + 2))

            for to, of in ((c_sb[:], c_d), (cols[:], cols_d), (consts[:], consts_d), (x[:], x_d), (h0, lru_h_d)):
                act.dma_start(to, of).then_inc(inputs_in, 16)
            act.dma_start(xs[:, :, 0:3, :].rearrange("p c j b -> p c (j b)"),
                          lru_conv_d.rearrange("p c j b -> p c (j b)")).then_inc(inputs_in, 16)
            act.wait_ge(inputs_in, 16 * 6)

            def norm(n):
                if n > 0:
                    act.wait_ge(x_ready, n)
                func(flat(sq), flat(x[:]), ACT.Square).then_inc(squares_done, 1)
                act.wait_ge(ms_ready, n + 1)
                func(rstd, rstd, ACT.Sqrt).then_inc(rms_ready, 1)
                if n < 4:
                    act.wait_ge(h_made, n + 1)
                    func(flat(h_hi[:]), flat(h), ACT.Copy).then_inc(h_hi_ready, 1)
                    act.wait_ge(h_ready, n + 1)

            func(lam8[:], col("lru_lambda", 0, NC), ACT.Abs).then_inc(lam_abs, 1)
            act.wait_ge(lam_abs, 1)
            func(lam8[:], lam8[:], ACT.Exp, scale=-1.0).then_inc(lam_exp, 1)
            norm(0)
            n0 = FIRST["lru_in"]
            for k in range(2):
                high(n0 + 3 * k, k, "lru_in")
            for k in range(2 * NC):
                if k + 2 < 2 * NC:
                    high(n0 + 3 * (k + 2), k + 2, "lru_in")
                if k >= NC:
                    tile_used("lru_in", k)
                    func(ybr[:, k - NC, :], ps[:, k % 4, 0:TOK], ACT.Gelu_apprx_tanh).then_inc(lin_y, 1)
            for g, (to, bias) in enumerate(((ra, "lru_b_a"), (ig, "lru_b_i"))):
                for c in range(NC):
                    n = g * NC + c
                    act.wait_ge(lgate_done, n + 1)
                    func(to[:, c, :], ps[:, n % 6, 0:TOK], ACT.Sigmoid, bias=col(bias, c)).then_inc(lgate_act, 1)
            act.wait_ge(loga_ready, 1)
            func(flat(ra), flat(la), ACT.Exp).then_inc(a_ready, 1)
            act.wait_ge(a_ready, 1)
            func(flat(la), flat(la), ACT.Tanh, scale=-1.0).then_inc(a_ready, 1)
            act.wait_ge(tt_ready, 1)
            func(flat(la), flat(la), ACT.Sqrt).then_inc(sqrt_ready, 1)

            def peer(l):
                norm(2 * l + 1)
                if l == 1:
                    act.wait_ge(stores, 16 * 6)
                    for i in range(CBUFS):
                        act.wait_ge(C_out[i], 16 * C_uses(i))
                n0 = FIRST[f"wq{l}"]
                for k in range(2):
                    high(n0 + k, k, f"wq{l}")
                for k in range(2 * PH):
                    if k + 2 < 2 * PH:
                        high(n0 + k + 2, k + 2, f"wq{l}")
                    tile_used(f"wq{l}", k)
                    func(pq[:, k, :], ps[:, k % 4, 0:TOK], ACT.Copy).then_inc(pq_ready[l], 1)
                n = 0
                for b, (t0, nb) in enumerate(BLOCKS):
                    for q in range(4):
                        act.wait_ge(sc_done[l], n + 1)
                        func(flat(S[0:nb, b, 4 * q:4 * q + 4, :]), ps[0:nb, 4 + n % 4, :], ACT.Copy)\
                            .then_inc(sc_ready[l], 1)
                        n += 1

                if l == 0:
                    act.wait_ge(stores, 16 * 3)

                def rows(r, first_row, n_rows=SLOTS):
                    for k in range(n_rows):
                        row = first_row + k
                        if not (isinstance(r, int) and row + SLOTS * r + 2 >= KEYS):
                            n, rounds = u_tile_at(l, row + 2, r)
                            high(n, row + 2, f"u{l}", r, rounds)
                        tile_used(f"u{l}", row, r)
                        func(BIG[:, bass.ds(r * (SLOTS * TOK) + row * TOK, TOK)], ps[:, row % 4, 0:TOK],
                             ACT.Gelu_apprx_tanh).then_inc(g_ready[l], 1)

                for row in range(2):
                    high(u_tile_at(l, row)[0], row, f"u{l}")
                at = 0
                for until in (EXP_ROWS[0], 6 * NC, EXP_ROWS[1], EXP_ROWS[2], FREE_ROW, KEYS):
                    ends = until in (6 * NC, KEYS)
                    if until - SLOTS * ends > at:
                        with act.Fori(0, (until - at) // SLOTS - ends) as r:
                            rows(r, at)
                    if ends:
                        rows(0, until - SLOTS)
                    at = until
                    if until in EXP_ROWS:
                        b = EXP_ROWS.index(until)
                        nb = BLOCKS[b][1]
                        act.wait_ge(top_ready[l], b + 1)
                        func(picks[0:nb, b, 2, :], picks[0:nb, b, 2, :], ACT.Exp).then_inc(topexp_ready[l], 1)
                    if until == FREE_ROW:
                        act.wait_ge(work_free[l], 1)

                def build(r, s):
                    if not (isinstance(r, int) and r == 0):
                        act.wait_ge(route_done[l], r * OH + (s + 1 - OH))
                    for i in range(4):
                        last = func(oh_j[s][:, i, :], iota, ACT.Abs, scale=-1.0,
                                    bias=pickT[:, 1, bass.ds(r * (4 * OH) + (4 * s + i), 1)])
                    last.then_inc(oh_j_abs[l], 1)
                    act.wait_ge(oh_j_abs[l], r * OH + (s + 1))
                    func(flat(oh_j[s]), flat(oh_j[s]), ACT.Relu, scale=-1.0, bias=1.0).then_inc(oh_j_ready[l], 1)
                act.wait_ge(pickT_ready[l], 1)
                for s in range(OH):
                    build(0, s)
                with act.Fori(1, GROUPS // OH) as r:
                    for s in range(OH):
                        build(r, s)
                for s in range(GROUPS % OH):
                    build(GROUPS // OH, s)

                act.wait_ge(route_done[l], GROUPS)
                act.wait_ge(routed[l], GROUPS)
                n0 = FIRST[f"v{l}"]

                def v_rows(r):
                    for k in range(SLOTS):
                        high(n0 + k, k, f"v{l}", r)
                        if not (isinstance(r, int) and k < 2):
                            act.wait_ge(half_used, r * (2 * SLOTS) + (HALF[f"v{l}"] + 2 * k - 2))
                        func(g_hi[:, k % 2, :], BIG[:, bass.ds(r * (SLOTS * TOK) + k * TOK, TOK)], ACT.Copy)\
                            .then_inc(g_hi_ready[l], 1)
                v_rows(0)
                with act.Fori(1, KEYS // SLOTS) as r:
                    v_rows(r)

            peer(0)

            norm(2)
            n0 = FIRST["ml_x"]
            for k in range(2):
                high(n0 + k, k, "ml_x")
            for k in range(KM + 1):
                if k + 2 < KM:
                    high(n0 + k + 2, k + 2, "ml_x")
                if k >= 1:
                    act.wait_ge(conv_ready, k)
                    func(xc[:, k - 1, :], xc[:, k - 1, :], ACT.Silu).then_inc(xc_ready, 1)
            n = 0
            for j, to in enumerate((qT, kT, vT)):
                for c in range(KM):
                    act.wait_ge(qkv_done, n + 1)
                    func(to[:, c, :], ps[:, 4 + n % 4, 0:TOK], ACT.Copy,
                         scale=float(MHD) ** -0.5 if j == 1 else 1.0).then_inc(qkv_act, 1)
                    n += 1
            act.wait_ge(gate_raw, 1)
            func(exp_f[0:HEADS], frow[0:HEADS], ACT.Abs).then_inc(gate_exp, 1)
            act.wait_ge(gate_exp, 1)
            func(exp_f[0:HEADS], exp_f[0:HEADS], ACT.Exp, scale=-1.0).then_inc(gate_exp, 1)
            act.wait_ge(bcast_done, 1)
            act.wait_ge(ml_conv_stored, 32)
            for i in range(2):
                last = func(flat(em[:, 2 * i:2 * i + 2, :]), ps[:, 6 + i, :], ACT.Exp, scale=-1.0)
            last.then_inc(em_ready, 1)
            act.wait_ge(rows_ready, 1)
            func(flat(srow[0:HEADS]), flat(srow[0:HEADS]), ACT.Exp).then_inc(srow_exp, 1)
            act.wait_ge(wexp_in, 1)
            for hd in range(HEADS):
                for b in range(2):
                    w = Wt[:, hd, 0:NPR] if b == 0 else Wt[:, hd, NPR:NPR + P]
                    last = func(w, w, ACT.Exp, bias=gcol[:, b * HEADS + hd:b * HEADS + hd + 1])
            last.then_inc(w_ready, 1)
            act.wait_ge(sqn_ready, 1)
            act.wait_ge(cp_copied, KM)
            n0 = FIRST["ml_z"]
            for k in range(2):
                high(n0 + k, k, "ml_z")
            for m in range(NSMP * HEADS):
                b, hd = m // HEADS, m % HEADS
                act.wait_ge(vb_done, m + 1)
                for q in range(2):
                    if m >= 1:
                        act.wait_ge(C_new, 2 * m + q - 1)
                    for i in range(HC // 2):
                        c = q * (HC // 2) + i
                        last = func(vk[q][:, i, :], ps[:, m % 2, :], ACT.Copy, scale=kw[:, hd * HC + c, b:b + 1])
                    last.then_inc(vb_used, 1)
                if m == 1:
                    for i in range(8):
                        act.wait_ge(cp_stored[i], 16 * KM // 8)
                if 1 <= m <= KM:
                    k = m - 1
                    if k + 2 < KM:
                        high(n0 + k + 2, k + 2, "ml_z")
                    tile_used("ml_z", k)
                    func(z[:, k, :], ps[:, 2 + k % 2, 0:TOK], ACT.Silu).then_inc(z_ready, 1)
                if m < KM:
                    func(xc[:, m, :], xc[:, m, :], ACT.Copy, scale=col("ml_skip", m)).then_inc(skip_ready, 1)
                for i in range(2):
                    if m == AT_SQUARE + i:
                        act.wait_ge(hc_ready, i + 1)
                        func(hsq[:, 8 * i:8 * i + 8, :], hT[:, 8 * i:8 * i + 8, 0:NPR], ACT.Square)\
                            .then_inc(hsq_ready, 1)
                    if m == AT_SQRT + i:
                        act.wait_ge(hvar_ready, i + 1)
                        func(flat(hstd[:, 2 * i:2 * i + 2]), flat(hstd[:, 2 * i:2 * i + 2]), ACT.Sqrt)\
                            .then_inc(hstd_ready, 1)
            act.wait_ge(hvar_ready, 3)
            func(flat(std_s), flat(std_s), ACT.Sqrt).then_inc(hstd_ready, 1)
            peer(1)
            norm(4)

        @block.gpsimd
        def _(pool):
            def joined(v):
                return v.rearrange("p c j b -> p c (j b)")

            def flat(v):
                return v.rearrange("p a b -> p (a b)")

            def load_C(m):
                pool.dma_start(flat(Cbuf[m % CBUFS]), C_d[m]).then_inc(C_in[m % CBUFS], 16)

            pool.wait_ge(hs_ready, 1)
            pool.dma_start(lru_h_o, xr[:, :, NPR - 1:TOK]).then_inc(stores, 16)
            pool.dma_start(lru_conv_p_o, xp[:, :, NPR:NPR + 3]).then_inc(stores, 16)
            pool.dma_start(joined(lru_conv_s_o), joined(xs[:, :, 1:4, :])).then_inc(stores, 16)
            pool.wait_ge(x_ready, 2)
            pool.dma_start(gates, gates_d).then_inc(ml_inputs_in, 16)
            pool.dma_start(nst, ml_n_d).then_inc(ml_inputs_in, 16)
            pool.dma_start(joined(xms[:, :, 0:3, :]), joined(ml_conv_d)).then_inc(ml_inputs_in, 16)
            pool.wait_ge(conv_ready, KM)
            pool.dma_start(ml_conv_p_o, xm[:, :, NPR:NPR + 3]).then_inc(ml_conv_stored, 16)
            pool.dma_start(joined(ml_conv_s_o), joined(xms[:, :, 1:4, :])).then_inc(ml_conv_stored, 16)
            pool.wait_ge(rows_ready, 1)
            pool.dma_start(m_o, mrow[0:HEADS, NPR - 1:TOK]).then_inc(stores, 16)
            pool.wait_ge(sqn_ready, 1)
            pool.dma_start(n_s_o, nst).then_inc(stores, 16)
            pool.wait_ge(st_done, 1)
            load_C(0)
            for n in range(KM):
                pool.wait_ge(cp_copied, n + 1)
                pool.dma_start(C_p_o[n], Cst[:, n % 8, :]).then_inc(cp_stored[n % 8], 16)
            pool.wait_ge(npr_ready, 1)
            pool.dma_start(n_p_o, npr).then_inc(stores, 16)
            pool.wait_ge(cp_done, KM)
            for m in range(1, CBUFS):
                load_C(m)
            for m in range(NSMP * HEADS):
                pool.wait_ge(C_read, m + 1)
                pool.dma_start(C_s_o[m], flat(Cbuf[m % CBUFS])).then_inc(C_out[m % CBUFS], 16)
                if 1 <= m and m - 1 + CBUFS < NSMP * HEADS:
                    pool.wait_ge(C_out[(m - 1) % CBUFS], 16 * ((m - 1) // CBUFS + 1))
                    load_C(m - 1 + CBUFS)
            pool.wait_ge(y_ready, 1)
            pool.dma_start(y_o, h).then_inc(stores, 16)
            pool.wait_ge(stores, 16 * 7)
            pool.wait_ge(ml_conv_stored, 16 * 2)
            for i in range(8):
                pool.wait_ge(cp_stored[i], 16 * KM // 8)
            for i in range(CBUFS):
                pool.wait_ge(C_out[i], 16 * C_uses(i))

        @block.vector
        def _(dve):
            count = [0]

            def link(ins):
                count[0] += 1
                ins.then_inc(dve_seq, 1)
                dve.wait_ge(dve_seq, count[0])

            vec = nc.vector
            tt, ts, stt = vec.tensor_tensor, vec.tensor_scalar, vec.scalar_tensor_tensor

            def flat(v):
                return v.rearrange("p c t -> p (c t)")

            def low(n, k, stage, r=0):
                for half in range(2):
                    j = HALF[stage] + 2 * k + half
                    dve.wait_ge(hi_ready, r * (2 * SLOTS) + (j + 1))
                    tt(w_lo[:, j % HALVES, :], half_of(n, half), w_hi[:, j % HALVES, :].bitcast(F32),
                       ALU.subtract).then_inc(lo_ready, 1)

            def tile_used(stage, k):
                dve.wait_ge(half_used, HALF[stage] + 2 * k + 2)

            def minus_softplus(out, raw, e, z_, z2, p, scale_):
                link(ts(z_, e, 2.0, None, ALU.add))
                link(vec.reciprocal(z_, z_))
                link(tt(z_, z_, e, ALU.mult))
                link(tt(z2, z_, z_, ALU.mult))
                link(ts(p, z2, 1.0 / (2 * N_LOG1P + 1), None, ALU.mult))
                for i in range(N_LOG1P - 1, 0, -1):
                    link(stt(p, p, 1.0 / (2 * i + 1), z2, ALU.add, ALU.mult))
                link(stt(p, p, 1.0, z_, ALU.add, ALU.mult))
                link(ts(out, raw, 0.0, None, ALU.min))
                link(stt(out, p, -2.0, out, ALU.mult, ALU.add))
                if scale_ != 1.0:
                    link(ts(out, out, scale_, None, ALU.mult))

            def over_tokens(v, n):
                return v.unsqueeze(2).to_broadcast([P, v.shape[1], n])

            def norm(n, gain, l, part):
                shift = mod[l][:, part * NC:(part + 1) * NC, :]
                link(stt(scale, mod[l][:, (part + 1) * NC:(part + 2) * NC, :], 1.0,
                         over_tokens(col(gain, 0, NC), NSEQ), ALU.add, ALU.mult))
                dve.wait_ge(ssq_done, n + 1)
                ts(rstd, ps[:, 0, 0:TOK], 1.0 / D, EPS, ALU.mult, ALU.add).then_inc(ms_ready, 1)
                dve.wait_ge(rms_ready, n + 1)
                link(vec.reciprocal(rstd, rstd))
                link(tt(h, x[:], rstd.unsqueeze(1).to_broadcast([P, NC, TOK]), ALU.mult))
                for c in range(NC):
                    ts(h[:, c, 0:NPR], h[:, c, 0:NPR], scale[:, c, 0:1], shift[:, c, 0:1], ALU.mult, ALU.add)
                link(tt(h[:, :, NPR:TOK], h[:, :, NPR:TOK], scale[:, :, 1:NSEQ], ALU.mult))
                tt(h[:, :, NPR:TOK], h[:, :, NPR:TOK], shift[:, :, 1:NSEQ], ALU.add).then_inc(h_made, 1)
                dve.wait_ge(h_hi_ready, n + 1)
                tt(h_lo[:], h, h_hi[:].bitcast(F32), ALU.subtract).then_inc(h_ready, 1)

            def residual(n, l, part):
                gate = mod[l][:, part * NC:(part + 1) * NC, :]
                gated = scr(TOK, NC, NSMP)
                if part == 5:
                    tile_used(f"v{l}", KEYS - 1)
                else:
                    dve.wait_ge(out_done, n // 2 + 1)
                link(tt(gated, ps[:, 0:NC, NPR:TOK], gate[:, :, 1:NSEQ], ALU.mult))
                for m in range(NC):
                    stt(x[:, m, 0:NPR], ps[:, m, 0:NPR], gate[:, m, 0:1], x[:, m, 0:NPR], ALU.mult, ALU.add)
                tt(x[:, :, NPR:TOK], x[:, :, NPR:TOK], gated, ALU.add).then_inc(x_ready, 1)
                dve.wait_ge(x_ready, n + 1)

            def convolve(out, prompt, samples, c, nch, w, b):
                o_p, o_s = out[:, c, 0:NPR], out[:, c, NPR:TOK]
                ts(o_p, prompt[:, c, 0:NPR], col(w, c), col(b, c), ALU.mult, ALU.add)
                link(ts(o_s, samples[:, c, 0, :], col(w, c), col(b, c), ALU.mult, ALU.add))
                for j in range(1, 4):
                    w_j = col(w, j * nch + c)
                    stt(o_p, prompt[:, c, j:j + NPR], w_j, o_p, ALU.mult, ALU.add)
                    last = stt(o_s, samples[:, c, j, :], w_j, o_s, ALU.mult, ALU.add)
                    if j < 3:
                        link(last)
                return last

            dve.wait_ge(inputs_in, 16 * 6)
            link(vec.memset(xp[:, :, 0:3], 0.0))
            dve.wait_ge(lam_exp, 1)
            minus_softplus(lam8[:], col("lru_lambda", 0, NC), lam8[:], scr(512, NC), scr(520, NC), scr(528, NC),
                           LRU_C)

            def modulation(l, first, n, seen):
                tt(mod[l][:, first:first + n, :],
                   ps[:, 6 + l, first * NSEQ:(first + n) * NSEQ].rearrange("p (c s) -> p c s", s=NSEQ),
                   over_tokens(col(f"b_ada{l}", first, n), NSEQ), ALU.add).then_inc(mod_ready, 1)
                dve.wait_ge(mod_ready, seen)

            dve.wait_ge(ada_done, 1)
            modulation(0, 0, 2 * NC, 1)

            norm(0, "norm_mix0", 0, 0)
            n0 = FIRST["lru_in"]
            for k in range(2):
                low(n0 + 3 * k, k, "lru_in")
            for c in range(2 * NC):
                if c + 2 < 2 * NC:
                    low(n0 + 3 * (c + 2), c + 2, "lru_in")
                if c >= NC:
                    continue
                tile_used("lru_in", c)
                vec.tensor_copy(xp[:, c, 3:3 + NPR], ps[:, c % 4, 0:NPR])
                vec.tensor_copy(xs[:, c, 3, :], ps[:, c % 4, NPR:TOK]).then_inc(lin_x, 1)
                dve.wait_ge(lin_x, c + 1)
                convolve(xr, xp, xs, c, NC, "lru_conv_w", "lru_conv_b").then_inc(xr_ready, 1)
            dve.wait_ge(xr_ready, NC)
            dve.wait_ge(ada_done, 2)
            modulation(0, 2 * NC, 4 * NC, 2)
            dve.wait_ge(lgate_act, 2 * NC)
            tt(la, ra, over_tokens(lam8[:], TOK), ALU.mult).then_inc(loga_ready, 1)
            link(tt(ig, ig, xr, ALU.mult))
            dve.wait_ge(a_ready, 2)
            link(tt(bx, ra, ra, ALU.mult))
            stt(la, bx, 1.0, la, ALU.add, ALU.mult).then_inc(tt_ready, 1)
            dve.wait_ge(sqrt_ready, 1)
            link(tt(bx, la, ig, ALU.mult))
            link(tt(stmp, ra[:, :, NPR:TOK], h0, ALU.mult))
            for c in range(NC):
                vec.tensor_tensor_scan(xr[:, c, 0:NPR], ra[:, c, 0:NPR], bx[:, c, 0:NPR], 0.0, ALU.mult, ALU.add)
            tt(xr[:, :, NPR:TOK], bx[:, :, NPR:TOK], stmp, ALU.add).then_inc(hs_ready, 1)
            dve.wait_ge(hs_ready, 1)
            dve.wait_ge(lin_y, NC)
            tt(ybr, ybr, xr, ALU.mult).then_inc(ly_ready, 1)
            residual(0, 0, 2)

            def peer(l):
                norm(2 * l + 1, f"norm_ffn{l}", l, 3)
                for k in range(2 * PH):
                    low(FIRST[f"wq{l}"] + k, k, f"wq{l}")
                rows = [0]

                def low_row():
                    if rows[0] < KEYS:
                        low(u_tile_at(l, rows[0])[0], rows[0], f"u{l}")
                        rows[0] += 1
                for _ in range(2):
                    low_row()
                for b, (t0, nb) in enumerate(BLOCKS):
                    Sb, V, I = S[0:nb, b], vals[0:nb], idx[0:nb]
                    cd, tp, ps_ = cand[0:nb], top[0:nb], pos[0:nb]

                    def top16(v, i, of, n):
                        for k in range(n):
                            if k % (n // 2) == 0:
                                low_row()
                            last = vec.max(v[:, k, 0:8], of[:, k, :])
                        link(last)
                        for k in range(n):
                            if k % (n // 2) == 0:
                                low_row()
                            last = vec.max_index(i[:, k, 0:8], v[:, k, 0:8], of[:, k, :])
                        link(last)
                        for k in range(n):
                            if k % (n // 2) == 0:
                                low_row()
                            last = vec.match_replace(of[:, k, :], v[:, k, 0:8], of[:, k, :], LOWEST)
                        link(last)
                        for k in range(n):
                            if k % (n // 2) == 0:
                                low_row()
                            last = vec.max(v[:, k, 8:16], of[:, k, :])
                        link(last)
                        for k in range(n):
                            if k % (n // 2) == 0:
                                low_row()
                            last = vec.max_index(i[:, k, 8:16], v[:, k, 8:16], of[:, k, :])
                        link(last)

                    dve.wait_ge(sc_ready[l], 4 * (b + 1))
                    top16(V, I, Sb, 2 * PH)
                    vec.tensor_copy(flat(idxf[0:nb]), flat(I))
                    V4 = V.rearrange("p (a two) k -> p a two k", two=2)
                    I4 = idxf[0:nb].rearrange("p (a two) k -> p a two k", two=2)
                    full = [nb, PH, TOPK, TOPK]
                    link(tt(cd.rearrange("p a (i j) -> p a i j", j=TOPK),
                            V4[:, :, 0, :].unsqueeze(3).to_broadcast(full),
                            V4[:, :, 1, :].unsqueeze(2).to_broadcast(full), ALU.add))
                    top16(tp, ps_, cd, PH)
                    tt(picks[0:nb, b, 2, :].rearrange("p (a k) -> p a k", a=PH), tp,
                       tp[:, :, 0:1].to_broadcast([nb, PH, TOPK]), ALU.subtract).then_inc(top_ready[l], 1)
                    assert b >= NB or rows[0] <= EXP_ROWS[b] + 2
                    vec.tensor_single_scalar(ab[0:nb, 0, :], flat(ps_), 4, ALU.logical_shift_right)
                    link(vec.tensor_single_scalar(ab[0:nb, 1, :], flat(ps_), TOPK - 1, ALU.bitwise_and))
                    link(vec.tensor_copy(flat(abf[0:nb]), flat(ab[0:nb])))
                    for i in range(2):
                        e = eq[0:nb]
                        link(tt(e, abf[0:nb, i, :].unsqueeze(2).to_broadcast([nb, PICKS, TOPK]),
                                iota[0:nb, 0:TOPK].unsqueeze(1).to_broadcast([nb, PICKS, TOPK]), ALU.is_equal))
                        low_row()
                        e4 = e.rearrange("p (a k) j -> p a k j", a=PH)
                        link(tt(e4, e4, I4[:, :, i, :].unsqueeze(2).to_broadcast(full), ALU.mult))
                        low_row()
                        last = vec.reduce_sum(picks[0:nb, b, i, :], e, axis=AX_X)
                        if b < NB - 1 or i == 0:
                            link(last)
                last.then_inc(work_free[l], 1)
                assert rows[0] <= FREE_ROW + 2
                while rows[0] < KEYS:
                    low_row()
                for b, (t0, nb) in enumerate(BLOCKS):
                    dve.wait_ge(topexp_ready[l], b + 1)
                    wexp = picks[0:nb, b, 2, :].rearrange("p (a k) -> p a k", a=PH)
                    link(vec.reduce_sum(ssum[0:nb, b], wexp, axis=AX_X))
                    link(vec.reciprocal(ssum[0:nb, b], ssum[0:nb, b]))
                    tt(wexp, wexp, ssum[0:nb, b].unsqueeze(2).to_broadcast([nb, PH, TOPK]), ALU.mult)\
                        .then_inc(picks_ready[l], 1)
                if l == 0:
                    dve.wait_ge(ada_done, 2 + 6 * NC)
                    modulation(1, 0, 6 * NC, 3)
                for b, (t0, nb) in enumerate(BLOCKS):
                    dve.wait_ge(pickT_done[l], b + 1)
                    last = vec.tensor_copy(
                        pickT[:, :, t0:t0 + nb],
                        ps[:, 4 + b, 0:3 * P].rearrange("p (i t) -> p i t", i=3)[:, :, 0:nb])
                last.then_inc(pickT_ready[l], 1)
                dve.wait_ge(pickT_ready[l], 1)

                def build(g, s):
                    for i in range(4):
                        t = bass.ds(g * 4 + i, 1)
                        last = ts(oh_i[s][:, i, :], iota, pickT[:, 0, t], pickT[:, 2, t], ALU.is_equal, ALU.mult)
                    last.then_inc(oh_i_ready[l], 1)

                def weigh(g, s):
                    Gt = G[:, :, bass.ds(g * 4, 4)].rearrange("p r t -> p t r")
                    tt(Gt, ps[:, s, :].rearrange("p (t r) -> p t r", t=4), Gt, ALU.mult).then_inc(routed[l], 1)
                build(0, 0)
                build(1, 1)
                dve.wait_ge(g_ready[l], KEYS)
                assert GROUPS % OH == 2
                with dve.Fori(0, GROUPS // OH) as r:
                    for s in range(OH):
                        dve.wait_ge(route_done[l], r * OH + (s + 1))
                        weigh(r * OH + s, s)
                        build(r * OH + (s + 2), (s + 2) % OH)
                for s in range(2):
                    dve.wait_ge(route_done[l], GROUPS - 1 + s)
                    weigh(GROUPS - 2 + s, s)

                dve.wait_ge(routed[l], GROUPS)

                def v_rows(r):
                    for k in range(SLOTS):
                        low(FIRST[f"v{l}"] + k, k, f"v{l}", r)
                        dve.wait_ge(g_hi_ready[l], r * SLOTS + (k + 1))
                        tt(g_lo[:, k % 2, :], BIG[:, bass.ds(r * (SLOTS * TOK) + k * TOK, TOK)],
                           g_hi[:, k % 2, :].bitcast(F32), ALU.subtract).then_inc(g_lo_ready[l], 1)
                with dve.Fori(0, KEYS // SLOTS) as r:
                    v_rows(r)
                residual(2 * l + 1, l, 5)

            peer(0)

            norm(2, "norm_mix1", 1, 0)
            link(vec.memset(xm[:, :, 0:3], 0.0))
            dve.wait_ge(ml_inputs_in, 16 * 3)
            for k in range(2):
                low(FIRST["ml_x"] + k, k, "ml_x")
            for k in range(KM):
                if k + 2 < KM:
                    low(FIRST["ml_x"] + k + 2, k + 2, "ml_x")
                tile_used("ml_x", k)
                vec.tensor_copy(xm[:, k, 3:3 + NPR], ps[:, k % 4, 0:NPR])
                vec.tensor_copy(xms[:, k, 3, :], ps[:, k % 4, NPR:TOK]).then_inc(mx_copied, 1)
                dve.wait_ge(mx_copied, k + 1)
                convolve(xc, xm, xms, k, KM, "ml_conv_w", "ml_conv_b").then_inc(conv_ready, 1)
            n = 0
            for to, factor, nblocks in ((kt, float(MHD) ** -0.5, 2), (vt, 1.0, 3)):
                for b in range(nblocks):
                    nb = BLOCKS[b][1]
                    for q in range(KM // 4):
                        dve.wait_ge(vk_done, n + 1)
                        o = to[:, b, q * BANK:(q + 1) * BANK] if b < 2 else vs[0:nb, q * BANK:(q + 1) * BANK]
                        ts(o, ps[0:nb, n % 4, :], factor, None, ALU.mult).then_inc(vk_copied, 1)
                        n += 1
            H_ = slice(0, HEADS)
            dve.wait_ge(gate_done, 1)
            ts(irow[H_], ps[H_, 4, 0:TOK], col("ml_b_ig")[H_], None, ALU.add)
            ts(frow[H_], ps[H_, 5, 0:TOK], col("ml_b_fg")[H_], None, ALU.add).then_inc(gate_raw, 1)
            dve.wait_ge(gate_exp, 2)
            link(vec.memset(zero[H_], 0.0))
            minus_softplus(t_c[H_], frow[H_], exp_f[H_], t_a[H_], t_b[H_], Frow[H_], 1.0)
            link(vec.tensor_tensor_scan(Frow[H_, 0:NPR], t_c[H_, 0:NPR], zero[H_, 0:NPR], 0.0, ALU.add, ALU.add))
            link(tt(Grow[H_, 0:NPR], irow[H_, 0:NPR], Frow[H_, 0:NPR], ALU.subtract))
            link(vec.tensor_tensor_scan(frow[H_, 0:NPR], Grow[H_, 0:NPR], Grow[H_, 0:NPR], 0.0, ALU.max, ALU.max))
            tt(mrow[H_, 0:NPR], Frow[H_, 0:NPR], frow[H_, 0:NPR], ALU.add)
            fs, is_, ms = t_c[H_, NPR:TOK], irow[H_, NPR:TOK], mrow[H_, NPR:TOK]
            link(tt(fs, fs, col("ml_m0", 0, NSMP)[H_], ALU.add))
            link(tt(ms, fs, is_, ALU.max))
            tt(srow[H_, 0, :], fs, ms, ALU.subtract)
            tt(srow[H_, 1, :], is_, ms, ALU.subtract)
            ts(srow[H_, 2, :], ms, -1.0, None, ALU.mult).then_inc(rows_ready, 1)
            dve.wait_ge(bcast_done, 1)
            for hd in range(HEADS):
                M = ps[:, 4 + hd // 2, hd % 2 * NPR:(hd % 2 + 1) * NPR]
                stt(Wt[:, hd, 0:P], M[:, 0:P], -1.0, causal, ALU.mult, ALU.add)
                ts(Wt[:, hd, P:NPR], M[:, P:NPR], -1.0, None, ALU.mult)
                stt(Wt[:, hd, NPR:NPR + P], M[:, P:NPR], -1.0, causal, ALU.mult, ALU.add)
            dve.wait_ge(gcol_done, 1)
            vec.tensor_copy(gcol, ps[:, 6, 0:2 * HEADS]).then_inc(wexp_in, 1)
            dve.wait_ge(sbc_done, 1)
            link(vec.tensor_copy(bc.rearrange("p a b c -> p (a b c)"), ps[:, 7, 0:HEADS * 3 * NSMP]))

            def per_head(v):
                return v.rearrange("p (a c) b -> p a c b", a=HEADS)

            def factor_of(i):
                return bc[:, :, i, :].unsqueeze(2).to_broadcast([P, HEADS, HC, NSMP])
            link(tt(per_head(nst), per_head(nst), factor_of(0), ALU.mult))
            link(tt(per_head(kw), per_head(kT[:, :, NPR:TOK]), factor_of(1), ALU.mult))
            link(tt(nst, nst, kw, ALU.add))
            tt(qn, qT[:, :, NPR:TOK], nst, ALU.mult).then_inc(sqn_ready, 1)
            dve.wait_ge(w_ready, 1)
            dve.wait_ge(st_done, 1)
            for hd in range(HEADS):
                last = tt(Sw[:, hd, :], ps[:, hd, 0:384], Wt[:, hd, :], ALU.mult)
            last.then_inc(sw_ready, 1)
            for hd in range(HEADS):
                for b in range(2):
                    e0 = NPR - 1 if b == 0 else NPR + P - 1
                    kh = kt[:, b, hd * MHD:(hd + 1) * MHD]
                    last = ts(kh, kh, Wt[:, hd, e0:e0 + 1], None, ALU.mult)
            last.then_inc(kw_ready, 1)
            dve.wait_ge(den_done, 1)
            dve.wait_ge(em_ready, 1)
            for i in range(2):
                e = flat(em[:, 2 * i:2 * i + 2, :])
                link(stt(e, ps[:, 4 + i, :], -1.0, e, ALU.mult, ALU.max))
                link(tt(e, ps[:, 4 + i, :], e, ALU.max))
            link(vec.reciprocal(flat(em), flat(em)))
            for hd in range(HEADS):
                dve.wait_ge(num_done, hd + 1)
                tt(hT[:, hd * HC:(hd + 1) * HC, 0:NPR],
                   ps[:, hd % 2 * 2:hd % 2 * 2 + 2, :].rearrange("p a (b t) -> p (a b) t", b=2),
                   em[:, hd:hd + 1, :].to_broadcast([P, HC, NPR]), ALU.mult).then_inc(num_read, 1)
            dve.wait_ge(sden_done, 1)
            sd = ps[:, 7, P:P + HEADS * NSMP].rearrange("p (a b) -> p a b", a=HEADS)
            link(stt(sden, sd, -1.0, bc[:, :, 2, :], ALU.mult, ALU.max))
            link(tt(sden, sd, sden, ALU.max))
            link(vec.reciprocal(sden, sden))
            dve.wait_ge(num_read, HEADS)
            for n in range(KM):
                dve.wait_ge(cp_done, n + 1)
                if n >= 8:
                    dve.wait_ge(cp_stored[n % 8], 16 * (n // 8))
                vec.tensor_copy(Cst[:, n % 8, :], ps[:, n % 4, :]).then_inc(cp_copied, 1)
            vec.tensor_copy(npr, ps[:, 6, 16:16 + KM]).then_inc(npr_ready, 1)
            link(vec.memset(qz, 0.0))
            vec.tensor_copy(qz[:, :, 0:NSMP * NSMP:NSMP + 1], qT[:, :, NPR:TOK]).then_inc(qz_ready, 1)
            for k in range(2):
                low(FIRST["ml_z"] + k, k, "ml_z")
            for m in range(NSMP * HEADS):
                b, hd = m // HEADS, m % HEADS
                dve.wait_ge(C_in[m % CBUFS], 16 * (m // CBUFS + 1))
                for q in range(2):
                    dve.wait_ge(vb_used, 2 * m + q + 1)
                    Cm = flat(Cbuf[m % CBUFS][:, q * (HC // 2):(q + 1) * (HC // 2), :])
                    stt(Cm, Cm, bc[:, hd, 0, b:b + 1], flat(vk[q]), ALU.mult, ALU.add).then_inc(C_new, 1)
                if 1 <= m < KM - 1:
                    low(FIRST["ml_z"] + m + 1, m + 1, "ml_z")
                for i in range(2):
                    part = hT[:, 8 * i:8 * i + 8, 0:NPR]
                    if m == AT_CENTRE + i:
                        dve.wait_ge(mu_done, i + 1)
                        for j in range(2):
                            ph = part[:, j * HC:(j + 1) * HC]
                            last = stt(ph, ps[:, 2 + i, j * NPR:(j + 1) * NPR].unsqueeze(1)
                                       .to_broadcast([P, HC, NPR]), -1.0 / MHD, ph, ALU.mult, ALU.add)
                        last.then_inc(hc_ready, 1)
                    if m == AT_MS + i:
                        dve.wait_ge(var_done, i + 1)
                        ts(flat(hstd[:, 2 * i:2 * i + 2]), ps[:, 2 + i, :], 1.0 / MHD, EPS, ALU.mult, ALU.add)\
                            .then_inc(hvar_ready, 1)
                    if m == AT_SCALE + i:
                        dve.wait_ge(hstd_ready, i + 1)
                        hs_ = hstd[:, 2 * i:2 * i + 2]
                        link(vec.reciprocal(hs_, hs_))
                        ph = part.rearrange("p (a c) t -> p a c t", a=2)
                        link(tt(ph, ph, hs_.unsqueeze(2).to_broadcast([P, 2, HC, NPR]), ALU.mult))
                    if m == AT_SKIP + i:
                        dve.wait_ge(skip_ready, KM)
                        for c in range(8 * i, 8 * i + 8):
                            last = stt(hT[:, c, 0:NPR], hT[:, c, 0:NPR], col("ml_ln_g", c), xc[:, c, 0:NPR],
                                       ALU.mult, ALU.add)
                        link(last)
                    if m == AT_Z + i:
                        dve.wait_ge(z_ready, KM)
                        tt(part, part, z[:, 8 * i:8 * i + 8, 0:NPR], ALU.mult)
            for hd in range(HEADS):
                dve.wait_ge(C_read, (NSMP - 1) * HEADS + hd + 1)
                vec.tensor_copy(Cq[0:NSMP, hd * MHD:(hd + 1) * MHD], ps[0:NSMP, 4 + hd, :]).then_inc(Cq_copied, 1)

            def each_chunk(v):
                return v.unsqueeze(2).to_broadcast([P, HEADS, HC, NSMP])

            def each_sample(name):
                return col(name, 0, KM).unsqueeze(2).to_broadcast([P, KM, NSMP])

            def head_sum(to, bank):
                link(vec.tensor_reduce(to, ps[:, bank, 0:KM * NSMP].rearrange("p (a c b) -> p a b c", a=HEADS, c=HC),
                                       AX_X, ALU.add))
            hs_ = hT[:, :, NPR:TOK]
            dve.wait_ge(Cq_turned, 1)
            tt(per_head(hs_), ps[:, 0, 0:KM * NSMP].rearrange("p (a c b) -> p a c b", a=HEADS, c=HC),
               each_chunk(sden), ALU.mult).then_inc(hT_ready, 1)
            dve.wait_ge(mu_done, 3)
            head_sum(mu_s, 2)
            link(ts(mu_s, mu_s, -1.0 / MHD, None, ALU.mult))
            link(tt(per_head(hs_), per_head(hs_), each_chunk(mu_s), ALU.add))
            tt(hsq_s, hs_, hs_, ALU.mult).then_inc(hsq_ready, 1)
            dve.wait_ge(var_done, 3)
            head_sum(std_s, 3)
            ts(std_s, std_s, 1.0 / MHD, EPS, ALU.mult, ALU.add).then_inc(hvar_ready, 1)
            dve.wait_ge(hstd_ready, 3)
            link(vec.reciprocal(std_s, std_s))
            link(tt(per_head(hs_), per_head(hs_), each_chunk(std_s), ALU.mult))
            link(tt(hs_, hs_, each_sample("ml_ln_g"), ALU.mult))
            link(tt(hs_, hs_, xc[:, :, NPR:TOK], ALU.add))
            tt(hs_, hs_, z[:, :, NPR:TOK], ALU.mult).then_inc(mly_ready, 1)
            residual(2, 1, 2)
            peer(1)

            dve.wait_ge(ssq_done, 5)
            ts(rstd, ps[:, 0, 0:TOK], 1.0 / D, EPS, ALU.mult, ALU.add).then_inc(ms_ready, 1)
            dve.wait_ge(rms_ready, 5)
            link(vec.reciprocal(rstd, rstd))
            link(tt(h, x[:], rstd.unsqueeze(1).to_broadcast([P, NC, TOK]), ALU.mult))
            for c in range(NC):
                last = ts(h[:, c, :], h[:, c, :], col("norm_f", c), None, ALU.mult)
            last.then_inc(y_ready, 1)


def kernel(**inputs):
    import numpy as np
    import concourse.bacc as bacc
    from concourse.bass_utils import run_bass_kernel_spmd as run

    a = {k: np.asarray(v) for k, v in inputs.items()}
    xpr, xsm = a["x_prompt"], a["x_sample"]
    T, D = xpr.shape[1:]
    B = xsm.shape[0]
    DR, MI = a["lru_w_out"].shape[1], a["ml_w_out"].shape[1]
    NC, KM = D // P, MI // P
    H = a["state_mlstm_m"].shape[2]
    f32 = np.float32

    def channels(v):
        return np.ascontiguousarray(v.reshape(v.shape[0], -1, P).transpose(2, 1, 0))

    def tiles(w):
        k, n = w.shape
        return w.reshape(k // TILE, NC, P, n // P, P).transpose(3, 0, 2, 1, 4).reshape(-1, P, TILE)

    def diagonal(w):
        n, b, _ = w.shape
        per = P // b
        out = np.zeros((n // per, P, P), f32)
        for i in range(per):
            out[:, i * b:(i + 1) * b, i * b:(i + 1) * b] = w[i::per]
        return out.reshape(-1, TILE // P, P, P).transpose(0, 2, 1, 3).reshape(-1, P, TILE)

    first, n_tiles = tile_plan(D, DR, MI, 2, P)
    stream = np.empty((n_tiles // 2, P, 2, TILE), f32)

    def put(name, t):
        n = first[name] // 2
        stream[n:n + len(t) // 2] = t.reshape(-1, 2, P, TILE).transpose(0, 2, 1, 3)

    def after_each(t, others, n):
        return np.concatenate([t[:, None], others.reshape(len(t), n, P, TILE)], axis=1).reshape(-1, P, TILE)

    ada = [tiles(a["w_ada"][l]) for l in range(2)]
    put("ada0", ada[0][:2 * NC])
    for l in range(2):
        put(f"wq{l}", tiles(a["peer_w_q"][l]))
        keys = a["peer_keys"][l].reshape(-1, P, P).transpose(0, 2, 1)
        put(f"keys{l}", keys.reshape(2, 8, P, P).transpose(0, 2, 1, 3).reshape(2, P, TILE))
        u = a["peer_u"][l].reshape(P, P, NC, P).transpose(0, 3, 2, 1).reshape(P, P, TILE)
        if l == 0:
            put("u0_ada1", after_each(u[:6 * NC], ada[1], 1))
            u = u[6 * NC:]
        put(f"u{l}", u)
        put(f"v{l}", a["peer_v"][l].reshape(P, P, TILE))
    w_in = a["lru_w_in"][0]
    put("lru_in", after_each(np.concatenate([tiles(w_in[:, DR:]), tiles(w_in[:, :DR])]), ada[0][2 * NC:], 2))
    put("lru_gates", np.concatenate([diagonal(a["lru_w_a"][0]), diagonal(a["lru_w_i"][0])]))
    put("lru_out", tiles(a["lru_w_out"][0]))
    w_in = a["ml_w_in"][0]
    put("ml_x", tiles(w_in[:, :MI]))
    put("ml_z", tiles(w_in[:, MI:]))
    put("ml_qkv", np.concatenate([diagonal(a[f"ml_w_{c}"][0]) for c in "qkv"]))
    put("ml_out", tiles(a["ml_w_out"][0]))

    where, n_cols = column_layout(D, DR, MI)
    cols = np.zeros((P, n_cols), f32)

    def put_cols(name, v):
        v = v.reshape(-1, P).T
        cols[:, where[name][0]:where[name][0] + v.shape[1]] = v

    for l in range(2):
        for name in ("norm_mix", "norm_ffn", "b_ada"):
            put_cols(f"{name}{l}", a[name][l])
    put_cols("norm_f", a["norm_f"])
    for name in ("lru_conv_w", "lru_conv_b", "lru_b_a", "lru_b_i", "lru_lambda", "ml_conv_w", "ml_conv_b",
                 "ml_skip", "ml_ln_g"):
        put_cols(name, a[name][0])
    for name in ("ml_b_ig", "ml_b_fg"):
        cols[:H, where[name][0]] = a[name][0]
    cols[:H, where["ml_m0"][0]:where["ml_m0"][0] + B] = a["state_mlstm_m"][0].T

    consts = np.zeros((P, 4 * P), f32)
    consts[:, :P] = np.eye(P)
    consts[:, P:2 * P] = np.arange(P)
    consts[:, 2 * P:3 * P] = 1.0
    consts[:, 3 * P:4 * P] = np.where(np.arange(P)[:, None] > np.arange(P)[None], MASKED, 0.0)

    gates = np.concatenate([a["ml_w_ig"][0], a["ml_w_fg"][0]], axis=1)
    arrays = {
        "stream": stream.reshape(n_tiles // 2, P, 2 * TILE),
        "cols": cols,
        "consts": consts,
        "c": channels(np.concatenate([a["c_prompt"], a["c_sample"]])),
        "x": channels(np.concatenate([xpr[0], xsm[:, 0]])),
        "lru_h": channels(a["state_lru_h"][0]),
        "lru_conv": np.ascontiguousarray(a["state_lru_conv"][0].reshape(B, 3, NC, P).transpose(3, 2, 1, 0)),
        "ml_conv": np.ascontiguousarray(a["state_mlstm_conv"][0].reshape(B, 3, KM, P).transpose(3, 2, 1, 0)),
        "ml_n": channels(a["state_mlstm_n"][0].reshape(B, MI)),
        "gates": np.ascontiguousarray(gates.reshape(3 * KM, P, 2 * H).transpose(1, 0, 2)),
        "C": np.ascontiguousarray(a["state_mlstm_C"][0].reshape(B * H, MI // H // P, P, MI // H)
                                  .transpose(0, 2, 1, 3)).reshape(B * H, P, -1),
    }
    outs = {
        "y": (P, NC, T + B), "lru_h_o": (P, NC, B + 1), "lru_conv_p": (P, NC, 3), "lru_conv_s": (P, NC, 3, B),
        "ml_conv_p": (P, KM, 3), "ml_conv_s": (P, KM, 3, B), "n_p": (P, KM), "n_s": (P, KM, B), "m": (H, B + 1),
        "C_p": (KM, P, MI // H), "C_s": (B * H, P, MI),
    }
    nc = bacc.Bacc("TRN2", target_bir_lowering=False, num_devices=1, dynamic_dma_scratch_size=4096)
    args = [nc.dram_tensor(f"in_{k}", v.shape, F32, kind="ExternalInput").ap() for k, v in arrays.items()]
    args += [nc.dram_tensor(f"out_{k}", s, F32, kind="ExternalOutput").ap() for k, s in outs.items()]
    decoder_step(nc, *args)
    r = run(nc, [{f"in_{k}": v for k, v in arrays.items()}], core_ids=[0]).results[0]
    r = {k: r[f"out_{k}"] for k in outs}

    def rows(v):
        return np.ascontiguousarray(v.transpose(2, 1, 0)).reshape(v.shape[2], -1)

    def conv(v):
        return np.ascontiguousarray(v.transpose(3, 2, 1, 0)).reshape(v.shape[3], 3, -1)

    y = rows(r["y"])
    hs = rows(r["lru_h_o"])
    mh = MI // H
    C_s = r["C_s"].reshape(B, H, P, mh // P, mh).transpose(0, 1, 3, 2, 4).reshape(B, H, mh, mh)
    return (y[None, :T], y[T:, None],
            hs[None, :1], conv(r["lru_conv_p"][..., None])[None],
            r["C_p"].reshape(1, 1, H, mh, mh), rows(r["n_p"][..., None]).reshape(1, 1, H, mh),
            np.ascontiguousarray(r["m"][:, :1].T)[None], conv(r["ml_conv_p"][..., None])[None],
            hs[None, 1:], conv(r["lru_conv_s"])[None],
            np.ascontiguousarray(C_s)[None], rows(r["n_s"]).reshape(1, B, H, mh),
            np.ascontiguousarray(r["m"][:, 1:].T)[None], conv(r["ml_conv_s"])[None])
```

```python
from contextlib import ExitStack

import concourse.bass as bass
from concourse import mybir

ALU = mybir.AluOpType
ACT = mybir.ActivationFunctionType
F32 = mybir.dt.float32
F32R = mybir.dt.float32r
U32 = mybir.dt.uint32
AX_X = mybir.AxisListType.X

P = 128
TILE = 1024
SLOTS = 8
HALVES = 4
PAIRS = SLOTS // 2
BANK = 512
LRU_C = 8.0
EPS = 1e-6
MASKED = -1e30
LOWEST = -3e38
N_LOG1P = 9
MIXED = (72, 120)


def column_layout(D, D_RNN, M_INNER):
    at, out = 0, {}
    kd, kr, km = D // P, D_RNN // P, M_INNER // P
    for name, n in [("norm_mix0", kd), ("norm_mix1", kd), ("norm_ffn0", kd), ("norm_ffn1", kd), ("norm_f", kd),
                    ("b_ada0", 6 * kd), ("b_ada1", 6 * kd), ("lru_conv_w", 4 * kr), ("lru_conv_b", kr),
                    ("lru_b_a", kr), ("lru_b_i", kr), ("lru_lambda", kr), ("ml_conv_w", 4 * km),
                    ("ml_conv_b", km), ("ml_skip", km), ("ml_ln_g", km), ("ml_b_ig", 1), ("ml_b_fg", 1),
                    ("ml_m0", 8)]:
        out[name] = (at, n)
        at += n
    return out, at


def tile_plan(D, D_RNN, M_INNER, DEPTH, N_KEYS):
    kd, kr, km = D // P, D_RNN // P, M_INNER // P
    at, first = 0, {}
    for name, n in [("ada0", 2 * kd), ("lru_in", 2 * kr + 4 * kd), ("lru_gates", 2), ("lru_out", kd),
                    ("wq0", 16), ("keys0", 2), ("u0", MIXED[0]), ("u0_ada1", 2 * 6 * kd),
                    ("u0_end", N_KEYS - MIXED[1]), ("v0", N_KEYS), ("ml_x", km), ("ml_qkv", 6), ("ml_z", km), ("ml_out", 2 * kd),
                    ("wq1", 16), ("keys1", 2), ("u1", N_KEYS), ("v1", N_KEYS)]:
        first[name] = at
        at += n
    return first, at


def half_plan(D, D_RNN, M_INNER, N_KEYS):
    kd, kr, km = D // P, D_RNN // P, M_INNER // P
    at, first = 0, {}
    for name, n in [("ada0", 2 * kd), ("lru_in", 2 * kr + 4 * kd), ("wq0", 16), ("u0", MIXED[0]),
                    ("u0_ada1", 2 * 6 * kd), ("u0_end", N_KEYS - MIXED[1]), ("v0", N_KEYS), ("ml_x", km),
                    ("ml_z", km), ("wq1", 16), ("u1", N_KEYS), ("v1", N_KEYS)]:
        first[name] = at
        at += 2 * n
        assert at % 16 == 0
    return first


def decoder_step(nc, stream, cols_d, consts_d, c_d, x_d, lru_h_d, lru_conv_d, ml_conv_d, ml_n_d, gates_d, C_d,
                 y_o, lru_h_o, lru_conv_p_o, lru_conv_s_o, ml_conv_p_o, ml_conv_s_o, n_p_o, n_s_o, m_o,
                 C_p_o, C_s_o):
    NC, TOK = x_d.shape[1], x_d.shape[2]
    NSMP = lru_conv_d.shape[3]
    NPR = TOK - NSMP
    KM = ml_conv_d.shape[1]
    D, M_INNER = NC * P, KM * P
    HEADS = 4
    HC = KM // HEADS
    MHD = M_INNER // HEADS
    NSEQ = NSMP + 1
    KEYS = P
    PH, TOPK = 8, 16
    PICKS = PH * TOPK
    COL, NCOLS = column_layout(D, D, M_INNER)
    FIRST, NTILES = tile_plan(D, D, M_INNER, 2, KEYS)
    HALF = half_plan(D, D, M_INNER, KEYS)
    BLOCKS = [(0, 128), (128, 128), (256, NSMP)]
    NB = len(BLOCKS)
    assert D == TILE and NPR == 256 and NSMP == 8 and KM == 16

    with ExitStack() as ctx:
        def sb(name, shape, dt=F32):
            return ctx.enter_context(nc.sbuf_tensor(name, shape, dt))

        def sem(name):
            return ctx.enter_context(nc.semaphore(name))

        ring = sb("ring", [P, SLOTS, TILE])
        x = sb("x", [P, NC, TOK])
        h_hi, h_lo = sb("h_hi", [P, NC, TOK], F32R), sb("h_lo", [P, NC, TOK], F32R)
        mod = [sb("mod0", [P, 6 * NC, NSEQ])]
        with nc.sbuf_tensor("mod1", [P, 6 * NC, NSEQ], F32) as mod1:
            mod.append(mod1)
        c_parts = sb("c_parts", [P, NC, 2 * NSEQ], F32R)
        sb("rest_of_mod1", [P, 4 * NC, NSEQ])
        add_parts = sb("add_parts", [2 * NSEQ, NSEQ])
        cols = sb("cols", [P, NCOLS])
        consts = sb("consts", [P, 3 * P + P])
        ident, iota, ones = (consts[:, i * P:(i + 1) * P] for i in range(3))
        causal = consts[:, 3 * P:4 * P]
        lam8 = sb("lam8", [P, NC])
        BIG = sb("BIG", [P, KEYS * TOK])
        with nc.sbuf_tensor("SCR", [P, 6144], F32) as SCR:
            pass
        g_parts = sb("g_parts", [P, 2, 2, TOK], F32R)
        sb("between", [P, 2048 - 4 * TOK])
        w_parts = sb("w_parts", [P, 2, HALVES, BANK], F32R)
        w_hi, w_lo = w_parts[:, 0], w_parts[:, 1]
        g_hi, g_lo = g_parts[:, 0], g_parts[:, 1]
        ps = ctx.enter_context(nc.psum_tensor("ps", [P, 8, BANK], F32))

        def big(at, *shape):
            n = 1
            for s in shape:
                n *= s
            assert at + n <= KEYS * TOK
            v = BIG[:, at:at + n]
            names = "abcd"[:len(shape)]
            if len(shape) == 1:
                return v
            return v.rearrange(f"p ({' '.join(names)}) -> p {' '.join(names)}", **dict(zip(names[1:], shape[1:])))

        def scr(at, *shape):
            n = 1
            for s in shape:
                n *= s
            assert at + n <= 6144
            v = SCR[:, at:at + n]
            names = "abcd"[:len(shape)]
            if len(shape) == 1:
                return v
            return v.rearrange(f"p ({' '.join(names)}) -> p {' '.join(names)}", **dict(zip(names[1:], shape[1:])))

        def col(name, i=0, n=1):
            return cols[:, COL[name][0] + i:COL[name][0] + i + n]

        NT = NC * TOK
        HALVES_OF_NC = (slice(0, NC // 2), slice(NC // 2, NC))
        rstd = scr(0, TOK)
        scale = scr(512, NC, NSEQ)
        h_raw = [big(at, NC, TOK) for at in (22000, 22000, 22000, 0, 22000)]
        c_sb = big(20000, NC, NSEQ)
        ada_rows = [(big(20480, BANK), big(20480 + BANK, BANK)), (scr(1152, BANK), big(KEYS * TOK - BANK, BANK))]
        xp = big(0, NC, 3 + NPR)
        xs = big(NC * (3 + NPR), NC, 4, NSMP)
        LB = NC * (3 + NPR) + NC * 4 * NSMP
        ybr, xr, ra, ig, la, bx = (big(LB + i * NT, NC, TOK) for i in range(6))
        sq = ra
        h0 = big(LB + 6 * NT, NC, NSMP)
        stmp = big(LB + 6 * NT + NC * NSMP, NC, NSMP)
        MT = KM * TOK
        xm = big(0, KM, 3 + NPR)
        xms = big(KM * (3 + NPR), KM, 4, NSMP)
        MB = KM * (3 + NPR) + KM * 4 * NSMP
        xc, qT, kT, vT = (big(MB + i * MT, KM, TOK) for i in range(4))
        hT = vT
        z = big(0, KM, TOK)
        VB = MB + 4 * MT
        vt, kt = (big(VB + i * 2 * M_INNER, 2, M_INNER) for i in range(2))
        KT2 = MB + 2 * MT + HC * MHD
        Cbuf = [big(MB + 2 * MT, HC, MHD)] + [big(VB + i * HC * MHD, HC, MHD) for i in range(4)]
        CBUFS = len(Cbuf)
        Cst = big(0, 8, MHD)
        RB = VB + 4 * M_INNER
        vs = Cq = big(RB, M_INNER)
        GB = RB + M_INNER
        gates = big(GB, 3 * KM, 2 * HEADS)
        irow = big(GB + 384, TOK)
        frow = big(GB + 384 + TOK, TOK)
        Grow = big(GB + 384 + 2 * TOK, TOK)
        mrow = big(GB + 384 + 3 * TOK, TOK)
        nst = big(GB + 384 + 4 * TOK, KM, NSMP)
        SB0 = GB + 384 + 4 * TOK + KM * NSMP
        kw = big(SB0, KM, NSMP)
        bc = big(SB0 + 128, HEADS, 3, NSMP)
        gcol = big(SB0 + 224, 8)
        srow = big(SB0 + 232, 3, NSMP)
        sden = big(SB0 + 256, HEADS, NSMP)
        npr = big(SB0 + 288, KM)
        qn = big(GB, KM, NSMP)
        qz = big(GB + 384, KM, NSMP * NSMP)
        em = big(0, HEADS, NPR)
        Wt = scr(0, HEADS, 384)
        Sw = scr(1536, HEADS, 384)
        vk = [scr(i * 1024, HC // 2, MHD) for i in range(2)]
        hsq = scr(2048, KM, NPR)
        hstd = big(KT2, HEADS, NPR)
        hsq_s = big(KT2 + HEADS * NPR, KM, NSMP)
        mu_s = big(KT2 + HEADS * NPR + KM * NSMP, HEADS, NSMP)
        std_s = big(KT2 + HEADS * NPR + KM * NSMP + HEADS * NSMP, HEADS, NSMP)
        exp_f, zero, Frow, t_a, t_b, t_c = (scr(i * TOK, TOK) for i in range(6))
        G = big(0, KEYS, TOK)
        TB = KEYS * TOK - 16 * TOK - NB * 2048 - 5768
        pq = big(TB, 16, TOK)
        S = big(TB + 16 * TOK, NB, 16, KEYS)
        TC = TB + 16 * TOK + NB * 2048
        cand = big(TC, PH, TOPK * TOPK)
        eq = big(TC + 2048, PICKS, TOPK)
        vals = big(TC + 4096, 16, TOPK)
        idxf = big(TC + 4352, 16, TOPK)
        top = big(TC + 4608, PH, TOPK)
        abf = big(TC + 4736, 2, PICKS)
        idx = big(TC + 4992, 16, TOPK).bitcast(U32)
        pos = big(TC + 5248, PH, TOPK).bitcast(U32)
        ab = big(TC + 5376, 2, PICKS).bitcast(U32)
        ssum = scr(1944, NB, PH)
        EXP_ROWS, FREE_ROW = (40, 72, (TB + 16 * TOK + 2 * 2048) // TOK // 8 * 8), TC // TOK // 8 * 8
        picks = scr(0, NB, 3, PICKS)
        pickT = scr(1152, 3, TOK)
        OH = 4
        oh_j = [scr(2048 + i * 1024, 4, KEYS) for i in range(OH)]
        oh_i = [scr(2048 + i * 1024 + 512, 4, KEYS) for i in range(OH)]

        pair_in = [sem(f"pair_in{i}") for i in range(PAIRS)]
        pairs_used = sem("pairs_used")
        inputs_in = sem("inputs_in")
        ml_inputs_in = sem("ml_inputs_in")
        dve_seq = sem("dve_seq")
        ada_done = sem("ada_done")
        mod_ready = sem("mod_ready")
        squares_done = sem("squares_done")
        ssq_done = sem("ssq_done")
        ms_ready = sem("ms_ready")
        rms_ready = sem("rms_ready")
        h_ready = sem("h_ready")
        out_done = sem("out_done")
        x_ready = sem("x_ready")
        cond_in = sem("cond_in")
        c_hi_ready = sem("c_hi_ready")
        c_parts_ready = sem("c_parts_ready")
        ada_copied = sem("ada_copied")
        lin_x = sem("lin_x")
        lin_y = sem("lin_y")
        lam_exp = sem("lam_exp")
        xr_ready = sem("xr_ready")
        lgate_done = sem("lgate_done")
        lgate_act = sem("lgate_act")
        loga_ready = sem("loga_ready")
        a_ready = sem("a_ready")
        tt_ready = sem("tt_ready")
        sqrt_ready = sem("sqrt_ready")
        hs_ready = sem("hs_ready")
        ly_ready = sem("ly_ready")
        stores = sem("stores")
        mx_copied = sem("mx_copied")
        conv_ready = sem("conv_ready")
        xc_ready = sem("xc_ready")
        qkv_done = sem("qkv_done")
        qkv_act = sem("qkv_act")
        vk_done = sem("vk_done")
        vk_copied = sem("vk_copied")
        gate_done = sem("gate_done")
        gate_rows = sem("gate_rows")
        gate_raw = sem("gate_raw")
        gate_exp = sem("gate_exp")
        rows_ready = sem("rows_ready")
        bcast_done = sem("bcast_done")
        srow_exp = sem("srow_exp")
        gcol_done = sem("gcol_done")
        st_done = sem("st_done")
        wexp_in = sem("wexp_in")
        w_ready = sem("w_ready")
        em_ready = sem("em_ready")
        sw_ready = sem("sw_ready")
        den_done = sem("den_done")
        num_done = sem("num_done")
        num_read = sem("num_read")
        kw_ready = sem("kw_ready")
        cp_done = sem("cp_done")
        cp_copied = sem("cp_copied")
        cp_stored = [sem(f"cp_stored{i}") for i in range(8)]
        sbc_done = sem("sbc_done")
        sqn_ready = sem("sqn_ready")
        sden_done = sem("sden_done")
        C_in = [sem(f"C_in{i}") for i in range(CBUFS)]
        C_out = [sem(f"C_out{i}") for i in range(CBUFS)]
        vb_done = sem("vb_done")
        vb_used = sem("vb_used")
        C_new = sem("C_new")
        C_read = sem("C_read")
        qz_ready = sem("qz_ready")
        skip_ready = sem("skip_ready")
        Cq_copied = sem("Cq_copied")
        Cq_turned = sem("Cq_turned")
        hT_ready = sem("hT_ready")
        mu_done = sem("mu_done")
        hc_ready = sem("hc_ready")
        hsq_ready = sem("hsq_ready")
        var_done = sem("var_done")
        hvar_ready = sem("hvar_ready")
        hstd_ready = sem("hstd_ready")
        z_ready = sem("z_ready")
        mly_ready = sem("mly_ready")
        pq_ready = [sem(f"pq_ready{l}") for l in range(2)]
        sc_done = [sem(f"sc_done{l}") for l in range(2)]
        sc_ready = [sem(f"sc_ready{l}") for l in range(2)]
        g_ready = [sem(f"g_ready{l}") for l in range(2)]
        top_ready = [sem(f"top_ready{l}") for l in range(2)]
        topexp_ready = [sem(f"topexp_ready{l}") for l in range(2)]
        picks_ready = [sem(f"picks_ready{l}") for l in range(2)]
        pickT_done = [sem(f"pickT_done{l}") for l in range(2)]
        pickT_ready = [sem(f"pickT_ready{l}") for l in range(2)]
        oh_i_ready = [sem(f"oh_i_ready{l}") for l in range(2)]
        oh_j_abs = [sem(f"oh_j_abs{l}") for l in range(2)]
        oh_j_ready = [sem(f"oh_j_ready{l}") for l in range(2)]
        route_done = [sem(f"route_done{l}") for l in range(2)]
        routed = [sem(f"routed{l}") for l in range(2)]
        y_ready = sem("y_ready")
        hi_ready = sem("hi_ready")
        lo_ready = [sem("lo_even_ready"), sem("lo_odd_ready")]
        half_used = sem("half_used")
        g_hi_ready = [sem(f"g_hi_ready{l}") for l in range(2)]
        g_lo_ready = [sem(f"g_lo_ready{l}") for l in range(2)]
        h_made = sem("h_made")
        h_hi_ready = sem("h_hi_ready")
        work_free = [sem(f"work_free{l}") for l in range(2)]
        def mixed(l, row):
            return l == 0 and MIXED[0] <= row < MIXED[1]
        def u_tile_at(l, row):
            if mixed(l, row):
                k = 2 * (row - MIXED[0])
                return FIRST["u0_ada1"] + k, HALF["u0_ada1"] + 2 * k
            name, k = ("u0_end", row - MIXED[1]) if l == 0 and row >= MIXED[1] else (f"u{l}", row)
            return FIRST[name] + k, HALF[name] + 2 * k
        def half_of(n, half):
            return ring[:, n % SLOTS, half * BANK:(half + 1) * BANK]
        def C_uses(i):
            return len(range(i, NSMP * HEADS, CBUFS))
        AT_MU, AT_CENTRE, AT_SQUARE, AT_VAR, AT_MS, AT_SQRT, AT_SCALE, AT_SKIP, AT_Z = \
            17, 18, 19, 21, 22, 23, 24, 26, 28
        POOL_ROWS = MIXED[0]
        lam_abs = sem("lam_abs")
        ml_conv_stored = sem("ml_conv_stored")
        npr_ready = sem("npr_ready")

        block = ctx.enter_context(nc.Block())
        GROUPS = TOK // 4
        N_STORES = 10

        @block.sync
        def _(sp):
            def pair(n, slot):
                sp.dma_start(ring[:, 2 * slot:2 * slot + 2, :].rearrange("p a b -> p (a b)"),
                             stream[n]).then_inc(pair_in[slot], 16)

            for n in range(PAIRS):
                pair(n, n)
            rounds = NTILES // 2 // PAIRS
            with sp.Fori(1, rounds) as r:
                for s in range(PAIRS):
                    sp.wait_ge(pairs_used, r * PAIRS + (s - PAIRS + 1))
                    pair(r * PAIRS + s, s)
            for n in range(rounds * PAIRS, NTILES // 2):
                sp.wait_ge(pairs_used, n - PAIRS + 1)
                pair(n, n % PAIRS)

        @block.tensor
        def _(pe):
            def need(n0, k, r=0):
                pe.wait_ge(pair_in[(n0 + k) // 2 % PAIRS], (r + (n0 + k) // SLOTS + 1) * 16)

            def w_at(n0, k, c):
                return ring[:, (n0 + k) % SLOTS, c * P:(c + 1) * P]

            def begins(ins, n0, k):
                if (n0 + k) % 2 == 0:
                    ins.then_inc(pairs_used, 1)

            def mm(out, lhsT, rhs, start=True, stop=True, shared=False):
                return nc.tensor.matmul(out, lhsT, rhs, start=start, stop=stop, skip_group_check=shared)

            def split_chunk(out, n, j0, rounds=0, start=True, stop=True, v_row=None, norm=None):
                for half in range(2):
                    j = j0 + half
                    pe.wait_ge(lo_ready[half], rounds * SLOTS + (j // 2 + 1))
                    for i in range(4):
                        c = 4 * half + i
                        w = (w_hi[:, j % HALVES, i * P:(i + 1) * P], w_lo[:, j % HALVES, i * P:(i + 1) * P])
                        if v_row is None:
                            x_hi, x_lo = h_hi[:, c, :], h_lo[:, c, :]
                            first, end = start and c == 0, stop and c == NC - 1
                        else:
                            x_hi, x_lo = g_hi[:, v_row % 2, :], g_lo[:, v_row % 2, :]
                            out, first, end = ps[:, c, 0:TOK], start, stop
                        if norm is not None:
                            pe.wait_ge(h_ready, norm * NC + c + 1)
                        last = mm(out, w[0], x_hi, first, False)
                        if c == 0:
                            begins(last, n, 0)
                        mm(out, w[0], x_lo, False, False)
                        last = mm(out, w[1], x_hi, False, end)
                    last.then_inc(half_used, 1)

            def norm_sum(n):
                for c in range(NC):
                    pe.wait_ge(squares_done, n * NC + c + 1)
                    last = mm(ps[:, 0, 0:TOK], ones, sq[:, c, :], c == 0, c == NC - 1)
                last.then_inc(ssq_done, 1)

            def residual_out(name, rhs, KC, chunk_ready=None):
                per = KC // NC
                for m in range(NC):
                    for t in range(per):
                        k = m * per + t
                        need(FIRST[name], k)
                        for c in range(NC):
                            if m == 0 and chunk_ready:
                                pe.wait_ge(chunk_ready, c + 1)
                            last = mm(ps[:, m, 0:TOK], w_at(FIRST[name], k, c), rhs[:, t * NC + c, :],
                                      t == 0 and c == 0, t == per - 1 and c == NC - 1)
                            if c == 0:
                                begins(last, FIRST[name], k)
                last.then_inc(out_done, 1)

            def ada_tile(n, c, j0, rounds=0):
                for half in range(2):
                    j = j0 + half
                    pe.wait_ge(lo_ready[half], rounds * SLOTS + (j // 2 + 1))
                    for i, w in enumerate((w_hi, w_lo)):
                        last = mm(ps[0:2 * NSEQ, 4 + half, :], c_parts[:, c, :], w[:, j % HALVES, :],
                                  c == 0 and i == 0, c == NC - 1 and i == 1)
                        if half == 0 and i == 0 and n > 0:
                            begins(last, n, 0)
                    last.then_inc(half_used, 1)

            def ada_part(l, copied, at):
                for half in range(2):
                    pe.wait_ge(ada_copied, copied + (half + 1))
                    for e in range(4):
                        last = mm(ps[:, 7, bass.ds(at + (4 * half + e) * NSEQ, NSEQ)],
                                  ada_rows[l][half][0:2 * NSEQ, e * P:(e + 1) * P], add_parts[:])
                return last

            pe.wait_ge(c_parts_ready, 1)
            for t in range(2 * NC):
                if t == NC:
                    ada_part(0, 0, 0)
                ada_tile(t, t % NC, HALF["ada0"] + 2 * t)
            ada_part(0, 2, NC * NSEQ).then_inc(ada_done, 1)

            norm_sum(0)
            n0 = FIRST["lru_in"]
            for k in range(2 * NC):
                if k >= 4:
                    pe.wait_ge((lin_x, lin_y)[k % 2], (k - 4) // 2 + 1)
                split_chunk(ps[:, k % 4, 0:TOK], n0 + 3 * k, HALF["lru_in"] + 6 * k,
                            norm=0 if k == 0 else None)
                if k > 0 and 2 * k % NC == 0:
                    part = 1 + 2 * k // NC
                    ada_part(0, 2 * part, part * NC * NSEQ)
                for i in range(2):
                    t = 3 * k + 1 + i
                    ada_tile(n0 + t, (2 * k + i) % NC, HALF["lru_in"] + 2 * t)
            ada_part(0, 2 * 5, 5 * NC * NSEQ).then_inc(ada_done, 1)
            n0 = FIRST["lru_gates"]
            need(n0, 0)
            pe.wait_ge(xr_ready, NC)
            pe.wait_ge(lin_y, NC)
            for g in range(2):
                for c in range(NC):
                    n = g * NC + c
                    if n >= 6:
                        pe.wait_ge(lgate_act, n - 5)
                    if n == 0:
                        begins(mm(ps[:, 0, NPR:TOK], w_at(n0, 0, 0), xr[:, 0, NPR:TOK]), n0, 0)
                        last = mm(ps[:, 0, 0:NPR], w_at(n0, 0, 0), xr[:, 0, 0:NPR])
                    else:
                        last = mm(ps[:, n % 6, 0:TOK], w_at(n0, g, c), xr[:, c, :])
                    last.then_inc(lgate_done, 1)
            pe.wait_ge(mod_ready, 2)
            residual_out("lru_out", ybr, NC, ly_ready)

            def peer(l):
                norm_sum(2 * l + 1)
                n0 = FIRST[f"wq{l}"]
                for k in range(2 * PH):
                    if k >= 4:
                        pe.wait_ge(pq_ready[l], k - 3)
                    split_chunk(ps[:, k % 4, 0:TOK], n0 + k, HALF[f"wq{l}"] + 2 * k,
                                norm=2 * l + 1 if k == 0 else None)
                n0 = FIRST[f"keys{l}"]
                need(n0, 0)
                pe.wait_ge(pq_ready[l], 2 * PH)
                n = 0
                for b, (t0, nb) in enumerate(BLOCKS):
                    for q in range(4):
                        if n >= 4:
                            pe.wait_ge(sc_ready[l], n - 3)
                        for i in range(4):
                            k = 4 * q + i
                            last = mm(ps[0:nb, 4 + n % 4, i * P:(i + 1) * P], pq[:, k, t0:t0 + nb],
                                      w_at(n0, k // 8, k % 8))
                            if n == 0 and i == 0:
                                begins(last, n0, 0)
                        last.then_inc(sc_done[l], 1)
                        n += 1

                def u_rows(r, first_row):
                    for k in range(SLOTS):
                        row = first_row + k
                        n, j = u_tile_at(l, row)
                        mix = mixed(l, row)
                        if l == 0 and row == MIXED[1] + 1:
                            ada_part(1, 2 * 11, 5 * NC * NSEQ).then_inc(ada_done, 1)
                        rounds = r * 2 if mix else r
                        if not (isinstance(r, int) and row + SLOTS * r < 4):
                            pe.wait_ge(g_ready[l], r * SLOTS + (row - 3))
                        split_chunk(ps[:, row % 4, 0:TOK], n, j, rounds)
                        if mix:
                            if k == 0 and not (isinstance(r, int) and r == 0):
                                ada_part(1, r * 2 + 10, (r - 1) * (NC * NSEQ))
                            ada_tile(n + 1, k, j + 2, rounds)
                pe.wait_ge(sc_ready[l], n)
                u_rows(0, 0)
                with pe.Fori(1, (MIXED[0] if l == 0 else KEYS) // SLOTS) as r:
                    u_rows(r, 0)
                if l == 0:
                    assert SLOTS == NC
                    u_rows(0, MIXED[0])
                    with pe.Fori(1, 6) as r:
                        u_rows(r, MIXED[0])
                    u_rows(0, MIXED[1])
                for b, (t0, nb) in enumerate(BLOCKS):
                    pe.wait_ge(picks_ready[l], b + 1)
                    for i in range(3):
                        last = nc.tensor.transpose(ps[:, 4 + b, i * P:i * P + nb], picks[0:nb, b, i, :],
                                                   ident[0:nb, 0:nb])
                    last.then_inc(pickT_done[l], 1)

                def route(r, s):
                    pe.wait_ge(oh_i_ready[l], r * OH + (s + 1))
                    pe.wait_ge(oh_j_ready[l], r * OH + (s + 1))
                    if not (isinstance(r, int) and r == 0):
                        pe.wait_ge(routed[l], r * OH + (s + 1 - OH))
                    for i in range(4):
                        last = mm(ps[:, s, i * P:(i + 1) * P], oh_j[s][:, i, :], oh_i[s][:, i, :])
                    last.then_inc(route_done[l], 1)
                pe.wait_ge(g_ready[l], KEYS)
                for s in range(OH):
                    route(0, s)
                with pe.Fori(1, GROUPS // OH) as r:
                    for s in range(OH):
                        route(r, s)
                for s in range(GROUPS % OH):
                    route(GROUPS // OH, s)
                n0 = FIRST[f"v{l}"]
                pe.wait_ge(routed[l], GROUPS)
                pe.wait_ge(mod_ready, 3)

                def v_rows(r, first=False, end=False):
                    for k in range(SLOTS):
                        pe.wait_ge(g_lo_ready[l], r * SLOTS + (k + 1))
                        split_chunk(None, n0 + k, HALF[f"v{l}"] + 2 * k, r, first and k == 0, end and k == SLOTS - 1, k)
                v_rows(0, first=True)
                with pe.Fori(1, KEYS // SLOTS - 1) as r:
                    v_rows(r)
                v_rows(KEYS // SLOTS - 1, end=True)

            peer(0)

            norm_sum(2)
            n0 = FIRST["ml_x"]
            for k in range(KM):
                if k >= 4:
                    pe.wait_ge(mx_copied, k - 3)
                split_chunk(ps[:, k % 4, 0:TOK], n0 + k, HALF["ml_x"] + 2 * k, norm=2 if k == 0 else None)
            n0 = FIRST["ml_qkv"]
            pe.wait_ge(ml_inputs_in, 16 * 3)
            n = nt = 0

            def tokens(j, c, lo, hi):
                if j < 2:
                    return xc[:, c, lo:hi]
                return xms[:, c, 3, :] if lo == NPR else xm[:, c, 3 + lo:3 + hi]
            for j in range(3):
                need(n0, 2 * j)
                for c in range(KM):
                    if n >= 4:
                        pe.wait_ge(qkv_act, n - 3)
                    if j == 0:
                        pe.wait_ge(xc_ready, c + 1)
                    w = w_at(n0, 2 * j + c // NC, c % NC)
                    if j == 2 or c == 0:
                        first = mm(ps[:, 4 + n % 4, NPR:TOK], w, tokens(j, c, NPR, TOK))
                        if c == 0 and j < 2:
                            begins(first, n0, 2 * j)
                        last = mm(ps[:, 4 + n % 4, 0:NPR], w, tokens(j, c, 0, NPR))
                    else:
                        last = mm(ps[:, 4 + n % 4, 0:TOK], w, xc[:, c, :])
                    last.then_inc(qkv_done, 1)
                    n += 1
            pe.wait_ge(qkv_act, 3 * KM)
            for j, src in enumerate((qT, kT, vT)):
                for c in range(KM):
                    last = mm(ps[0:2 * HEADS, 4, 0:TOK], gates[:, j * KM + c, :], src[:, c, :],
                              j == 0 and c == 0, j == 2 and c == KM - 1)
            last.then_inc(gate_done, 1)
            for j in (1, 2):
                for t0, nb in BLOCKS[:j + 1]:
                    for q in range(KM // 4):
                        if nt >= 4:
                            pe.wait_ge(vk_copied, nt - 3)
                        for i in range(4):
                            c = 4 * q + i
                            last = mm(ps[0:nb, nt % 4, i * P:(i + 1) * P], tokens(j, c, t0, t0 + nb),
                                      w_at(n0, 2 * j + c // NC, c % NC))
                            if j == 2 and t0 == 0 and c == 0:
                                begins(last, n0, 2 * j)
                        last.then_inc(vk_done, 1)
                        nt += 1
                        if nt == 1:
                            pe.wait_ge(gate_rows, 1)
                            mm(ps[0:HEADS, 5, 0:TOK], ident[0:2 * HEADS, HEADS:2 * HEADS], Frow[0:2 * HEADS])\
                                .then_inc(gate_done, 1)
            pe.wait_ge(vk_copied, nt)
            for hd in range(HEADS):
                for b in range(2):
                    o = ps[:, hd, 0:NPR] if b == 0 else ps[:, hd, NPR:NPR + P]
                    for c in range(HC):
                        last = mm(o, kT[:, hd * HC + c, b * P:(b + 1) * P], qT[:, hd * HC + c, b * P:NPR],
                                  c == 0, c == HC - 1)
            last.then_inc(st_done, 1)
            pe.wait_ge(rows_ready, 1)
            for hd in range(HEADS):
                pick = ident[0:HEADS, hd:hd + 1].to_broadcast([HEADS, P])
                half = slice(hd % 2 * NPR, (hd % 2 + 1) * NPR)
                mm(ps[:, 4 + hd // 2, half], pick, frow[0:HEADS, 0:NPR])
                last = mm(ps[:, 6 + hd // 2, half], pick, mrow[0:HEADS, 0:NPR])
            last.then_inc(bcast_done, 1)
            pe.wait_ge(em_ready, 1)
            for b in range(2):
                last = nc.tensor.transpose(ps[:, 6, b * HEADS:(b + 1) * HEADS], Grow[0:HEADS, b * P:(b + 1) * P],
                                           ident[0:HEADS, 0:HEADS])
            last.then_inc(gcol_done, 1)
            pe.wait_ge(srow_exp, 1)
            for hd in range(HEADS):
                last = mm(ps[:, 7, hd * 3 * NSMP:(hd + 1) * 3 * NSMP],
                          ident[0:HEADS, hd:hd + 1].to_broadcast([HEADS, P]),
                          srow[0:HEADS].rearrange("p a b -> p (a b)"))
            last.then_inc(sbc_done, 1)
            pe.wait_ge(sw_ready, 1)
            for hd in range(HEADS):
                o = ps[:, 4 + hd // 2, hd % 2 * NPR:(hd % 2 + 1) * NPR]
                mm(o, ones, Sw[:, hd, 0:NPR])
                last = mm(o[:, P:NPR], ones, Sw[:, hd, NPR:NPR + P], False, True, True)
            last.then_inc(den_done, 1)
            for hd in range(HEADS):
                if hd >= 2:
                    pe.wait_ge(num_read, hd - 1)
                for e in range(HC):
                    o = ps[:, hd % 2 * 2 + e // 2, e % 2 * NPR:(e % 2 + 1) * NPR]
                    e0 = (hd * HC + e) * P
                    mm(o, vt[:, 0, e0:e0 + P], Sw[:, hd, 0:NPR])
                    last = mm(o[:, P:NPR], vt[:, 1, e0:e0 + P], Sw[:, hd, NPR:NPR + P], False, True, True)
                last.then_inc(num_done, 1)
            pe.wait_ge(sqn_ready, 1)
            for hd in range(HEADS):
                for c in range(HC):
                    last = mm(ps[:, 7, P + hd * NSMP:P + (hd + 1) * NSMP], ones, qn[:, hd * HC + c, :],
                              c == 0, c == HC - 1)
            last.then_inc(sden_done, 1)
            pe.wait_ge(kw_ready, 1)
            pe.wait_ge(num_read, HEADS)
            for n in range(KM):
                hd = n // HC
                if n >= 4:
                    pe.wait_ge(cp_copied, n - 3)
                for b in range(2):
                    mm(ps[:, 6, 16 + n:17 + n], kt[:, b, n * P:(n + 1) * P], ones[:, 0:1], b == 0, b == 1)
                for b in range(2):
                    last = mm(ps[:, n % 4, :], kt[:, b, n * P:(n + 1) * P],
                              vt[:, b, hd * MHD:(hd + 1) * MHD], b == 0, b == 1)
                last.then_inc(cp_done, 1)
            pe.wait_ge(cp_copied, KM)
            pe.wait_ge(qz_ready, 1)

            def read_C(m):
                b, hd = m // HEADS, m % HEADS
                pe.wait_ge(C_new, 2 * m + 2)
                for c in range(HC):
                    last = mm(ps[0:NSMP, 4 + hd, :], qz[:, hd * HC + c, b * NSMP:(b + 1) * NSMP],
                              Cbuf[m % CBUFS][:, c, :], b == 0 and c == 0, b == NSMP - 1 and c == HC - 1)
                last.then_inc(C_read, 1)

            def head_sums(i, src, ready):
                for hd in (2 * i, 2 * i + 1):
                    o = ps[:, 2 + i, hd % 2 * NPR:(hd % 2 + 1) * NPR]
                    for c in range(HC):
                        last = mm(o, ones, src[:, hd * HC + c, 0:NPR], c == 0, c == HC - 1)
                last.then_inc(ready, 1)
            n0 = FIRST["ml_z"]
            for m in range(NSMP * HEADS):
                b, hd = m // HEADS, m % HEADS
                if m >= 2:
                    pe.wait_ge(vb_used, 2 * m - 2)
                mm(ps[:, m % 2, :], ident[0:NSMP, b:b + 1].to_broadcast([NSMP, P]),
                   vs[0:NSMP, hd * MHD:(hd + 1) * MHD]).then_inc(vb_done, 1)
                if m >= 1:
                    read_C(m - 1)
                if m < KM:
                    if m >= 2:
                        pe.wait_ge(z_ready, m - 1)
                    split_chunk(ps[:, 2 + m % 2, 0:TOK], n0 + m, HALF["ml_z"] + 2 * m)
                for i in range(2):
                    if m == AT_MU + i:
                        pe.wait_ge(z_ready, KM)
                        head_sums(i, hT, mu_done)
                    if m == AT_VAR + i:
                        pe.wait_ge(hsq_ready, i + 1)
                        head_sums(i, hsq, var_done)
            read_C(NSMP * HEADS - 1)
            for hd in range(HEADS):
                pe.wait_ge(Cq_copied, hd + 1)
                for e in range(hd * HC, (hd + 1) * HC):
                    last = nc.tensor.transpose(ps[:, 0, e * NSMP:(e + 1) * NSMP], Cq[0:NSMP, e * P:(e + 1) * P],
                                               ident[0:NSMP, 0:NSMP])
            last.then_inc(Cq_turned, 1)
            pe.wait_ge(hT_ready, 1)
            mm(ps[:, 2, 0:KM * NSMP], ones, hT[:, :, NPR:TOK]).then_inc(mu_done, 1)
            pe.wait_ge(hsq_ready, 3)
            mm(ps[:, 3, 0:KM * NSMP], ones, hsq_s).then_inc(var_done, 1)
            pe.wait_ge(mly_ready, 1)
            residual_out("ml_out", hT, KM)
            peer(1)
            norm_sum(4)

        @block.scalar
        def _(act):
            def flat(v):
                return v.rearrange("p c t -> p (c t)")

            def func(to, of, f, **kw_):
                return nc.scalar.activation(to, of, f, **kw_)

            def high(n, j0, rounds=0):
                act.wait_ge(pair_in[n // 2 % PAIRS], (rounds + n // SLOTS + 1) * 16)
                for half in range(2):
                    j = j0 + half
                    if j >= HALVES or not isinstance(rounds, int):
                        act.wait_ge(half_used, rounds * (2 * SLOTS) + (j - HALVES + 1))
                    func(w_hi[:, j % HALVES, :], half_of(n, half), ACT.Copy).then_inc(hi_ready, 1)

            def tile_used(j0, rounds=0):
                act.wait_ge(half_used, rounds * (2 * SLOTS) + (j0 + 2))

            act.dma_start(c_sb, c_d).then_inc(cond_in, 16)
            for to, of in ((cols[:], cols_d), (consts[:], consts_d), (x[:], x_d), (h0, lru_h_d)):
                act.dma_start(to, of).then_inc(inputs_in, 16)
            act.dma_start(xs[:, :, 0:3, :].rearrange("p c j b -> p c (j b)"),
                          lru_conv_d.rearrange("p c j b -> p c (j b)")).then_inc(inputs_in, 16)
            act.wait_ge(cond_in, 16)
            func(c_parts[:, :, 0:NSEQ], c_sb, ACT.Copy).then_inc(c_hi_ready, 1)
            for t in range(NC):
                high(t, HALF["ada0"] + 2 * t)
            act.wait_ge(inputs_in, 16 * 5)

            def norm(n, stage=None):
                for c in range(NC):
                    if n > 0:
                        act.wait_ge(x_ready, (n - 1) * NC + c + 1)
                    func(sq[:, c, :], x[:, c, :], ACT.Square).then_inc(squares_done, 1)
                if stage:
                    for t in range(2):
                        high(FIRST[stage] + t, HALF[stage] + 2 * t)
                act.wait_ge(ms_ready, n + 1)
                func(rstd, rstd, ACT.Sqrt).then_inc(rms_ready, 1)
                if stage:
                    act.wait_ge(h_made, n * (NC + 1) + 1)
                    func(h_hi[:, :, NPR:TOK], h_raw[n][:, :, NPR:TOK], ACT.Copy).then_inc(h_hi_ready, 1)
                    for c in range(NC):
                        act.wait_ge(h_made, n * (NC + 1) + c + 2)
                        func(h_hi[:, c, 0:NPR], h_raw[n][:, c, 0:NPR], ACT.Identity,
                             bias=mod[n // 2][:, n % 2 * 3 * NC + c, 0:1]).then_inc(h_hi_ready, 1)

            def last_tap(out, prompt, samples, c, nch, bank, w, b):
                func(out[:, c, :], ps[:, bank, 0:TOK], ACT.Identity, scale=col(w, 3 * nch + c), bias=col(b, c))
                func(prompt[:, c, 3:3 + NPR], ps[:, bank, 0:NPR], ACT.Copy)
                return func(samples[:, c, 3, :], ps[:, bank, NPR:TOK], ACT.Copy)

            for t in range(NC, 2 * NC):
                high(t, HALF["ada0"] + 2 * t)
            func(lam8[:], col("lru_lambda", 0, NC), ACT.Abs).then_inc(lam_abs, 1)
            act.wait_ge(lam_abs, 1)
            func(lam8[:], lam8[:], ACT.Exp, scale=-1.0).then_inc(lam_exp, 1)
            norm(0, "lru_in")
            n0, j0 = FIRST["lru_in"], HALF["lru_in"]
            for t in range(6 * NC):
                if t + 2 < 6 * NC:
                    high(n0 + t + 2, j0 + 2 * t + 4)
                k = t // 3
                if t % 3 == 0:
                    tile_used(j0 + 2 * t)
                if t % 3 == 0 and k % 2 == 0:
                    last_tap(xr, xp, xs, k // 2, NC, k % 4, "lru_conv_w", "lru_conv_b").then_inc(lin_x, 1)
                if t % 3 == 0 and k % 2 == 1:
                    func(ybr[:, k // 2, :], ps[:, k % 4, 0:TOK], ACT.Gelu_apprx_tanh).then_inc(lin_y, 1)
            for g, (to, bias) in enumerate(((ra, "lru_b_a"), (ig, "lru_b_i"))):
                for c in range(NC):
                    n = g * NC + c
                    act.wait_ge(lgate_done, n + 1)
                    func(to[:, c, :], ps[:, n % 6, 0:TOK], ACT.Sigmoid, bias=col(bias, c)).then_inc(lgate_act, 1)
            act.wait_ge(loga_ready, 1)
            for hf in HALVES_OF_NC:
                func(flat(ra[:, hf, :]), flat(la[:, hf, :]), ACT.Exp).then_inc(a_ready, 1)
            for i, hf in enumerate(HALVES_OF_NC):
                act.wait_ge(a_ready, i + 1)
                func(flat(la[:, hf, :]), flat(la[:, hf, :]), ACT.Tanh, scale=-1.0).then_inc(a_ready, 1)
            for i, hf in enumerate(HALVES_OF_NC):
                act.wait_ge(tt_ready, i + 1)
                func(flat(la[:, hf, :]), flat(la[:, hf, :]), ACT.Sqrt).then_inc(sqrt_ready, 1)

            def peer(l):
                norm(2 * l + 1, f"wq{l}")
                if l == 1:
                    act.wait_ge(stores, 16 * 6)
                    for i in range(CBUFS):
                        act.wait_ge(C_out[i], 16 * C_uses(i))
                n0, j0 = FIRST[f"wq{l}"], HALF[f"wq{l}"]
                for k in range(2 * PH):
                    if k + 2 < 2 * PH:
                        high(n0 + k + 2, j0 + 2 * k + 4)
                    tile_used(j0 + 2 * k)
                    func(pq[:, k, :], ps[:, k % 4, 0:TOK], ACT.Copy).then_inc(pq_ready[l], 1)
                n = 0
                for b, (t0, nb) in enumerate(BLOCKS):
                    for q in range(4):
                        act.wait_ge(sc_done[l], n + 1)
                        func(flat(S[0:nb, b, 4 * q:4 * q + 4, :]), ps[0:nb, 4 + n % 4, :], ACT.Copy)\
                            .then_inc(sc_ready[l], 1)
                        n += 1

                if l == 0:
                    act.wait_ge(stores, 16 * 3)

                order, tile_of = [], {}
                for row in range(KEYS):
                    n, j = u_tile_at(l, row)
                    tile_of[row] = len(order)
                    order += [(n, j)] + [(n + 1, j + 2)] * mixed(l, row)

                def rows(r, first_row):
                    for row in range(first_row, first_row + SLOTS):
                        mix = mixed(l, row)
                        rounds = r * 2 if mix else r
                        for i in range(2 if mix else 1):
                            ahead = tile_of[row] + i + 2
                            if ahead < len(order):
                                high(*order[ahead], rounds)
                            if i == 0:
                                tile_used(u_tile_at(l, row)[1], rounds)
                                func(BIG[:, bass.ds(r * (SLOTS * TOK) + row * TOK, TOK)], ps[:, row % 4, 0:TOK],
                                     ACT.Gelu_apprx_tanh).then_inc(g_ready[l], 1)

                for i in range(2):
                    high(*order[i])
                at = 0
                for until in sorted({*EXP_ROWS, *MIXED, FREE_ROW, KEYS}):
                    ends = until in (*MIXED, KEYS)
                    if until - SLOTS * ends > at:
                        with act.Fori(0, (until - at) // SLOTS - ends) as r:
                            rows(r, at)
                    if ends:
                        rows(0, until - SLOTS)
                    at = until
                    if until in EXP_ROWS:
                        b = EXP_ROWS.index(until)
                        nb = BLOCKS[b][1]
                        act.wait_ge(top_ready[l], b + 1)
                        func(picks[0:nb, b, 2, :], picks[0:nb, b, 2, :], ACT.Exp).then_inc(topexp_ready[l], 1)
                    if until == FREE_ROW:
                        act.wait_ge(work_free[l], 1)

                def build(r, s):
                    if not (isinstance(r, int) and r == 0):
                        act.wait_ge(route_done[l], r * OH + (s + 1 - OH))
                    for i in range(4):
                        last = func(oh_j[s][:, i, :], iota, ACT.Abs, scale=-1.0,
                                    bias=pickT[:, 1, bass.ds(r * (4 * OH) + (4 * s + i), 1)])
                    last.then_inc(oh_j_abs[l], 1)
                    act.wait_ge(oh_j_abs[l], r * OH + (s + 1))
                    func(flat(oh_j[s]), flat(oh_j[s]), ACT.Relu, scale=-1.0, bias=1.0).then_inc(oh_j_ready[l], 1)
                act.wait_ge(pickT_ready[l], 1)
                for s in range(OH):
                    build(0, s)
                with act.Fori(1, GROUPS // OH) as r:
                    for s in range(OH):
                        build(r, s)
                for s in range(GROUPS % OH):
                    build(GROUPS // OH, s)

                act.wait_ge(route_done[l], GROUPS)
                act.wait_ge(routed[l], GROUPS)
                n0, j0 = FIRST[f"v{l}"], HALF[f"v{l}"]

                def v_rows(r):
                    for k in range(SLOTS):
                        high(n0 + k, j0 + 2 * k, r)
                        if not (isinstance(r, int) and k < 2):
                            act.wait_ge(half_used, r * (2 * SLOTS) + (j0 + 2 * k - 2))
                        func(g_hi[:, k % 2, :], BIG[:, bass.ds(r * (SLOTS * TOK) + k * TOK, TOK)], ACT.Copy)\
                            .then_inc(g_hi_ready[l], 1)
                v_rows(0)
                with act.Fori(1, KEYS // SLOTS) as r:
                    v_rows(r)

            peer(0)

            norm(2, "ml_x")
            act.wait_ge(ml_inputs_in, 16 * 3)
            n0, j0 = FIRST["ml_x"], HALF["ml_x"]
            for k in range(KM + 2):
                if k + 2 < KM:
                    high(n0 + k + 2, j0 + 2 * k + 4)
                if k < KM:
                    tile_used(j0 + 2 * k)
                    last_tap(xc, xm, xms, k, KM, k % 4, "ml_conv_w", "ml_conv_b").then_inc(mx_copied, 1)
                if k >= 2:
                    act.wait_ge(conv_ready, k - 1)
                    func(xc[:, k - 2, :], xc[:, k - 2, :], ACT.Silu).then_inc(xc_ready, 1)
            n = 0
            for j, to in enumerate((qT, kT, vT)):
                for c in range(KM):
                    act.wait_ge(qkv_done, n + 1)
                    func(to[:, c, :], ps[:, 4 + n % 4, 0:TOK], ACT.Copy,
                         scale=float(MHD) ** -0.5 if j == 1 else 1.0).then_inc(qkv_act, 1)
                    n += 1
            act.wait_ge(gate_raw, 1)
            func(exp_f[0:HEADS], frow[0:HEADS], ACT.Abs).then_inc(gate_exp, 1)
            act.wait_ge(gate_exp, 1)
            func(exp_f[0:HEADS], exp_f[0:HEADS], ACT.Exp, scale=-1.0).then_inc(gate_exp, 1)
            n = 0
            for to, factor, nblocks in ((kt, float(MHD) ** -0.5, 2), (vt, 1.0, 3)):
                for b in range(nblocks):
                    nb = BLOCKS[b][1]
                    for q in range(KM // 4):
                        act.wait_ge(vk_done, n + 1)
                        o = to[:, b, q * BANK:(q + 1) * BANK] if b < 2 else vs[0:nb, q * BANK:(q + 1) * BANK]
                        func(o, ps[0:nb, n % 4, :], ACT.Copy, scale=factor).then_inc(vk_copied, 1)
                        n += 1
            act.wait_ge(bcast_done, 1)
            act.wait_ge(ml_conv_stored, 32)
            for i in range(2):
                last = func(flat(em[:, 2 * i:2 * i + 2, :]), ps[:, 6 + i, :], ACT.Exp, scale=-1.0)
            last.then_inc(em_ready, 1)
            act.wait_ge(rows_ready, 1)
            func(flat(srow[0:HEADS]), flat(srow[0:HEADS]), ACT.Exp).then_inc(srow_exp, 1)
            act.wait_ge(wexp_in, 1)
            for hd in range(HEADS):
                for b in range(2):
                    w = Wt[:, hd, 0:NPR] if b == 0 else Wt[:, hd, NPR:NPR + P]
                    last = func(w, w, ACT.Exp, bias=gcol[:, b * HEADS + hd:b * HEADS + hd + 1])
            last.then_inc(w_ready, 1)
            act.wait_ge(sqn_ready, 1)
            act.wait_ge(cp_copied, KM)
            n0, j0 = FIRST["ml_z"], HALF["ml_z"]
            for k in range(2):
                high(n0 + k, j0 + 2 * k)
            for m in range(NSMP * HEADS):
                b, hd = m // HEADS, m % HEADS
                act.wait_ge(vb_done, m + 1)
                for q in range(2):
                    if m >= 1:
                        act.wait_ge(C_new, 2 * m + q - 1)
                    for i in range(HC // 2):
                        c = q * (HC // 2) + i
                        last = func(vk[q][:, i, :], ps[:, m % 2, :], ACT.Copy, scale=kw[:, hd * HC + c, b:b + 1])
                    last.then_inc(vb_used, 1)
                if m == 1:
                    for i in range(8):
                        act.wait_ge(cp_stored[i], 16 * KM // 8)
                if 1 <= m <= KM:
                    k = m - 1
                    if k + 2 < KM:
                        high(n0 + k + 2, j0 + 2 * k + 4)
                    tile_used(j0 + 2 * k)
                    func(z[:, k, :], ps[:, 2 + k % 2, 0:TOK], ACT.Silu).then_inc(z_ready, 1)
                if m < KM:
                    func(xc[:, m, :], xc[:, m, :], ACT.Copy, scale=col("ml_skip", m)).then_inc(skip_ready, 1)
                for i in range(2):
                    if m == AT_SQUARE + i:
                        act.wait_ge(hc_ready, i + 1)
                        func(hsq[:, 8 * i:8 * i + 8, :], hT[:, 8 * i:8 * i + 8, 0:NPR], ACT.Square)\
                            .then_inc(hsq_ready, 1)
                    if m == AT_SQRT + i:
                        act.wait_ge(hvar_ready, i + 1)
                        func(flat(hstd[:, 2 * i:2 * i + 2]), flat(hstd[:, 2 * i:2 * i + 2]), ACT.Sqrt)\
                            .then_inc(hstd_ready, 1)
            act.wait_ge(hvar_ready, 3)
            func(flat(std_s), flat(std_s), ACT.Sqrt).then_inc(hstd_ready, 1)
            peer(1)
            norm(4)

        @block.gpsimd
        def _(pool):
            def joined(v):
                return v.rearrange("p c j b -> p c (j b)")

            def flat(v):
                return v.rearrange("p a b -> p (a b)")

            def load_C(m):
                pool.dma_start(flat(Cbuf[m % CBUFS]), C_d[m]).then_inc(C_in[m % CBUFS], 16)

            def low_rows(l):
                j0 = HALF[f"u{l}"]
                pool.wait_ge(lo_ready[1], j0 // 2)
                with pool.Fori(0, POOL_ROWS // SLOTS) as r:
                    for k in range(SLOTS):
                        j = j0 + 2 * k + 1
                        pool.wait_ge(hi_ready, r * (2 * SLOTS) + (j + 1))
                        nc.gpsimd.tensor_tensor(w_lo[:, j % HALVES, :], half_of(FIRST[f"u{l}"] + k, 1),
                                                w_hi[:, j % HALVES, :].bitcast(F32), ALU.subtract)\
                            .then_inc(lo_ready[1], 1)

            pool.wait_ge(hs_ready, NC)
            pool.dma_start(lru_h_o, xr[:, :, NPR - 1:TOK]).then_inc(stores, 16)
            pool.dma_start(lru_conv_p_o, xp[:, :, NPR:NPR + 3]).then_inc(stores, 16)
            pool.dma_start(joined(lru_conv_s_o), joined(xs[:, :, 1:4, :])).then_inc(stores, 16)
            low_rows(0)
            pool.wait_ge(x_ready, 2 * NC)
            pool.dma_start(gates, gates_d).then_inc(ml_inputs_in, 16)
            pool.dma_start(nst, ml_n_d).then_inc(ml_inputs_in, 16)
            pool.dma_start(joined(xms[:, :, 0:3, :]), joined(ml_conv_d)).then_inc(ml_inputs_in, 16)
            pool.wait_ge(conv_ready, KM)
            pool.dma_start(ml_conv_p_o, xm[:, :, NPR:NPR + 3]).then_inc(ml_conv_stored, 16)
            pool.dma_start(joined(ml_conv_s_o), joined(xms[:, :, 1:4, :])).then_inc(ml_conv_stored, 16)
            pool.wait_ge(rows_ready, 1)
            pool.dma_start(m_o, mrow[0:HEADS, NPR - 1:TOK]).then_inc(stores, 16)
            pool.wait_ge(sqn_ready, 1)
            pool.dma_start(n_s_o, nst).then_inc(stores, 16)
            pool.wait_ge(st_done, 1)
            load_C(0)
            for n in range(KM):
                pool.wait_ge(cp_copied, n + 1)
                pool.dma_start(C_p_o[n], Cst[:, n % 8, :]).then_inc(cp_stored[n % 8], 16)
            pool.wait_ge(npr_ready, 1)
            pool.dma_start(n_p_o, npr).then_inc(stores, 16)
            pool.wait_ge(cp_done, KM)
            for m in range(1, CBUFS):
                load_C(m)
            for m in range(NSMP * HEADS):
                pool.wait_ge(C_read, m + 1)
                pool.dma_start(C_s_o[m], flat(Cbuf[m % CBUFS])).then_inc(C_out[m % CBUFS], 16)
                if 1 <= m and m - 1 + CBUFS < NSMP * HEADS:
                    pool.wait_ge(C_out[(m - 1) % CBUFS], 16 * ((m - 1) // CBUFS + 1))
                    load_C(m - 1 + CBUFS)
            low_rows(1)
            pool.wait_ge(y_ready, 1)
            pool.dma_start(y_o, h_raw[4]).then_inc(stores, 16)
            pool.wait_ge(stores, 16 * 7)
            pool.wait_ge(ml_conv_stored, 16 * 2)
            for i in range(8):
                pool.wait_ge(cp_stored[i], 16 * KM // 8)
            for i in range(CBUFS):
                pool.wait_ge(C_out[i], 16 * C_uses(i))

        @block.vector
        def _(dve):
            count = [0]

            def link(ins):
                count[0] += 1
                ins.then_inc(dve_seq, 1)
                dve.wait_ge(dve_seq, count[0])

            vec = nc.vector
            tt, ts, stt = vec.tensor_tensor, vec.tensor_scalar, vec.scalar_tensor_tensor

            def flat(v):
                return v.rearrange("p c t -> p (c t)")

            def low(n, j0, r=0, halves=2):
                for half in range(halves):
                    j = j0 + half
                    dve.wait_ge(hi_ready, r * (2 * SLOTS) + (j + 1))
                    tt(w_lo[:, j % HALVES, :], half_of(n, half), w_hi[:, j % HALVES, :].bitcast(F32),
                       ALU.subtract).then_inc(lo_ready[half], 1)

            def tile_used(j0):
                dve.wait_ge(half_used, j0 + 2)

            def copy_part(l, j0):
                tile_used(j0)
                for half in range(2):
                    vec.tensor_copy(ada_rows[l][half][0:2 * NSEQ, :], ps[0:2 * NSEQ, 4 + half, :])\
                        .then_inc(ada_copied, 1)

            def minus_softplus(out, raw, e, z_, z2, p, scale_):
                link(ts(z_, e, 2.0, None, ALU.add))
                link(vec.reciprocal(z_, z_))
                link(tt(z_, z_, e, ALU.mult))
                link(tt(z2, z_, z_, ALU.mult))
                link(ts(p, z2, 1.0 / (2 * N_LOG1P + 1), None, ALU.mult))
                for i in range(N_LOG1P - 1, 0, -1):
                    link(stt(p, p, 1.0 / (2 * i + 1), z2, ALU.add, ALU.mult))
                link(stt(p, p, 1.0, z_, ALU.add, ALU.mult))
                link(ts(out, raw, 0.0, None, ALU.min))
                link(stt(out, p, -2.0, out, ALU.mult, ALU.add))
                if scale_ != 1.0:
                    link(ts(out, out, scale_, None, ALU.mult))

            def over_tokens(v, n):
                return v.unsqueeze(2).to_broadcast([P, v.shape[1], n])

            def norm(n, gain, l, part, stage):
                low(FIRST[stage], HALF[stage])
                h = h_raw[n]
                shift = mod[l][:, part * NC:(part + 1) * NC, :]
                link(stt(scale, mod[l][:, (part + 1) * NC:(part + 2) * NC, :], 1.0,
                         over_tokens(col(gain, 0, NC), NSEQ), ALU.add, ALU.mult))
                dve.wait_ge(ssq_done, n + 1)
                ts(rstd, ps[:, 0, 0:TOK], 1.0 / D, EPS, ALU.mult, ALU.add).then_inc(ms_ready, 1)
                dve.wait_ge(rms_ready, n + 1)
                link(vec.reciprocal(rstd, rstd))
                hs_ = h[:, :, NPR:TOK]
                link(tt(hs_, x[:, :, NPR:TOK], rstd[:, NPR:TOK].unsqueeze(1).to_broadcast([P, NC, NSMP]), ALU.mult))
                link(tt(hs_, hs_, scale[:, :, 1:NSEQ], ALU.mult))
                tt(hs_, hs_, shift[:, :, 1:NSEQ], ALU.add).then_inc(h_made, 1)
                for c in range(NC + 2):
                    if c < NC:
                        stt(h[:, c, 0:NPR], x[:, c, 0:NPR], scale[:, c, 0:1], rstd[:, 0:NPR], ALU.mult, ALU.mult)\
                            .then_inc(h_made, 1)
                    if c == 1:
                        dve.wait_ge(h_hi_ready, n * (NC + 1) + 1)
                        tt(h_lo[:, :, NPR:TOK], hs_, h_hi[:, :, NPR:TOK].bitcast(F32), ALU.subtract)
                    if c >= 2:
                        dve.wait_ge(h_hi_ready, n * (NC + 1) + c)
                        stt(h_lo[:, c - 2, 0:NPR], h[:, c - 2, 0:NPR], shift[:, c - 2, 0:1],
                            h_hi[:, c - 2, 0:NPR].bitcast(F32), ALU.add, ALU.subtract).then_inc(h_ready, 1)

            def residual(n, l, part):
                gate = mod[l][:, part * NC:(part + 1) * NC, :]
                gated = scr(TOK, NC, NSMP)
                if part == 5:
                    tile_used(HALF[f"v{l}"] + 2 * (KEYS - 1))
                else:
                    dve.wait_ge(out_done, n // 2 + 1)
                link(tt(gated, ps[:, 0:NC, NPR:TOK], gate[:, :, 1:NSEQ], ALU.mult))
                link(tt(x[:, :, NPR:TOK], x[:, :, NPR:TOK], gated, ALU.add))
                for m in range(NC):
                    stt(x[:, m, 0:NPR], ps[:, m, 0:NPR], gate[:, m, 0:1], x[:, m, 0:NPR], ALU.mult, ALU.add)\
                        .then_inc(x_ready, 1)
                dve.wait_ge(x_ready, (n + 1) * NC)

            def tap(out, prompt, samples, c, nch, w, j):
                w_j = col(w, j * nch + c)
                stt(out[:, c, 0:NPR], prompt[:, c, j:j + NPR], w_j, out[:, c, 0:NPR], ALU.mult, ALU.add)
                return stt(out[:, c, NPR:TOK], samples[:, c, j, :], w_j, out[:, c, NPR:TOK], ALU.mult, ALU.add)

            dve.wait_ge(cond_in, 16)
            dve.wait_ge(c_hi_ready, 1)
            tt(c_parts[:, :, NSEQ:2 * NSEQ], c_sb, c_parts[:, :, 0:NSEQ].bitcast(F32), ALU.subtract)\
                .then_inc(c_parts_ready, 1)
            for t in range(2 * NC):
                low(t, HALF["ada0"] + 2 * t)
                if t == NC - 1:
                    dve.wait_ge(inputs_in, 16 * 5)
                    tt(add_parts[:], ident[0:2 * NSEQ, 0:NSEQ], ident[0:2 * NSEQ, NSEQ:2 * NSEQ], ALU.add)
                if t in (NC, 2 * NC - 1):
                    copy_part(0, HALF["ada0"] + 2 * (t - (t == NC)))
            link(vec.memset(xp[:, :, 0:3], 0.0))
            dve.wait_ge(lam_exp, 1)
            minus_softplus(lam8[:], col("lru_lambda", 0, NC), lam8[:], scr(512, NC), scr(520, NC), scr(528, NC),
                           LRU_C)

            def modulation(l, first, n, seen):
                tt(mod[l][:, first:first + n, :],
                   ps[:, 7, first * NSEQ:(first + n) * NSEQ].rearrange("p (c s) -> p c s", s=NSEQ),
                   over_tokens(col(f"b_ada{l}", first, n), NSEQ), ALU.add).then_inc(mod_ready, 1)
                dve.wait_ge(mod_ready, seen)

            dve.wait_ge(ada_done, 1)
            modulation(0, 0, 2 * NC, 1)

            norm(0, "norm_mix0", 0, 0, "lru_in")
            n0, j0 = FIRST["lru_in"], HALF["lru_in"]
            for t in range(6 * NC):
                if t + 1 < 6 * NC:
                    low(n0 + t + 1, j0 + 2 * t + 2)
                if t % 12 == 11:
                    copy_part(0, j0 + 2 * t)
                c, j = t // 6, t % 6 - 1
                if j in (0, 1, 2):
                    if j == 0:
                        dve.wait_ge(lin_x, c + 1)
                    last = tap(xr, xp, xs, c, NC, "lru_conv_w", j)
                    if j < 2:
                        link(last)
                    else:
                        last.then_inc(xr_ready, 1)
            dve.wait_ge(xr_ready, NC)
            dve.wait_ge(ada_done, 2)
            modulation(0, 2 * NC, 4 * NC, 2)
            dve.wait_ge(lgate_act, NC)
            tt(la, ra, over_tokens(lam8[:], TOK), ALU.mult).then_inc(loga_ready, 1)
            dve.wait_ge(lgate_act, 2 * NC)
            link(tt(ig, ig, xr, ALU.mult))
            for i, hf in enumerate(HALVES_OF_NC):
                dve.wait_ge(a_ready, i + 3)
                link(tt(bx[:, hf, :], ra[:, hf, :], ra[:, hf, :], ALU.mult))
                stt(la[:, hf, :], bx[:, hf, :], 1.0, la[:, hf, :], ALU.add, ALU.mult).then_inc(tt_ready, 1)
            link(tt(stmp, ra[:, :, NPR:TOK], h0, ALU.mult))
            dve.wait_ge(lin_y, NC)
            for c in range(NC + 1):
                if c in (0, NC // 2):
                    i = c // (NC // 2)
                    hf = HALVES_OF_NC[i]
                    dve.wait_ge(sqrt_ready, i + 1)
                    link(tt(bx[:, hf, :], la[:, hf, :], ig[:, hf, :], ALU.mult))
                    tt(xr[:, hf, NPR:TOK], bx[:, hf, NPR:TOK], stmp[:, hf, :], ALU.add)
                if c < NC:
                    vec.tensor_tensor_scan(xr[:, c, 0:NPR], ra[:, c, 0:NPR], bx[:, c, 0:NPR], 0.0, ALU.mult, ALU.add)\
                        .then_inc(hs_ready, 1)
                if c >= 1:
                    dve.wait_ge(hs_ready, c)
                    tt(ybr[:, c - 1, :], ybr[:, c - 1, :], xr[:, c - 1, :], ALU.mult).then_inc(ly_ready, 1)
            residual(0, 0, 2)

            def peer(l):
                norm(2 * l + 1, f"norm_ffn{l}", l, 3, f"wq{l}")
                for k in range(1, 2 * PH):
                    low(FIRST[f"wq{l}"] + k, HALF[f"wq{l}"] + 2 * k)
                rows = [0]

                def low_row():
                    row = rows[0]
                    if row < KEYS:
                        n, j = u_tile_at(l, row)
                        if row == POOL_ROWS:
                            dve.wait_ge(lo_ready[1], j // 2)
                        low(n, j, halves=1 if row < POOL_ROWS else 2)
                        if mixed(l, row):
                            low(n + 1, j + 2)
                        if l == 0 and row > MIXED[0] and mixed(l, row - 1) and row % SLOTS == 0:
                            copy_part(1, u_tile_at(l, row - 1)[1] + 2)
                        rows[0] += 1
                for _ in range(2):
                    low_row()
                for b, (t0, nb) in enumerate(BLOCKS):
                    Sb, V, I = S[0:nb, b], vals[0:nb], idx[0:nb]
                    cd, tp, ps_ = cand[0:nb], top[0:nb], pos[0:nb]

                    def top16(v, i, of, n):
                        for k in range(n):
                            if k % (n // 2) == 0:
                                low_row()
                            last = vec.max(v[:, k, 0:8], of[:, k, :])
                        link(last)
                        for k in range(n):
                            if k % (n // 2) == 0:
                                low_row()
                            last = vec.max_index(i[:, k, 0:8], v[:, k, 0:8], of[:, k, :])
                        link(last)
                        for k in range(n):
                            if k % (n // 2) == 0:
                                low_row()
                            last = vec.match_replace(of[:, k, :], v[:, k, 0:8], of[:, k, :], LOWEST)
                        link(last)
                        for k in range(n):
                            if k % (n // 2) == 0:
                                low_row()
                            last = vec.max(v[:, k, 8:16], of[:, k, :])
                        link(last)
                        for k in range(n):
                            if k % (n // 2) == 0:
                                low_row()
                            last = vec.max_index(i[:, k, 8:16], v[:, k, 8:16], of[:, k, :])
                        link(last)

                    dve.wait_ge(sc_ready[l], 4 * (b + 1))
                    top16(V, I, Sb, 2 * PH)
                    vec.tensor_copy(flat(idxf[0:nb]), flat(I))
                    V4 = V.rearrange("p (a two) k -> p a two k", two=2)
                    I4 = idxf[0:nb].rearrange("p (a two) k -> p a two k", two=2)
                    full = [nb, PH, TOPK, TOPK]
                    link(tt(cd.rearrange("p a (i j) -> p a i j", j=TOPK),
                            V4[:, :, 0, :].unsqueeze(3).to_broadcast(full),
                            V4[:, :, 1, :].unsqueeze(2).to_broadcast(full), ALU.add))
                    top16(tp, ps_, cd, PH)
                    tt(picks[0:nb, b, 2, :].rearrange("p (a k) -> p a k", a=PH), tp,
                       tp[:, :, 0:1].to_broadcast([nb, PH, TOPK]), ALU.subtract).then_inc(top_ready[l], 1)
                    assert b >= NB or rows[0] <= EXP_ROWS[b] + 2
                    vec.tensor_single_scalar(ab[0:nb, 0, :], flat(ps_), 4, ALU.logical_shift_right)
                    link(vec.tensor_single_scalar(ab[0:nb, 1, :], flat(ps_), TOPK - 1, ALU.bitwise_and))
                    link(vec.tensor_copy(flat(abf[0:nb]), flat(ab[0:nb])))
                    for i in range(2):
                        e = eq[0:nb]
                        link(tt(e, abf[0:nb, i, :].unsqueeze(2).to_broadcast([nb, PICKS, TOPK]),
                                iota[0:nb, 0:TOPK].unsqueeze(1).to_broadcast([nb, PICKS, TOPK]), ALU.is_equal))
                        low_row()
                        e4 = e.rearrange("p (a k) j -> p a k j", a=PH)
                        link(tt(e4, e4, I4[:, :, i, :].unsqueeze(2).to_broadcast(full), ALU.mult))
                        low_row()
                        last = vec.reduce_sum(picks[0:nb, b, i, :], e, axis=AX_X)
                        if b < NB - 1 or i == 0:
                            link(last)
                last.then_inc(work_free[l], 1)
                assert rows[0] <= FREE_ROW + 2
                while rows[0] < KEYS:
                    low_row()
                for b, (t0, nb) in enumerate(BLOCKS):
                    dve.wait_ge(topexp_ready[l], b + 1)
                    wexp = picks[0:nb, b, 2, :].rearrange("p (a k) -> p a k", a=PH)
                    link(vec.reduce_sum(ssum[0:nb, b], wexp, axis=AX_X))
                    link(vec.reciprocal(ssum[0:nb, b], ssum[0:nb, b]))
                    tt(wexp, wexp, ssum[0:nb, b].unsqueeze(2).to_broadcast([nb, PH, TOPK]), ALU.mult)\
                        .then_inc(picks_ready[l], 1)
                if l == 0:
                    dve.wait_ge(ada_done, 3)
                    modulation(1, 0, 6 * NC, 3)
                for b, (t0, nb) in enumerate(BLOCKS):
                    dve.wait_ge(pickT_done[l], b + 1)
                    last = vec.tensor_copy(
                        pickT[:, :, t0:t0 + nb],
                        ps[:, 4 + b, 0:3 * P].rearrange("p (i t) -> p i t", i=3)[:, :, 0:nb])
                last.then_inc(pickT_ready[l], 1)
                dve.wait_ge(pickT_ready[l], 1)

                def build(g, s):
                    for i in range(4):
                        t = bass.ds(g * 4 + i, 1)
                        last = ts(oh_i[s][:, i, :], iota, pickT[:, 0, t], pickT[:, 2, t], ALU.is_equal, ALU.mult)
                    last.then_inc(oh_i_ready[l], 1)

                def weigh(g, s):
                    Gt = G[:, :, bass.ds(g * 4, 4)].rearrange("p r t -> p t r")
                    tt(Gt, ps[:, s, :].rearrange("p (t r) -> p t r", t=4), Gt, ALU.mult).then_inc(routed[l], 1)
                build(0, 0)
                build(1, 1)
                dve.wait_ge(g_ready[l], KEYS)
                assert GROUPS % OH == 2
                with dve.Fori(0, GROUPS // OH) as r:
                    for s in range(OH):
                        dve.wait_ge(route_done[l], r * OH + (s + 1))
                        weigh(r * OH + s, s)
                        build(r * OH + (s + 2), (s + 2) % OH)
                for s in range(2):
                    dve.wait_ge(route_done[l], GROUPS - 1 + s)
                    weigh(GROUPS - 2 + s, s)

                dve.wait_ge(routed[l], GROUPS)

                def v_rows(r):
                    for k in range(SLOTS):
                        low(FIRST[f"v{l}"] + k, HALF[f"v{l}"] + 2 * k, r)
                        dve.wait_ge(g_hi_ready[l], r * SLOTS + (k + 1))
                        tt(g_lo[:, k % 2, :], BIG[:, bass.ds(r * (SLOTS * TOK) + k * TOK, TOK)],
                           g_hi[:, k % 2, :].bitcast(F32), ALU.subtract).then_inc(g_lo_ready[l], 1)
                with dve.Fori(0, KEYS // SLOTS) as r:
                    v_rows(r)
                residual(2 * l + 1, l, 5)

            peer(0)

            norm(2, "norm_mix1", 1, 0, "ml_x")
            link(vec.memset(xm[:, :, 0:3], 0.0))
            dve.wait_ge(ml_inputs_in, 16 * 3)
            for k in range(1, KM + 1):
                if k < KM:
                    low(FIRST["ml_x"] + k, HALF["ml_x"] + 2 * k)
                dve.wait_ge(mx_copied, k)
                for j in range(2):
                    link(tap(xc, xm, xms, k - 1, KM, "ml_conv_w", j))
                tap(xc, xm, xms, k - 1, KM, "ml_conv_w", 2).then_inc(conv_ready, 1)
            H_ = slice(0, HEADS)
            dve.wait_ge(gate_done, 1)
            vec.tensor_copy(Frow[0:2 * HEADS], ps[0:2 * HEADS, 4, 0:TOK]).then_inc(gate_rows, 1)
            ts(irow[H_], ps[H_, 4, 0:TOK], col("ml_b_ig")[H_], None, ALU.add)
            dve.wait_ge(gate_done, 2)
            ts(frow[H_], ps[H_, 5, 0:TOK], col("ml_b_fg")[H_], None, ALU.add).then_inc(gate_raw, 1)
            dve.wait_ge(gate_exp, 2)
            link(vec.memset(zero[H_], 0.0))
            minus_softplus(t_c[H_], frow[H_], exp_f[H_], t_a[H_], t_b[H_], Frow[H_], 1.0)
            link(vec.tensor_tensor_scan(Frow[H_, 0:NPR], t_c[H_, 0:NPR], zero[H_, 0:NPR], 0.0, ALU.add, ALU.add))
            link(tt(Grow[H_, 0:NPR], irow[H_, 0:NPR], Frow[H_, 0:NPR], ALU.subtract))
            link(vec.tensor_tensor_scan(frow[H_, 0:NPR], Grow[H_, 0:NPR], Grow[H_, 0:NPR], 0.0, ALU.max, ALU.max))
            tt(mrow[H_, 0:NPR], Frow[H_, 0:NPR], frow[H_, 0:NPR], ALU.add)
            fs, is_, ms = t_c[H_, NPR:TOK], irow[H_, NPR:TOK], mrow[H_, NPR:TOK]
            link(tt(fs, fs, col("ml_m0", 0, NSMP)[H_], ALU.add))
            link(tt(ms, fs, is_, ALU.max))
            tt(srow[H_, 0, :], fs, ms, ALU.subtract)
            tt(srow[H_, 1, :], is_, ms, ALU.subtract)
            ts(srow[H_, 2, :], ms, -1.0, None, ALU.mult).then_inc(rows_ready, 1)
            dve.wait_ge(bcast_done, 1)
            for hd in range(HEADS):
                M = ps[:, 4 + hd // 2, hd % 2 * NPR:(hd % 2 + 1) * NPR]
                stt(Wt[:, hd, 0:P], M[:, 0:P], -1.0, causal, ALU.mult, ALU.add)
                ts(Wt[:, hd, P:NPR], M[:, P:NPR], -1.0, None, ALU.mult)
                stt(Wt[:, hd, NPR:NPR + P], M[:, P:NPR], -1.0, causal, ALU.mult, ALU.add)
            dve.wait_ge(gcol_done, 1)
            vec.tensor_copy(gcol, ps[:, 6, 0:2 * HEADS]).then_inc(wexp_in, 1)
            dve.wait_ge(sbc_done, 1)
            link(vec.tensor_copy(bc.rearrange("p a b c -> p (a b c)"), ps[:, 7, 0:HEADS * 3 * NSMP]))

            def per_head(v):
                return v.rearrange("p (a c) b -> p a c b", a=HEADS)

            def factor_of(i):
                return bc[:, :, i, :].unsqueeze(2).to_broadcast([P, HEADS, HC, NSMP])
            link(tt(per_head(nst), per_head(nst), factor_of(0), ALU.mult))
            link(tt(per_head(kw), per_head(kT[:, :, NPR:TOK]), factor_of(1), ALU.mult))
            link(tt(nst, nst, kw, ALU.add))
            tt(qn, qT[:, :, NPR:TOK], nst, ALU.mult).then_inc(sqn_ready, 1)
            dve.wait_ge(w_ready, 1)
            dve.wait_ge(st_done, 1)
            for hd in range(HEADS):
                last = tt(Sw[:, hd, :], ps[:, hd, 0:384], Wt[:, hd, :], ALU.mult)
            last.then_inc(sw_ready, 1)
            for hd in range(HEADS):
                for b in range(2):
                    e0 = NPR - 1 if b == 0 else NPR + P - 1
                    kh = kt[:, b, hd * MHD:(hd + 1) * MHD]
                    last = ts(kh, kh, Wt[:, hd, e0:e0 + 1], None, ALU.mult)
            last.then_inc(kw_ready, 1)
            dve.wait_ge(den_done, 1)
            dve.wait_ge(em_ready, 1)
            for i in range(2):
                e = flat(em[:, 2 * i:2 * i + 2, :])
                link(stt(e, ps[:, 4 + i, :], -1.0, e, ALU.mult, ALU.max))
                link(tt(e, ps[:, 4 + i, :], e, ALU.max))
            link(vec.reciprocal(flat(em), flat(em)))
            for hd in range(HEADS):
                dve.wait_ge(num_done, hd + 1)
                tt(hT[:, hd * HC:(hd + 1) * HC, 0:NPR],
                   ps[:, hd % 2 * 2:hd % 2 * 2 + 2, :].rearrange("p a (b t) -> p (a b) t", b=2),
                   em[:, hd:hd + 1, :].to_broadcast([P, HC, NPR]), ALU.mult).then_inc(num_read, 1)
            dve.wait_ge(sden_done, 1)
            sd = ps[:, 7, P:P + HEADS * NSMP].rearrange("p (a b) -> p a b", a=HEADS)
            link(stt(sden, sd, -1.0, bc[:, :, 2, :], ALU.mult, ALU.max))
            link(tt(sden, sd, sden, ALU.max))
            link(vec.reciprocal(sden, sden))
            dve.wait_ge(num_read, HEADS)
            for n in range(KM):
                dve.wait_ge(cp_done, n + 1)
                if n >= 8:
                    dve.wait_ge(cp_stored[n % 8], 16 * (n // 8))
                vec.tensor_copy(Cst[:, n % 8, :], ps[:, n % 4, :]).then_inc(cp_copied, 1)
            vec.tensor_copy(npr, ps[:, 6, 16:16 + KM]).then_inc(npr_ready, 1)
            link(vec.memset(qz, 0.0))
            vec.tensor_copy(qz[:, :, 0:NSMP * NSMP:NSMP + 1], qT[:, :, NPR:TOK]).then_inc(qz_ready, 1)
            for k in range(2):
                low(FIRST["ml_z"] + k, HALF["ml_z"] + 2 * k)
            for m in range(NSMP * HEADS):
                b, hd = m // HEADS, m % HEADS
                dve.wait_ge(C_in[m % CBUFS], 16 * (m // CBUFS + 1))
                for q in range(2):
                    dve.wait_ge(vb_used, 2 * m + q + 1)
                    Cm = flat(Cbuf[m % CBUFS][:, q * (HC // 2):(q + 1) * (HC // 2), :])
                    stt(Cm, Cm, bc[:, hd, 0, b:b + 1], flat(vk[q]), ALU.mult, ALU.add).then_inc(C_new, 1)
                if 1 <= m < KM - 1:
                    low(FIRST["ml_z"] + m + 1, HALF["ml_z"] + 2 * m + 2)
                for i in range(2):
                    part = hT[:, 8 * i:8 * i + 8, 0:NPR]
                    if m == AT_CENTRE + i:
                        dve.wait_ge(mu_done, i + 1)
                        for j in range(2):
                            ph = part[:, j * HC:(j + 1) * HC]
                            last = stt(ph, ps[:, 2 + i, j * NPR:(j + 1) * NPR].unsqueeze(1)
                                       .to_broadcast([P, HC, NPR]), -1.0 / MHD, ph, ALU.mult, ALU.add)
                        last.then_inc(hc_ready, 1)
                    if m == AT_MS + i:
                        dve.wait_ge(var_done, i + 1)
                        ts(flat(hstd[:, 2 * i:2 * i + 2]), ps[:, 2 + i, :], 1.0 / MHD, EPS, ALU.mult, ALU.add)\
                            .then_inc(hvar_ready, 1)
                    if m == AT_SCALE + i:
                        dve.wait_ge(hstd_ready, i + 1)
                        hs_ = hstd[:, 2 * i:2 * i + 2]
                        link(vec.reciprocal(hs_, hs_))
                        ph = part.rearrange("p (a c) t -> p a c t", a=2)
                        link(tt(ph, ph, hs_.unsqueeze(2).to_broadcast([P, 2, HC, NPR]), ALU.mult))
                    if m == AT_SKIP + i:
                        dve.wait_ge(skip_ready, KM)
                        for c in range(8 * i, 8 * i + 8):
                            last = stt(hT[:, c, 0:NPR], hT[:, c, 0:NPR], col("ml_ln_g", c), xc[:, c, 0:NPR],
                                       ALU.mult, ALU.add)
                        link(last)
                    if m == AT_Z + i:
                        dve.wait_ge(z_ready, KM)
                        tt(part, part, z[:, 8 * i:8 * i + 8, 0:NPR], ALU.mult)
            for hd in range(HEADS):
                dve.wait_ge(C_read, (NSMP - 1) * HEADS + hd + 1)
                vec.tensor_copy(Cq[0:NSMP, hd * MHD:(hd + 1) * MHD], ps[0:NSMP, 4 + hd, :]).then_inc(Cq_copied, 1)

            def each_chunk(v):
                return v.unsqueeze(2).to_broadcast([P, HEADS, HC, NSMP])

            def each_sample(name):
                return col(name, 0, KM).unsqueeze(2).to_broadcast([P, KM, NSMP])

            def head_sum(to, bank):
                link(vec.tensor_reduce(to, ps[:, bank, 0:KM * NSMP].rearrange("p (a c b) -> p a b c", a=HEADS, c=HC),
                                       AX_X, ALU.add))
            hs_ = hT[:, :, NPR:TOK]
            dve.wait_ge(Cq_turned, 1)
            tt(per_head(hs_), ps[:, 0, 0:KM * NSMP].rearrange("p (a c b) -> p a c b", a=HEADS, c=HC),
               each_chunk(sden), ALU.mult).then_inc(hT_ready, 1)
            dve.wait_ge(mu_done, 3)
            head_sum(mu_s, 2)
            link(ts(mu_s, mu_s, -1.0 / MHD, None, ALU.mult))
            link(tt(per_head(hs_), per_head(hs_), each_chunk(mu_s), ALU.add))
            tt(hsq_s, hs_, hs_, ALU.mult).then_inc(hsq_ready, 1)
            dve.wait_ge(var_done, 3)
            head_sum(std_s, 3)
            ts(std_s, std_s, 1.0 / MHD, EPS, ALU.mult, ALU.add).then_inc(hvar_ready, 1)
            dve.wait_ge(hstd_ready, 3)
            link(vec.reciprocal(std_s, std_s))
            link(tt(per_head(hs_), per_head(hs_), each_chunk(std_s), ALU.mult))
            link(tt(hs_, hs_, each_sample("ml_ln_g"), ALU.mult))
            link(tt(hs_, hs_, xc[:, :, NPR:TOK], ALU.add))
            tt(hs_, hs_, z[:, :, NPR:TOK], ALU.mult).then_inc(mly_ready, 1)
            residual(2, 1, 2)
            peer(1)

            dve.wait_ge(ssq_done, 5)
            ts(rstd, ps[:, 0, 0:TOK], 1.0 / D, EPS, ALU.mult, ALU.add).then_inc(ms_ready, 1)
            dve.wait_ge(rms_ready, 5)
            link(vec.reciprocal(rstd, rstd))
            for c in range(NC):
                last = stt(h_raw[4][:, c, :], x[:, c, :], col("norm_f", c), rstd, ALU.mult, ALU.mult)
            last.then_inc(y_ready, 1)


def kernel(**inputs):
    import numpy as np
    import concourse.bacc as bacc
    from concourse.bass_utils import run_bass_kernel_spmd as run

    a = {k: np.asarray(v) for k, v in inputs.items()}
    xpr, xsm = a["x_prompt"], a["x_sample"]
    T, D = xpr.shape[1:]
    B = xsm.shape[0]
    DR, MI = a["lru_w_out"].shape[1], a["ml_w_out"].shape[1]
    NC, KM = D // P, MI // P
    H = a["state_mlstm_m"].shape[2]
    f32 = np.float32

    def channels(v):
        return np.ascontiguousarray(v.reshape(v.shape[0], -1, P).transpose(2, 1, 0))

    def tiles(w):
        k, n = w.shape
        return w.reshape(k // TILE, NC, P, n // P, P).transpose(3, 0, 2, 1, 4).reshape(-1, P, TILE)

    def diagonal(w):
        n, b, _ = w.shape
        per = P // b
        out = np.zeros((n // per, P, P), f32)
        for i in range(per):
            out[:, i * b:(i + 1) * b, i * b:(i + 1) * b] = w[i::per]
        return out.reshape(-1, TILE // P, P, P).transpose(0, 2, 1, 3).reshape(-1, P, TILE)

    first, n_tiles = tile_plan(D, DR, MI, 2, P)
    stream = np.empty((n_tiles // 2, P, 2, TILE), f32)

    def put(name, t):
        n = first[name] // 2
        stream[n:n + len(t) // 2] = t.reshape(-1, 2, P, TILE).transpose(0, 2, 1, 3)

    def after_each(t, others, n):
        return np.concatenate([t[:, None], others.reshape(len(t), n, P, TILE)], axis=1).reshape(-1, P, TILE)

    ada = [a["w_ada"][l].reshape(NC, P, 6, TILE).transpose(2, 0, 1, 3).reshape(-1, P, TILE) for l in range(2)]
    put("ada0", ada[0][:2 * NC])
    for l in range(2):
        put(f"wq{l}", tiles(a["peer_w_q"][l]))
        keys = a["peer_keys"][l].reshape(-1, P, P).transpose(0, 2, 1)
        put(f"keys{l}", keys.reshape(2, 8, P, P).transpose(0, 2, 1, 3).reshape(2, P, TILE))
        u = a["peer_u"][l].reshape(P, P, NC, P).transpose(0, 3, 2, 1).reshape(P, P, TILE)
        if l == 0:
            put("u0_ada1", after_each(u[MIXED[0]:MIXED[1]], ada[1], 1))
            put("u0_end", u[MIXED[1]:])
            u = u[:MIXED[0]]
        put(f"u{l}", u)
        put(f"v{l}", a["peer_v"][l].reshape(P, P, TILE))
    w_in = a["lru_w_in"][0]
    put("lru_in", after_each(np.stack([tiles(w_in[:, DR:]), tiles(w_in[:, :DR])], axis=1).reshape(-1, P, TILE),
                              ada[0][2 * NC:], 2))
    put("lru_gates", np.concatenate([diagonal(a["lru_w_a"][0]), diagonal(a["lru_w_i"][0])]))
    put("lru_out", tiles(a["lru_w_out"][0]))
    w_in = a["ml_w_in"][0]
    put("ml_x", tiles(w_in[:, :MI]))
    put("ml_z", tiles(w_in[:, MI:]))
    put("ml_qkv", np.concatenate([diagonal(a[f"ml_w_{c}"][0]) for c in "qkv"]))
    put("ml_out", tiles(a["ml_w_out"][0]))

    where, n_cols = column_layout(D, DR, MI)
    cols = np.zeros((P, n_cols), f32)

    def put_cols(name, v):
        v = v.reshape(-1, P).T
        cols[:, where[name][0]:where[name][0] + v.shape[1]] = v

    for l in range(2):
        for name in ("norm_mix", "norm_ffn", "b_ada"):
            put_cols(f"{name}{l}", a[name][l])
    put_cols("norm_f", a["norm_f"])
    for name in ("lru_conv_w", "lru_conv_b", "lru_b_a", "lru_b_i", "lru_lambda", "ml_conv_w", "ml_conv_b",
                 "ml_skip", "ml_ln_g"):
        put_cols(name, a[name][0])
    for name in ("ml_b_ig", "ml_b_fg"):
        cols[:H, where[name][0]] = a[name][0]
    cols[:H, where["ml_m0"][0]:where["ml_m0"][0] + B] = a["state_mlstm_m"][0].T

    consts = np.zeros((P, 4 * P), f32)
    consts[:, :P] = np.eye(P)
    consts[:, P:2 * P] = np.arange(P)
    consts[:, 2 * P:3 * P] = 1.0
    consts[:, 3 * P:4 * P] = np.where(np.arange(P)[:, None] > np.arange(P)[None], MASKED, 0.0)

    gates = np.concatenate([a["ml_w_ig"][0], a["ml_w_fg"][0]], axis=1)
    arrays = {
        "stream": stream.reshape(n_tiles // 2, P, 2 * TILE),
        "cols": cols,
        "consts": consts,
        "c": channels(np.concatenate([a["c_prompt"], a["c_sample"]])),
        "x": channels(np.concatenate([xpr[0], xsm[:, 0]])),
        "lru_h": channels(a["state_lru_h"][0]),
        "lru_conv": np.ascontiguousarray(a["state_lru_conv"][0].reshape(B, 3, NC, P).transpose(3, 2, 1, 0)),
        "ml_conv": np.ascontiguousarray(a["state_mlstm_conv"][0].reshape(B, 3, KM, P).transpose(3, 2, 1, 0)),
        "ml_n": channels(a["state_mlstm_n"][0].reshape(B, MI)),
        "gates": np.ascontiguousarray(gates.reshape(3 * KM, P, 2 * H).transpose(1, 0, 2)),
        "C": np.ascontiguousarray(a["state_mlstm_C"][0].reshape(B * H, MI // H // P, P, MI // H)
                                  .transpose(0, 2, 1, 3)).reshape(B * H, P, -1),
    }
    outs = {
        "y": (P, NC, T + B), "lru_h_o": (P, NC, B + 1), "lru_conv_p": (P, NC, 3), "lru_conv_s": (P, NC, 3, B),
        "ml_conv_p": (P, KM, 3), "ml_conv_s": (P, KM, 3, B), "n_p": (P, KM), "n_s": (P, KM, B), "m": (H, B + 1),
        "C_p": (KM, P, MI // H), "C_s": (B * H, P, MI),
    }
    nc = bacc.Bacc("TRN2", target_bir_lowering=False, num_devices=1, dynamic_dma_scratch_size=4096)
    args = [nc.dram_tensor(f"in_{k}", v.shape, F32, kind="ExternalInput").ap() for k, v in arrays.items()]
    args += [nc.dram_tensor(f"out_{k}", s, F32, kind="ExternalOutput").ap() for k, s in outs.items()]
    decoder_step(nc, *args)
    r = run(nc, [{f"in_{k}": v for k, v in arrays.items()}], core_ids=[0]).results[0]
    r = {k: r[f"out_{k}"] for k in outs}

    def rows(v):
        return np.ascontiguousarray(v.transpose(2, 1, 0)).reshape(v.shape[2], -1)

    def conv(v):
        return np.ascontiguousarray(v.transpose(3, 2, 1, 0)).reshape(v.shape[3], 3, -1)

    y = rows(r["y"])
    hs = rows(r["lru_h_o"])
    mh = MI // H
    C_s = r["C_s"].reshape(B, H, P, mh // P, mh).transpose(0, 1, 3, 2, 4).reshape(B, H, mh, mh)
    return (y[None, :T], y[T:, None],
            hs[None, :1], conv(r["lru_conv_p"][..., None])[None],
            r["C_p"].reshape(1, 1, H, mh, mh), rows(r["n_p"][..., None]).reshape(1, 1, H, mh),
            np.ascontiguousarray(r["m"][:, :1].T)[None], conv(r["ml_conv_p"][..., None])[None],
            hs[None, 1:], conv(r["lru_conv_s"])[None],
            np.ascontiguousarray(C_s)[None], rows(r["n_s"]).reshape(1, B, H, mh),
            np.ascontiguousarray(r["m"][:, 1:].T)[None], conv(r["ml_conv_s"])[None])
```
